# Optimizing a Trainium2 kernel written in Bass

```python
import math
import jax, jax.numpy as jnp
from jax import lax
import numpy as np

D_MODEL = 1024
BATCH = 1
SEQ = 512
DEPTH = 2

HEAD_DIM = 64
D_MIX = D_MODEL
HA = (D_MIX // 2) // (2 * HEAD_DIM)
HB = (D_MIX // 4) // HEAD_DIM
HC = (D_MIX // 4) // HEAD_DIM
WA = HA * 2 * HEAD_DIM
WB = HB * HEAD_DIM
WC = HC * HEAD_DIM
ROT_DIM = HEAD_DIM // 4
ROPE_THETA = 500000.0
Q_BLOCK = 128
LN_EPS = 1e-5
SUBLN_EPS = 1e-5
DEEPNORM_ALPHA = (2 * DEPTH) ** 0.25
DEEPNORM_BETA = (8 * DEPTH) ** -0.25
SPLIT_SIZES = (WA, WA, WA, WA, WB, WB, WB, HB, WB, WC, WC, WC, WC)
VALUE_SEGMENTS = (2, 6, 11)
D_IN = sum(SPLIT_SIZES)
SPLIT_POINTS = tuple(int(v) for v in np.cumsum(SPLIT_SIZES)[:-1])


def _layernorm(t, g, b):
    tf = t.astype(jnp.float32)
    mu = jnp.mean(tf, -1, keepdims=True)
    var = jnp.mean(jnp.square(tf - mu), -1, keepdims=True)
    out = (tf - mu) * lax.rsqrt(var + LN_EPS) * g.astype(jnp.float32) + b.astype(jnp.float32)
    return out.astype(t.dtype)

def _rope_tables(seq):
    inv = ROPE_THETA ** (-jnp.arange(0, ROT_DIM, 2, dtype=jnp.float32) / ROT_DIM)
    ang = jnp.arange(seq, dtype=jnp.float32)[:, None] * inv[None, :]
    return jnp.cos(ang), jnp.sin(ang)

def _partial_rope(t, cos, sin):
    half = ROT_DIM // 2
    x1 = t[..., :half].astype(jnp.float32)
    x2 = t[..., half:ROT_DIM].astype(jnp.float32)
    r1 = (x1 * cos - x2 * sin).astype(t.dtype)
    r2 = (x2 * cos + x1 * sin).astype(t.dtype)
    return jnp.concatenate([r1, r2, t[..., ROT_DIM:]], axis=-1)

def _split_heads(t, n_heads):
    b_, s_, w_ = t.shape
    return t.reshape(b_, s_, n_heads, w_ // n_heads).transpose(0, 2, 1, 3)

def _to_blocks(t):
    b_, h_, s_ = t.shape[:3]
    t = t.reshape((b_, h_, s_ // Q_BLOCK, Q_BLOCK) + t.shape[3:])
    return jnp.moveaxis(t, 2, 0)

def _from_blocks(t):
    nb, b_, h_, blk, dv = t.shape
    return t.transpose(1, 0, 3, 2, 4).reshape(b_, nb * blk, h_ * dv)

def _differential_attention(q1, q2, k1, k2, v, lam):
    seq = k1.shape[2]
    kpos = jnp.arange(seq)
    starts = jnp.arange(seq // Q_BLOCK) * Q_BLOCK
    scale = HEAD_DIM ** -0.5

    def block(args):
        q1b, q2b, start = args
        qpos = start + jnp.arange(Q_BLOCK)
        causal = kpos[None, :] <= qpos[:, None]
        s1 = jnp.einsum('bhqd,bhkd->bhqk', q1b, k1).astype(jnp.float32) * scale
        s2 = jnp.einsum('bhqd,bhkd->bhqk', q2b, k2).astype(jnp.float32) * scale
        p1 = jax.nn.softmax(jnp.where(causal, s1, -jnp.inf), axis=-1)
        p2 = jax.nn.softmax(jnp.where(causal, s2, -jnp.inf), axis=-1)
        w = (p1 - lam * p2).astype(v.dtype)
        return jnp.einsum('bhqk,bhkd->bhqd', w, v)

    return lax.map(block, (_to_blocks(q1), _to_blocks(q2), starts))

def _forgetting_attention(q, k, v, cum_logf):
    seq = k.shape[2]
    kpos = jnp.arange(seq)
    starts = jnp.arange(seq // Q_BLOCK) * Q_BLOCK
    scale = HEAD_DIM ** -0.5

    def block(args):
        qb, cqb, start = args
        qpos = start + jnp.arange(Q_BLOCK)
        causal = kpos[None, :] <= qpos[:, None]
        s = jnp.einsum('bhqd,bhkd->bhqk', qb, k).astype(jnp.float32) * scale
        logits = s + cqb[..., :, None] - cum_logf[..., None, :]
        p = jax.nn.softmax(jnp.where(causal, logits, -jnp.inf), axis=-1)
        return jnp.einsum('bhqk,bhkd->bhqd', p.astype(v.dtype), v)

    return lax.map(block, (_to_blocks(q), _to_blocks(cum_logf), starts))

def _stick_breaking_attention(q, k, v):
    seq = k.shape[2]
    kpos = jnp.arange(seq)
    starts = jnp.arange(seq // Q_BLOCK) * Q_BLOCK
    scale = HEAD_DIM ** -0.5

    def block(args):
        qb, start = args
        qpos = start + jnp.arange(Q_BLOCK)
        strict = kpos[None, :] < qpos[:, None]
        z = jnp.einsum('bhqd,bhkd->bhqk', qb, k).astype(jnp.float32) * scale
        log_fail = jnp.where(strict, jax.nn.log_sigmoid(-z), 0.0)
        after = lax.cumsum(log_fail, axis=3, reverse=True) - log_fail
        weights = jnp.where(strict, jnp.exp(jax.nn.log_sigmoid(z) + after), 0.0)
        return jnp.einsum('bhqk,bhkd->bhqd', weights.astype(v.dtype), v)

    return lax.map(block, (_to_blocks(q), starts))

def first_inputs(seed: int = 0) -> dict:
    key = jax.random.key(seed)
    ks = jax.random.split(key, 13)
    x = jax.random.normal(ks[0], (BATCH, SEQ, D_MODEL), jnp.float32)
    ln_in_g = 1.0 + 0.02 * jax.random.normal(ks[1], (D_MODEL,), jnp.float32)
    ln_in_b = 0.02 * jax.random.normal(ks[2], (D_MODEL,), jnp.float32)
    col_scale = jnp.concatenate([
        jnp.full((n,), DEEPNORM_BETA if i in VALUE_SEGMENTS else 1.0, jnp.float32)
        for i, n in enumerate(SPLIT_SIZES)])
    w_in = (jax.random.normal(ks[3], (DEPTH, D_MODEL, D_IN), jnp.float32)
            * (D_MODEL ** -0.5) * col_scale)
    b_forget = 1.0 + 0.1 * jax.random.normal(ks[4], (DEPTH, HB), jnp.float32)
    lambda_q1 = 0.1 * jax.random.normal(ks[5], (DEPTH, HEAD_DIM), jnp.float32)
    lambda_k1 = 0.1 * jax.random.normal(ks[6], (DEPTH, HEAD_DIM), jnp.float32)
    lambda_q2 = 0.1 * jax.random.normal(ks[7], (DEPTH, HEAD_DIM), jnp.float32)
    lambda_k2 = 0.1 * jax.random.normal(ks[8], (DEPTH, HEAD_DIM), jnp.float32)
    subln_g = 1.0 + 0.02 * jax.random.normal(ks[9], (DEPTH, 2 * HEAD_DIM), jnp.float32)
    w_out = (jax.random.normal(ks[10], (DEPTH, D_MIX, D_MODEL), jnp.float32)
             * (D_MIX ** -0.5) * DEEPNORM_BETA)
    ln_g = 1.0 + 0.02 * jax.random.normal(ks[11], (DEPTH, D_MODEL), jnp.float32)
    ln_b = 0.02 * jax.random.normal(ks[12], (DEPTH, D_MODEL), jnp.float32)
    return {'x': x, 'ln_in_g': ln_in_g, 'ln_in_b': ln_in_b, 'w_in': w_in,
            'b_forget': b_forget, 'lambda_q1': lambda_q1, 'lambda_k1': lambda_k1,
            'lambda_q2': lambda_q2, 'lambda_k2': lambda_k2, 'subln_g': subln_g,
            'w_out': w_out, 'ln_g': ln_g, 'ln_b': ln_b}

def first_block(x, ln_in_g, ln_in_b, w_in, b_forget, lambda_q1, lambda_k1, lambda_q2,
              lambda_k2, subln_g, w_out, ln_g, ln_b):
    bsz, seq, _ = x.shape
    cos, sin = _rope_tables(seq)
    h = _layernorm(x, ln_in_g, ln_in_b)
    for layer in range(DEPTH):
        proj = jnp.einsum('bsd,de->bse', h, w_in[layer])
        (aq, ak, av, ag, bq, bk, bv, bf, bg, cq, ck, cv, cg) = jnp.split(proj, SPLIT_POINTS, axis=-1)

        qa = _partial_rope(_split_heads(aq, 2 * HA), cos, sin).reshape(bsz, HA, 2, seq, HEAD_DIM)
        ka = _partial_rope(_split_heads(ak, 2 * HA), cos, sin).reshape(bsz, HA, 2, seq, HEAD_DIM)
        va = _split_heads(av, HA)
        lam_init = 0.8 - 0.6 * math.exp(-0.3 * layer)
        lam = (jnp.exp(jnp.sum(lambda_q1[layer].astype(jnp.float32) * lambda_k1[layer].astype(jnp.float32)))
               - jnp.exp(jnp.sum(lambda_q2[layer].astype(jnp.float32) * lambda_k2[layer].astype(jnp.float32)))
               + lam_init)
        oa = _differential_attention(qa[:, :, 0], qa[:, :, 1], ka[:, :, 0], ka[:, :, 1], va, lam)
        oaf = oa.astype(jnp.float32)
        oa = (oaf * lax.rsqrt(jnp.mean(jnp.square(oaf), -1, keepdims=True) + SUBLN_EPS)
              * subln_g[layer].astype(jnp.float32) * (1.0 - lam_init)).astype(h.dtype)
        ya = _from_blocks(oa) * jax.nn.silu(ag)

        logf = jax.nn.log_sigmoid((bf + b_forget[layer]).astype(jnp.float32))
        cum_logf = jnp.cumsum(logf, axis=1).transpose(0, 2, 1)
        ob = _forgetting_attention(_split_heads(bq, HB), _split_heads(bk, HB),
                                   _split_heads(bv, HB), cum_logf)
        yb = _from_blocks(ob) * jax.nn.silu(bg)

        oc = _stick_breaking_attention(_split_heads(cq, HC), _split_heads(ck, HC), _split_heads(cv, HC))
        yc = _from_blocks(oc) * jax.nn.silu(cg)

        y = jnp.einsum('bse,ed->bsd', jnp.concatenate([ya, yb, yc], axis=-1), w_out[layer])
        h = _layernorm(DEEPNORM_ALPHA * h + y, ln_g[layer], ln_b[layer])
    return h


DEPTH_2 = 1

A_HEADS = 4
A_HEAD_DIM = 128
IDX_HEADS = 8
IDX_DIM = 64
TOPK_MAX = 256
B_HEADS = 4
B_KEY_DIM = 128
B_VAL_DIM = 128
B_CHUNK = 64
C_HEADS = 4
C_Q_RANK = 384
C_KV_RANK = 256
C_NOPE = 128
C_ROPE = 64
C_V = 128
ROPE_THETA_2 = 10000.0
REL_BUCKETS = 32
REL_MAX_DIST = 128
D_FF = -(-8 * D_MODEL // (3 * 256)) * 256
QBLOCK = 128
EPS = 1e-6
N_BRANCH = 3
NEG_BIG = -1e30
LB_FLOOR = 1e-30

A_WIDTH = A_HEADS * A_HEAD_DIM
B_WIDTH = B_HEADS * B_VAL_DIM
C_WIDTH = C_HEADS * C_V
IN_SPLITS = (A_HEADS * A_HEAD_DIM, A_HEAD_DIM, A_HEAD_DIM,
             IDX_HEADS * IDX_DIM, IDX_DIM, IDX_HEADS,
             B_HEADS * B_KEY_DIM, B_HEADS * B_KEY_DIM,
             B_HEADS * B_VAL_DIM, B_HEADS * B_VAL_DIM,
             C_Q_RANK, C_KV_RANK, C_ROPE,
             N_BRANCH * D_MODEL)
IN_COLS = sum(IN_SPLITS)


def rms_norm(x, g):
    x32 = x.astype(jnp.float32)
    y = x32 * lax.rsqrt(jnp.mean(x32 * x32, axis=-1, keepdims=True) + EPS)
    return (y * g.astype(jnp.float32)).astype(x.dtype)

def apply_rope(x, cos, sin):
    x32 = x.astype(jnp.float32)
    x1, x2 = jnp.split(x32, 2, axis=-1)
    return jnp.concatenate([x1 * cos - x2 * sin, x2 * cos + x1 * sin], axis=-1).astype(x.dtype)

def t5_bucket(dist):
    max_exact = REL_BUCKETS // 2
    d = jnp.maximum(dist, 0)
    dl = jnp.maximum(d, max_exact).astype(jnp.float32)
    large = max_exact + (jnp.log(dl / max_exact) / math.log(REL_MAX_DIST / max_exact)
                         * (REL_BUCKETS - max_exact)).astype(jnp.int32)
    large = jnp.minimum(large, REL_BUCKETS - 1)
    return jnp.where(d < max_exact, d, large)

def dsa_attention(q, k, v, iq, ik, iw, positions, rel_bias):
    bsz, s_len = q.shape[0], q.shape[1]
    topk = min(TOPK_MAX, s_len // 4)
    n_blk = s_len // QBLOCK
    key_idx = jnp.arange(s_len)
    scale = A_HEAD_DIM ** -0.5
    idx_scale = (IDX_DIM ** -0.5) * (IDX_HEADS ** -0.5)
    ik32 = ik.astype(jnp.float32)
    gather = jax.vmap(lambda arr, ix: arr[ix])

    def block(i):
        start = i * QBLOCK
        qb = lax.dynamic_slice_in_dim(q, start, QBLOCK, axis=1)
        iqb = lax.dynamic_slice_in_dim(iq, start, QBLOCK, axis=1).astype(jnp.float32)
        iwb = lax.dynamic_slice_in_dim(iw, start, QBLOCK, axis=1).astype(jnp.float32)
        pb = lax.dynamic_slice_in_dim(positions, start, QBLOCK, axis=1)
        t_idx = start + jnp.arange(QBLOCK)
        causal = key_idx[None, :] <= t_idx[:, None]
        logits = jnp.einsum('bthd,bsd->bths', iqb, ik32)
        score = jnp.einsum('bths,bth->bts', jax.nn.relu(logits), iwb) * idx_scale
        score = jnp.where(causal[None], score, NEG_BIG)
        _, sel = lax.top_k(score, topk)
        k_sel = gather(k, sel)
        v_sel = gather(v, sel)
        p_sel = gather(positions, sel)
        bias = rel_bias[t5_bucket(pb[:, :, None] - p_sel)]
        s = (jnp.einsum('bthd,btkd->bthk', qb, k_sel).astype(jnp.float32) * scale
             + jnp.moveaxis(bias, -1, 2).astype(jnp.float32))
        valid = sel <= t_idx[None, :, None]
        s = jnp.where(valid[:, :, None, :], s, NEG_BIG)
        p = jax.nn.softmax(s, axis=-1).astype(v.dtype)
        return jnp.einsum('bthk,btkd->bthd', p, v_sel)

    out = lax.map(block, jnp.arange(n_blk))
    return jnp.moveaxis(out, 0, 1).reshape(bsz, s_len, A_WIDTH)

def hgrn2_mixer(q, f_raw, inp, g, lb, out_gain):
    bsz, s_len = q.shape[0], q.shape[1]
    f32 = jnp.float32
    n_chunk = s_len // B_CHUNK
    fr = f_raw.astype(f32)
    log_lb = jnp.log(jnp.maximum(lb, LB_FLOOR))
    log_f = jnp.logaddexp(log_lb, jnp.log1p(-lb) + jax.nn.log_sigmoid(fr))
    k_in = (1.0 - lb) * jax.nn.sigmoid(-fr)
    q_s = q.astype(f32) * (B_KEY_DIM ** -0.5)

    def chunks(t, d):
        return t.astype(f32).reshape(bsz, n_chunk, B_CHUNK, B_HEADS, d).transpose(1, 0, 3, 2, 4)

    causal = jnp.tril(jnp.ones((B_CHUNK, B_CHUNK), dtype=bool))

    def step(state, xs):
        qc, kc, vc, lfc = xs
        b = jnp.cumsum(lfc, axis=2)
        o_inter = jnp.einsum('bhck,bhkv->bhcv', qc * jnp.exp(b), state)
        diff = b[:, :, :, None, :] - b[:, :, None, :, :]
        decay = jnp.exp(jnp.where(causal[None, None, :, :, None], diff, NEG_BIG))
        attn = jnp.einsum('bhtk,bhsk,bhtsk->bhts', qc, kc, decay)
        o_intra = jnp.einsum('bhts,bhsv->bhtv', attn, vc)
        b_last = b[:, :, -1:, :]
        new_state = (jnp.exp(b_last[:, :, 0, :])[..., None] * state
                     + jnp.einsum('bhsk,bhsv->bhkv', kc * jnp.exp(b_last - b), vc))
        return new_state, o_inter + o_intra

    xs = (chunks(q_s, B_KEY_DIM), chunks(k_in, B_KEY_DIM), chunks(inp, B_VAL_DIM), chunks(log_f, B_KEY_DIM))
    state0 = jnp.zeros((bsz, B_HEADS, B_KEY_DIM, B_VAL_DIM), f32)
    _, o = lax.scan(step, state0, xs)
    o = o.transpose(1, 0, 3, 2, 4).reshape(bsz, s_len, B_HEADS, B_VAL_DIM)
    o = rms_norm(o, out_gain) * jax.nn.silu(g.astype(f32).reshape(bsz, s_len, B_HEADS, B_VAL_DIM))
    return o.reshape(bsz, s_len, B_WIDTH).astype(q.dtype)

def mla_attention(q_nope, q_pe, k_nope, k_pe, v):
    bsz, s_len = q_nope.shape[0], q_nope.shape[1]
    n_blk = s_len // QBLOCK
    scale = (C_NOPE + C_ROPE) ** -0.5
    key_idx = jnp.arange(s_len)

    def block(i):
        start = i * QBLOCK
        qn = lax.dynamic_slice_in_dim(q_nope, start, QBLOCK, axis=1)
        qp = lax.dynamic_slice_in_dim(q_pe, start, QBLOCK, axis=1)
        t_idx = start + jnp.arange(QBLOCK)
        causal = key_idx[None, :] <= t_idx[:, None]
        s = (jnp.einsum('bthd,bshd->bhts', qn, k_nope)
             + jnp.einsum('bthr,bsr->bhts', qp, k_pe)).astype(jnp.float32) * scale
        s = jnp.where(causal[None, None], s, NEG_BIG)
        p = jax.nn.softmax(s, axis=-1).astype(v.dtype)
        return jnp.einsum('bhts,bshd->bthd', p, v)

    out = lax.map(block, jnp.arange(n_blk))
    return jnp.moveaxis(out, 0, 1).reshape(bsz, s_len, C_WIDTH)

def second_inputs(seed: int = 0) -> dict:
    key = jax.random.key(seed)
    ks = jax.random.split(key, 24)
    f32 = jnp.float32
    res_scale = (2 * DEPTH_2) ** -0.5

    def dense(k, shape, fan_in, scale=1.0):
        return jax.random.normal(k, shape, f32) * (scale * fan_in ** -0.5)

    def gain(k, shape):
        return 1.0 + 0.02 * jax.random.normal(k, shape, f32)

    x = jax.random.normal(ks[0], (BATCH, SEQ, D_MODEL), f32)
    offset = jax.random.randint(ks[1], (BATCH, 1), 0, 4096, dtype=jnp.int32)
    positions = offset + jnp.arange(SEQ, dtype=jnp.int32)[None, :]
    return {
        'x': x,
        'positions': positions,
        'w_in': dense(ks[2], (DEPTH_2, D_MODEL, IN_COLS), D_MODEL),
        'w_up_a': dense(ks[3], (DEPTH_2, A_WIDTH, D_MODEL), A_WIDTH),
        'w_up_b': dense(ks[4], (DEPTH_2, B_WIDTH, D_MODEL), B_WIDTH),
        'w_up_c': dense(ks[5], (DEPTH_2, C_WIDTH, D_MODEL), C_WIDTH),
        'w_out': dense(ks[6], (DEPTH_2, D_MODEL, D_MODEL), D_MODEL, res_scale),
        'mla_q_norm': gain(ks[7], (DEPTH_2, C_Q_RANK)),
        'mla_w_qb': dense(ks[8], (DEPTH_2, C_Q_RANK, C_HEADS * (C_NOPE + C_ROPE)), C_Q_RANK),
        'mla_kv_norm': gain(ks[9], (DEPTH_2, C_KV_RANK)),
        'mla_w_kvb': dense(ks[10], (DEPTH_2, C_KV_RANK, C_HEADS * (C_NOPE + C_V)), C_KV_RANK),
        'hgrn_lb_logits': 0.5 * jax.random.normal(ks[11], (DEPTH_2, B_HEADS * B_KEY_DIM), f32),
        'hgrn_out_norm': gain(ks[12], (DEPTH_2, B_VAL_DIM)),
        'rel_bias': 0.5 * jax.random.normal(ks[13], (REL_BUCKETS, A_HEADS), f32),
        'attn_norm': gain(ks[14], (DEPTH_2, D_MODEL)),
        'ffn_norm': gain(ks[15], (DEPTH_2, D_MODEL)),
        'w_ffn_gate': dense(ks[16], (DEPTH_2, D_MODEL, D_FF), D_MODEL),
        'w_ffn_up': dense(ks[17], (DEPTH_2, D_MODEL, D_FF), D_MODEL),
        'w_ffn_down': dense(ks[18], (DEPTH_2, D_FF, D_MODEL), D_FF, res_scale),
        'final_norm': gain(ks[19], (D_MODEL,)),
    }

def second_block(x, positions, w_in, w_up_a, w_up_b, w_up_c, w_out, mla_q_norm, mla_w_qb, mla_kv_norm,
              mla_w_kvb, hgrn_lb_logits, hgrn_out_norm, rel_bias, attn_norm, ffn_norm, w_ffn_gate,
              w_ffn_up, w_ffn_down, final_norm):
    bsz, s_len, _ = x.shape
    f32 = jnp.float32
    split_pts = np.cumsum(IN_SPLITS)[:-1].tolist()
    p_lb = jax.nn.softmax(hgrn_lb_logits.astype(f32), axis=0)
    lower_bounds = jnp.cumsum(p_lb, axis=0) - p_lb[0:1]
    inv_freq = ROPE_THETA_2 ** (-jnp.arange(0, C_ROPE, 2, dtype=f32) / C_ROPE)
    ang = positions.astype(f32)[..., None] * inv_freq
    cos, sin = jnp.cos(ang), jnp.sin(ang)

    for l in range(DEPTH_2):
        h = rms_norm(x, attn_norm[l])
        proj = h @ w_in[l]
        (aq, ak, av, iq, ik, iw, bq, bf, bi, bg, cq, ckv, ckpe, gate_logits) = jnp.split(proj, split_pts, axis=-1)
        o_a = dsa_attention(aq.reshape(bsz, s_len, A_HEADS, A_HEAD_DIM), ak, av,
                            iq.reshape(bsz, s_len, IDX_HEADS, IDX_DIM), ik, iw, positions, rel_bias)
        o_b = hgrn2_mixer(bq, bf, bi, bg, lower_bounds[l], hgrn_out_norm[l])
        q_c = (rms_norm(cq, mla_q_norm[l]) @ mla_w_qb[l]).reshape(bsz, s_len, C_HEADS, C_NOPE + C_ROPE)
        q_nope, q_pe = q_c[..., :C_NOPE], q_c[..., C_NOPE:]
        kv_c = (rms_norm(ckv, mla_kv_norm[l]) @ mla_w_kvb[l]).reshape(bsz, s_len, C_HEADS, C_NOPE + C_V)
        k_nope, v_c = kv_c[..., :C_NOPE], kv_c[..., C_NOPE:]
        q_pe = apply_rope(q_pe, cos[:, :, None, :], sin[:, :, None, :])
        k_pe = apply_rope(ckpe, cos, sin)
        o_c = mla_attention(q_nope, q_pe, k_nope, k_pe, v_c)
        gates = jax.nn.sigmoid(gate_logits.astype(f32)).astype(x.dtype)
        g_a, g_b, g_c = jnp.split(gates, N_BRANCH, axis=-1)
        mixed = g_a * (o_a @ w_up_a[l]) + g_b * (o_b @ w_up_b[l]) + g_c * (o_c @ w_up_c[l])
        x = x + mixed @ w_out[l]
        h = rms_norm(x, ffn_norm[l])
        x = x + (jax.nn.silu(h @ w_ffn_gate[l]) * (h @ w_ffn_up[l])) @ w_ffn_down[l]

    return rms_norm(x, final_norm)


def setup_inputs(seed=0):
    out = dict(first_inputs(seed))
    for name, value in second_inputs(seed + 1).items():
        if name != "x":
            out[name + "_2"] = value
    return out


def reference(
    x, ln_in_g, ln_in_b, w_in, b_forget, lambda_q1, lambda_k1, lambda_q2, lambda_k2, subln_g,
    w_out, ln_g, ln_b, positions_2, w_in_2, w_up_a_2, w_up_b_2, w_up_c_2, w_out_2, mla_q_norm_2,
    mla_w_qb_2, mla_kv_norm_2, mla_w_kvb_2, hgrn_lb_logits_2, hgrn_out_norm_2, rel_bias_2,
    attn_norm_2, ffn_norm_2, w_ffn_gate_2, w_ffn_up_2, w_ffn_down_2, final_norm_2,
):
    x = first_block(
        x, ln_in_g, ln_in_b, w_in, b_forget, lambda_q1, lambda_k1, lambda_q2, lambda_k2,
        subln_g, w_out, ln_g, ln_b,
    )
    return second_block(
        x, positions_2, w_in_2, w_up_a_2, w_up_b_2, w_up_c_2, w_out_2, mla_q_norm_2, mla_w_qb_2,
        mla_kv_norm_2, mla_w_kvb_2, hgrn_lb_logits_2, hgrn_out_norm_2, rel_bias_2, attn_norm_2,
        ffn_norm_2, w_ffn_gate_2, w_ffn_up_2, w_ffn_down_2, final_norm_2,
    )


_drawn_inputs = setup_inputs


def setup_inputs(seed=0):
    import zlib

    import numpy as np

    out = dict(_drawn_inputs(seed))
    spreads = {}
    factors = {'b_forget': 51.825,
     'lambda_q1': 4.075,
     'lambda_q2': 3.062,
     'lambda_k2': 4.246,
     'subln_g': 8.0,
     'mla_q_norm_2': 8.0,
     'mla_kv_norm_2': 8.0,
     'hgrn_out_norm_2': 8.0,
     'attn_norm_2': 4.074,
     'ffn_norm_2': 5.291}
    for name, (base, spread) in spreads.items():
        noise = np.random.default_rng([zlib.crc32(name.encode()), seed]).standard_normal(out[name].shape)
        drawn = base * np.exp(spread * noise) if base else spread * noise
        out[name] = __import__('jax').numpy.asarray(drawn.astype(out[name].dtype))
    for name, factor in factors.items():
        out[name] = (out[name] * factor).astype(out[name].dtype)
    return out
```

```python
import math
from contextlib import ExitStack

import numpy as np
import concourse.bass as bass
from concourse import mybir

F32 = mybir.dt.float32
BF16 = mybir.dt.bfloat16
I32 = mybir.dt.int32
U8 = mybir.dt.uint8
ACT = mybir.ActivationFunctionType
ALU = mybir.AluOpType
AX = mybir.AxisListType.X

P = 128
S = 512
NT = S // P
D = 1024
KD = D // P
DEPTH = 2
HD = 64
NEG = -1e30
ALPHA = (2 * DEPTH) ** 0.25
W_SLOTS = 3
PROJ_BANKS = 2
SCORE_BANKS = 3
FREQS = 32
LEVELS = 6
CHUNK = 64
EXP_AND_LN = "natural_log_exp_and_others"
NCH = S // CHUNK
REL_BUCKETS = 32
REL_MAX_DIST = 128
TOPK = 128
IDX_HEADS = 8
D_FF = 2816
KF = D_FF // P

AQ, AK, AV, AG, BQ, BK, BV, BFG, BG, CQ, CK, CV, CG = (
    0, 512, 1024, 1536, 2048, 2304, 2560, 2816, 2820, 3076, 3332, 3588, 3844)
(XQ, XK, XV, IQ, IK, IW, HQ, HF, HI, HG, MQ, MKV, MPE, GATE) = (
    0, 512, 640, 768, 1280, 1344, 1352, 1864, 2376, 2888, 3400, 3784, 4040, 4104)


def bucket_starts():
    exact = REL_BUCKETS // 2
    d = np.arange(4 * REL_MAX_DIST)
    large = exact + (np.log(np.maximum(d, exact).astype(np.float32) / exact) / math.log(REL_MAX_DIST / exact)
                     * (REL_BUCKETS - exact)).astype(np.int32)
    b = np.where(d < exact, d, np.minimum(large, REL_BUCKETS - 1))
    return [int(np.argmax(b >= k)) for k in range(REL_BUCKETS)]


CONST_COLS = {}


def constants():
    p = np.arange(P)
    q = np.arange(S)
    out = {}
    out["ident"] = np.eye(P)
    out["ones"] = np.ones((P, P))
    half, inv1 = 8, (500000.0 ** (-np.arange(0, 16, 2, dtype=np.float32) / 16)).astype(np.float32)
    r = p % HD
    partner = np.where(r < half, p + half, np.where(r < 2 * half, p - half, p))
    out["swap1"] = (p[:, None] == partner[None, :]).astype(np.float32)
    ang = (q.astype(np.float32)[None, :] * inv1[r % half][:, None]).astype(np.float32)
    rot = (r < 2 * half)[:, None]
    out["cos1"] = np.where(rot, np.cos(ang), 1.0)
    out["sin1"] = np.where(rot, np.where((r < half)[:, None], -1.0, 1.0) * np.sin(ang), 0.0)
    partner2 = np.where(r < FREQS, p + FREQS, p - FREQS)
    out["swap2"] = (p[:, None] == partner2[None, :]).astype(np.float32)
    inv2 = (10000.0 ** (-np.arange(0, HD, 2, dtype=np.float32) / HD)).astype(np.float32)
    out["inv_freq"] = inv2[r % FREQS][:, None]
    out["sin_sign"] = np.where(r < FREQS, -1.0, 1.0)[:, None]
    out["neg_causal"] = np.where(p[None, :] <= p[:, None], 0.0, NEG)
    out["neg_strict"] = np.where(p[None, :] < p[:, None], 0.0, NEG)
    out["chunk_keep"] = np.broadcast_to((q % CHUNK != 0).astype(np.float32), (P, S))
    s_, t_ = p[:, None], p[None, :]
    same = (s_ // CHUNK) == (t_ // CHUNK)
    masks = [s_ == t_]
    for lv in range(LEVELS):
        h = 1 << lv
        masks.append(same & (s_ // (2 * h) == t_ // (2 * h)) & (s_ % (2 * h) < h) & (t_ % (2 * h) >= h))
    out["level_masks"] = np.concatenate([m.astype(np.float32) for m in masks], 1)
    col, parts = 0, []
    for name, a in out.items():
        a = np.ascontiguousarray(a, np.float32)
        CONST_COLS[name] = (col, a.shape[1])
        col += a.shape[1]
        parts.append(a)
    return np.ascontiguousarray(np.concatenate(parts, 1))


N_CONST = constants().shape[1]
CONST_AT = CONST_COLS
STAGED_Z = 2 * P + S
CONST_USED = N_CONST - STAGED_Z - (LEVELS + 1) * P
OFF = [P * t * (t + 1) // 2 for t in range(NT + 1)]
BUCKET_STARTS = bucket_starts()
N_BIAS = 4 * NT * (REL_BUCKETS - 1)
N_PREP = 4
BIAS_RATES = {"A": 2.0, "B": 0.95, "C": 0.95}
RATES = {"A": 1.1, "B": 2.4, "C": 2.6, "I": 2.7, "M": 0.62, "X": 0.62}
N_DOWN = (KF + 3) // 4
IDX_SCALE = HD ** -0.5 * IDX_HEADS ** -0.5
SPARSE_SCALE = P ** -0.5
MLA_SCALE = 192 ** -0.5
LB_FLOOR = 1e-30
LOG_SCALE = 2.0 ** 50
STRUCK = -3e38
MAGIC = 1.5 * 2.0 ** 23
PI_F = 3.1415925


def split_two_pi():
    rest, parts = 2 * math.pi, []
    for bits in (8, 11):
        unit = 2.0 ** (math.floor(math.log2(rest)) - bits + 1)
        parts.append(math.floor(rest / unit) * unit)
        rest -= parts[-1]
    return parts + [rest]


TWO_PI = split_two_pi()


def NT_BIAS(t, b):
    return t * (REL_BUCKETS - 1) + REL_BUCKETS - 1 - b


class Count:

    def __init__(self, sem):
        self.sem, self.n = sem, 0

    def on(self, ins, k=1):
        ins.then_inc(self.sem, k)
        self.n += k
        return self.n


def plan(only_block1=False):
    steps, groups, slabs, items, units = [], [], [], [], []

    def slab(name, **kw):
        slabs.append(dict(name=name, last=None, extra=[], **kw))
        slot_for(len(slabs) - 1)
        return len(slabs) - 1

    def group(kind, slab=None, **kw):
        g = len(groups)
        groups.append(dict(kind=kind, slab=slab, g=g, **kw))
        if slab is not None:
            slabs[slab]["last"] = g
            if state["mid"] and kw.get("K") == KD:
                steps.append(("half", g))
                groups[g]["split"] = True
                state["mid"]()
        steps.append(("group", g))
        return g

    def slot_for(i):
        s_ = slabs[i]
        s_["slot"] = state["slots"][state["turn"] % len(state["slots"])]
        state["turn"] += 1
        before = [j for j in range(i) if slabs[j]["slot"] == s_["slot"]]
        s_["prev"] = before[-1] if before else None
        s_["nth"] = len(before)

    stages = [("scores", 0), ("soft1", 0), ("soft2", 1), ("trans", 2), ("pv", 3)]
    state = dict(lo=0, n=0, fin=0, slots=list(range(W_SLOTS)), turn=0, bias=0, bias_due=0.0, squared=None, mid=None)
    bias_steps = [(t, b) for t in range(NT) for b in range(REL_BUCKETS - 1, 0, -1)]

    def tick():
        n = state["n"]
        for name, lag in stages:
            if state["lo"] <= n - lag < len(items):
                it = items[n - lag]
                if it["kind"] == "I" and lag >= 2:
                    continue
                steps.append((name, n - lag))
                if name == "soft2" and it["kind"] == "I" and it["head"] == IDX_HEADS - 1:
                    steps.append(("topk", it["tile"]))
        state["bias_due"] += BIAS_RATES.get(items[min(n, len(items) - 1)]["kind"], 2)
        while state["bias_due"] >= 1:
            state["bias_due"] -= 1
            if state["bias"] < len(bias_steps) and not only_block1:
                steps.append(("bias", bias_steps[state["bias"]]))
                state["bias"] += 1
        if state["squared"] is not None:
            group("meansq", unit=state["squared"])
            steps.append(("fin2", state["squared"]))
            state["squared"] = None
        while state["fin"] < len(units) and units[state["fin"]]["last"] <= n - 4:
            u = state["fin"]
            steps.append(("fin", u))
            if units[u]["kind"] == "A":
                state["squared"] = u
            state["fin"] += 1
        state["n"] += 1

    def flush():
        while state["fin"] < len(units) or state["n"] < len(items) + 4 or state["squared"] is not None:
            tick()
        state["lo"] = state["n"] = len(items)

    def add_items(its):
        for it in its:
            it["n"] = len(items)
            items.append(it)
            if it.get("unit") is not None:
                units[it["unit"]]["last"] = it["n"]

    def weave(jobs, new_items):
        base = len(items)
        add_items(new_items)
        due = dict(done=0, credit=0.0, gain=0.0)

        def ticks(most):
            due["credit"] = min(due["credit"] + due["gain"], 3.0)
            while due["credit"] >= 1 and most and state["n"] < len(items) \
                    and items[state["n"]]["after"] <= due["done"]:
                tick()
                due["credit"] -= 1
                most -= 1

        def between():
            if items[min(state["n"], len(items) - 1)]["kind"] in "BC" and state["squared"] is None:
                ticks(1)

        for fn, weight, needs in jobs:
            while state["n"] < base + needs:
                tick()
            due["gain"] = weight * RATES[items[min(state["n"], len(items) - 1)]["kind"]] / 2
            state["mid"] = between if state["n"] < len(items) and items[state["n"]]["kind"] in "BC" else None
            if state["mid"] is None:
                due["credit"] += due["gain"]
            fn()
            state["mid"] = None
            due["done"] += 1
            ticks(3)

    for t in range(NT + 1):
        if t < NT:
            steps.append(("ln_in", t))
        if t:
            for half in range(2):
                group("to_hT", tile=t - 1, half=half)
    steps.append(("prep", 0))
    rope_n, gate_n = 0, 0
    for l in range(DEPTH):
        sv = slab("av", layer=l)
        sq = slab("aq", layer=l)
        sk = slab("ak", layer=l)
        for t in range(NT):
            group("T", sv, c0=0, N=512, K=KD, tile=t, dst=("V", 0), layer=l)
        steps.append(("layer", l))

        raws = {}

        def rope_raw(h, i, l=l, s2=(sq, sk), raws=raws):
            raws[i] = group("F", s2[i], c0=128 * h, M=P, K=KD, dst=("raw", i), scale=HD ** -0.5 if i == 0 else 1.0,
                            layer=l)

        def rope_turn(h, i, raws=raws):
            group("swap", raw=raws[i], dst=("qk", 2 * h + i), ring=i, table=0)

        def rope_two(h):
            rope_raw(h, 1)
            rope_turn(h, 0)

        rope_raw(0, 0)
        rope_two(0)
        rope_turn(0, 1)
        jobs = []
        for h in range(1, 4):
            jobs += [(lambda h=h: rope_raw(h, 0), 1, 0), (lambda h=h: rope_two(h), 1.1, 0),
                     (lambda h=h: rope_turn(h, 1), 0.1, 0)]

        hold = {}

        def vv(t, l=l):
            if t == 0:
                hold["bv"] = slab("bvcv", layer=l)
            group("T", hold["bv"], c0=0, N=512, K=KD, tile=t, dst=("V", 512), layer=l)

        for t in range(NT):
            jobs.append((lambda t=t: vv(t), 1, 0))

        def cum_groups(l=l):
            group("F", hold["bv"], c0=512, M=4, K=KD, dst=("cumlog", 0), layer=l)
            for h in range(4):
                group("spread_cum", head=h)
            group("turn_cum")

        jobs.append((cum_groups, 1.5, 0))

        def bqk(c, i, l=l):
            if c == 0 and i == 0:
                hold["bqk"] = slab("bqk", layer=l)
            group("F", hold["bqk"], c0=256 * i + 128 * c, M=P, K=KD, dst=("qk", 2 * c + i),
                  scale=HD ** -0.5 if i == 0 else 1.0, layer=l)

        for c in range(2):
            for i in range(2):
                jobs.append((lambda c=c, i=i: bqk(c, i), 1, 4 * (c + 1)))

        def cqk(c, i, l=l):
            if c == 0 and i == 0:
                hold["cqk"] = slab("cqk", layer=l)
            group("F", hold["cqk"], c0=256 * i + 128 * c, M=P, K=KD, dst=("qk", 4 + 2 * c + i),
                  scale=HD ** -0.5 if i == 0 else 1.0, layer=l)

        for c in range(2):
            for i in range(2):
                jobs.append((lambda c=c, i=i: cqk(c, i), 1, 4 * (c + 3)))

        def gate(c, l=l):
            if c == 0:
                hold["ag"] = slab("ag", layer=l)
            if c == 6:
                hold["ag"] = slab("bgcg", layer=l)
            g = group("gate", hold["ag"], c0=128 * (c % 4), M=P, K=KD, chunk=c, layer=l, first=c >= 6)
            steps.append(("gate2", g))
            steps.append(("gate3", g))

        for c in (0, 1, 2, 3, 6, 7, 4, 5):
            need = 0 if c >= 6 else 4 * (c + 1) + 6 if c < 4 else 16 + 8 * (c - 3) + 5
            jobs.append((lambda c=c: gate(c), 1, need))
        its = []
        for h in range(4):
            units.append(dict(kind="A", chunk=h, layer=l))
            for t in range(NT):
                its.append(dict(kind="A", head=h, tile=t, K=P * (t + 1), maps=2, unit=len(units) - 1,
                                rows=(0, P), q=2 * h, k=2 * h + 1, v=(128 * h, 128), after=3 * h))
        for kind, base in (("B", 0), ("C", 2)):
            for c in range(2):
                units.append(dict(kind=kind, chunk=4 + base + c, layer=l))
                for e in range(2):
                    for t in range(NT):
                        its.append(dict(kind=kind, head=2 * c + e, tile=t, K=P * (t + 1), maps=1,
                                        unit=len(units) - 1, rows=(64 * e, 64),
                                        q=2 * (c + base), k=2 * (c + base) + 1,
                                        v=(512 + 128 * (c + base) + 64 * e, 64),
                                        after=(14 + 2 * (c + 1) if kind == "B" else 18 + 2 * (c + 1))))
        weave(jobs, its)
        flush()
        wo = [slab("wo", layer=l, half=h) for h in range(2)]
        for t in range(NT):
            for half in range(2):
                group("T", wo[half], c0=0, N=512, K=KD, tile=t, dst=("resid", half), src="y", layer=l)
            steps.append(("ln", (l, t)))
            if t:
                for half in range(2):
                    group("to_hT", tile=t - 1, half=half, layer=l)
        for half in range(2):
            group("to_hT", tile=NT - 1, half=half, layer=l)
    if not only_block1:
        second(steps, groups, slabs, items, units, state, slab, group, weave, flush)
    annotate(steps, groups, items, units)
    return dict(steps=steps, groups=groups, slabs=slabs, items=items, units=units)


def second(steps, groups, slabs, items, units, state, slab, group, weave, flush):
    l = DEPTH
    for t in range(NT + 1):
        if t < NT:
            steps.append(("norm", dict(tile=t, row=0, nth=t)))
        if t:
            for half in range(2):
                group("to_hT", tile=t - 1, half=half, norm=t - 1)
    steps.append(("bounds", 0))
    steps.append(("angles", 0))
    state["slots"] = [0, 1]
    s_iq = slab("iq", K=KD, cols=512)
    s_ak = slab("avak", K=KD, cols=392)
    for c in range(4):
        group("F", s_iq, c0=128 * c, M=P, K=KD, dst=("qk", 4 + c), scale=1.0)
    steps.append(("sines", 0))
    group("F", s_ak, c0=264, M=P, K=KD, dst=("ik", 0), scale=1.0)
    for t in range(NT):
        group("T", s_ak, c0=0, N=136, K=KD, tile=t, dst=("av", 0))
    hold, made = {}, {}

    def from_slab(name, new, K=KD, cols=512):
        if new:
            made[name] = made.get(name, -1) + 1
            hold[name] = slab(name, K=K, cols=cols, nth_of_kind=made[name])
        return hold[name]

    jobs = [(lambda: group("F", s_ak, c0=136, M=P, K=KD, dst=("ak", 0), scale=1.0), 1, 0)]
    for c in range(4):
        jobs.append((lambda c=c: group("F", from_slab("saq", c == 0), c0=128 * c, M=P, K=KD, dst=("qk", c), scale=1.0), 1, 0))
    for c in range(3):
        jobs.append((lambda c=c: group("F", from_slab("mq", c == 0, cols=384), c0=128 * c, M=P, K=KD,
                                       dst=("cq", c), scale=1.0), 1, 0))
    for c in range(2):
        jobs.append((lambda c=c: group("F", from_slab("mkv", c == 0, cols=384), c0=128 * c, M=P, K=KD,
                                       dst=("ckv", c), scale=1.0), 1, 0))
    rot = {}

    def kpe():
        rot["kpe"] = group("F", hold["mkv"], c0=256, M=P, K=KD, dst=("raw", 0), scale=1.0)

    jobs.append((kpe, 1, 0))
    for t in range(NT):
        jobs.append((lambda t=t: group("T", from_slab("hi", t == 0), c0=0, N=512, K=KD, tile=t, dst=("V", 512)), 1, 0))
    its = [dict(kind="I", head=h, tile=t, K=P * (t + 1), maps=1, unit=None, after=0)
           for t in range(1, NT) for h in range(IDX_HEADS)]
    weave(jobs, its)
    flush()
    steps.append(("squares", "cq"))
    group("sumsq", what="cq", K=3)
    steps.append(("latent", "cq"))
    steps.append(("squares", "ckv"))
    group("sumsq", what="ckv", K=2)
    steps.append(("latent", "ckv"))
    group("swap", raw=rot["kpe"], dst=("kpe", 0), ring=0, table=1)
    s_qb = slab("qb", K=3, cols=768)
    s_kv = slab("kvb", K=2, cols=1024)
    raws = [group("F", s_qb, c0=512 + 128 * c, M=P, K=3, src="cq", dst=("raw", c), scale=1.0) for c in range(2)]
    for h in range(4):
        group("F", s_qb, c0=128 * h, M=P, K=3, src="cq", dst=("qn", h), scale=1.0)
        if h == 0:
            group("swap", raw=raws[0], dst=("qp", 0), ring=0, table=1)
        if h == 1:
            group("swap", raw=raws[1], dst=("qp", 1), ring=1, table=1)
    for h in range(4):
        group("F", s_kv, c0=128 * h, M=P, K=2, src="ckv", dst=("kn", h), scale=1.0)
    for t in range(NT):
        group("T", s_kv, c0=512, N=512, K=2, tile=t, src="ckv", dst=("V", 0))
    jobs = []

    def hgrn_q(h):
        hold["last_hgrn"] = hold.get("hgrn")
        group("F", from_slab("hgrn", True, cols=384), c0=128, M=P, K=KD, dst=("hq", 0), scale=P ** -0.5)

    def hgrn_f(h):
        group("F", hold["hgrn"], c0=0, M=P, K=KD, dst=("hf", 0), scale=1.0)

    def hgrn_project(h):
        hgrn_q(h)
        hgrn_f(h)

    def hgrn_level(h, lv):
        if lv + 1 < LEVELS:
            steps.append(("hg_level", (h, lv + 1)))
            steps.append(("hg_diff", (h, lv + 2)))
        else:
            steps.append(("hg_decay", h))
        g = group("hg_attn", head=h, level=lv)
        steps.append(("hg_put", g))

    def hgrn_state(h):
        group("hg_turn", head=h)
        if h < 3:
            hgrn_q(h + 1)
        gs = [group("hg_state", head=h, part=i) for i in range(2)]
        if h < 3:
            hgrn_f(h + 1)
        steps.append(("hg_chain", (h, gs)))
        hold["states"] = gs

    def hgrn_out(h):
        hold["hgout"] = group("hg_out", head=h, states=hold["states"])
        g = hgrn_gate(h)
        group("hg_meansq", head=h)
        steps.append(("hg_norm", h))
        steps.append(("gate3", g))

    def hgrn_gate(h):
        g = group("gate", hold["last_hgrn"] if h < 3 else hold["hgrn"], c0=256, M=P, K=KD, chunk=4 + h, layer=l,
                  first=False, unit=None)
        steps.append(("gate2", g))
        return g

    for h in range(4):
        if h == 0:
            jobs.append((lambda h=h: hgrn_project(h), 2, 0))
        jobs.append((lambda h=h: steps.extend([("hg_gates", h), ("hg_diff", (h, 0))]), 1, 0))
        for lv in range(-1, LEVELS):
            jobs.append((lambda h=h, lv=lv: hgrn_level(h, lv), 1, 0))
        jobs.append((lambda h=h: hgrn_state(h), 1.5, 0))
        jobs.append((lambda h=h: hgrn_out(h), 2.5, 0))
    its = []
    for kind in "MX":
        for h in range(4):
            units.append(dict(kind=kind, chunk=h, layer=l))
            for t in range(NT):
                its.append(dict(kind=kind, head=h, tile=t, K=P * (t + 1), maps=1, unit=len(units) - 1,
                                rows=(0, P), q=h, k=None, v=(128 * h if kind == "M" else 0, 128), after=0))
    weave(jobs, its)
    flush()
    state["slots"] = [0, 1, 2]
    first2 = True
    for b, (name, src) in enumerate((("w_up_a_2", "ya"), ("w_up_b_2", "yb"), ("w_up_c_2", "oc"))):
        s_up = None
        for c in range(8):
            if c % 4 == 0:
                s_g = slab("gates", K=KD, cols=512, at=1024 * b + 512 * (c // 4))
                slabs[s_g]["extra"] = [("group", hold["hgout"]), ("scores", len(items) - 1)]
            if c == 0:
                s_up = slab("up", K=4, cols=1024, what=name)
                slabs[s_up]["extra"] = [("group", hold["hgout"]), ("scores", len(items) - 1)]
            group("sigmoid", s_g, c0=128 * (c % 4), M=P, K=KD, ring=c % 2)
            group("up", s_up, c0=128 * c, M=P, K=4, src=src, branch=b, chunk=c, ring=c % 2)
    wo = [slab("wo2", K=KD, cols=512, half=h) for h in range(2)]
    for t in range(NT):
        for half in range(2):
            group("T", wo[half], c0=0, N=512, K=KD, tile=t, dst=("resid2", half), src="mix")
        steps.append(("norm", dict(tile=t, row=0, nth=NT + t)))
        if t:
            for half in range(2):
                group("to_hT", tile=t - 1, half=half, norm=NT + t - 1)
    for half in range(2):
        group("to_hT", tile=NT - 1, half=half, norm=2 * NT - 1)
    for c in range(KF):
        if c % 4 == 0:
            if c < 20:
                s_g = slab("ffg", K=KD, cols=512, at=128 * c)
                s_u = slab("ffu", K=KD, cols=512, at=128 * c)
            else:
                s_g = s_u = slab("ffgu", K=KD, cols=512, at=128 * c)
        off = 128 * (c % 4)
        g = group("ffgate", s_g, c0=off, M=P, K=KD, ring=c % 2)
        u = group("ffup", s_u, c0=off + (256 if c >= 20 else 0), M=P, K=KD, chunk=c, ring=c % 2, gate=g)
    n_down = (KF + 3) // 4
    for i in range(n_down):
        k = min(4, KF - 4 * i)
        sl = slab("down", K=k, cols=1024, at=4 * i)
        slabs[sl]["last_down"] = i
        steps.append(("down", dict(i=i, K=k, slab=sl, last=i == n_down - 1)))
    for t in range(NT):
        steps.append(("final", t))


def annotate(steps, groups, items, units):
    count = {}

    def nth(key):
        count[key] = count.get(key, 0) + 1
        return count[key]

    hT_groups, tile_groups, norms = [], {}, 0
    slot, values, cums, seen = {}, {}, {}, {}
    ffups, resid2, turned_norm = [], {}, {}
    last_gate, done, order = None, {}, []
    for i, u in enumerate(units):
        u["sem"] = u["kind"] if u["kind"] in "AC" else "other"
        u["nth"] = nth(u["sem"])
        if u["kind"] == "C":
            done[(u["layer"], u["chunk"])] = ("unit", i)
    for op, arg in steps:
        if op == "gate3" and not groups[arg]["first"]:
            order.append((groups[arg]["layer"], groups[arg]["chunk"]))
        if op == "fin" and units[arg]["kind"] == "C":
            u = units[arg]
            order.append((u["layer"], u["chunk"]))
            u["gate"] = max(g["g"] for g in groups if g["kind"] == "gate" and (g["layer"], g["chunk"]) == order[-1])
            assert any(s_ == ("gate3", u["gate"]) for s_ in steps[:steps.index((op, arg))])
        if op in ("ln_in", "ln"):
            norms += 1
            seen[arg if op == "ln_in" else arg[1]] = norms
        elif op == "group":
            gr = groups[arg]
            kind, dst = gr["kind"], gr.get("dst") or ("", 0)
            if kind == "to_hT":
                if "norm" not in gr:
                    gr["after_ln"] = seen[gr["tile"]]
                hT_groups = (hT_groups + [arg])[-2:]
                tile_groups[gr["tile"]] = tile_groups.get(gr["tile"], [])[-1:] + [arg]
            gr["hT_group"], gr["hT_tile"] = list(hT_groups), list(tile_groups.get(gr.get("tile"), []))
            if dst[0] == "raw":
                gr["raw_free"] = count.get("swap", 0)
            if kind == "swap":
                gr["nth"] = nth("swap")
                slot[dst] = ("rot", gr["nth"])
                gr["tg_gate"] = last_gate
            if kind == "F" and dst[0] not in ("raw", "cumlog"):
                slot[dst] = ("group", arg)
            if dst[0] in ("V", "av"):
                values[(dst, gr["tile"])] = arg
            if dst[0] == "cumlog":
                gr["nth"] = nth("cumlog")
            if kind == "spread_cum":
                cums[gr["head"]] = arg
                gr["nth"] = count["cumlog"]
            if kind == "turn_cum":
                cums["turn"] = arg
            if kind == "gate":
                gr["nth"] = nth("gate")
                gr["tg_rot"] = count.get("swap", 0)
                gr["last_gate"] = last_gate
                if gr["first"]:
                    last_gate = ("group", arg)
                else:
                    last_gate = ("gated", nth("gated"))
                    done[(gr["layer"], gr["chunk"])] = last_gate
                if gr["layer"] < DEPTH:
                    gr["unit"] = max(i for i, u in enumerate(units)
                                     if u["chunk"] == gr["chunk"] and u["layer"] == gr["layer"])
            if kind == "meansq":
                units[gr["unit"]]["meansq"] = arg
                gr["nth"] = units[gr["unit"]]["nth"]
            if kind in ("gate", "ffgate"):
                gr["min_nth"] = nth("min")
            if kind == "ffup":
                ffups.append(arg)
            if kind == "ffgate":
                gr["free"] = ffups[-2] if len(ffups) >= 2 else None
            if dst[0] == "resid2":
                resid2[gr["tile"]] = resid2.get(gr["tile"], []) + [arg]
            if "norm" in gr:
                turned_norm[gr["norm"]] = arg + 1
            if kind in ("sigmoid", "up", "ffgate", "ffup", "hg_state", "hg_attn", "hg_turn", "hg_out"):
                gr["nth"] = nth(kind)
            if dst[0] in ("hf", "hq"):
                slot[dst[0]] = ("group", arg)
            if gr.get("src") == "y":
                gr["order"] = [(c, done[(gr["layer"], c)]) for c in sorted(range(KD), key=lambda c: order.index((gr["layer"], c)))]
            if gr.get("src") == "yb":
                gr["done"] = done[(DEPTH, 7)]
            gr["slots"] = dict(slot) if kind.startswith("hg_") else None
            gr["vals"] = dict(values) if kind.startswith("hg_") else None
        elif op == "norm":
            if arg["nth"] >= NT:
                arg["groups"] = resid2[arg["tile"]]
            if arg["nth"] >= 2:
                arg["turned"] = turned_norm[arg["nth"] - 2]
        elif op == "scores":
            it = items[arg]
            kind, h = it["kind"], it["head"]
            if kind in "ABC":
                names = [("qk", it["q"]), ("qk", it["k"])]
                vkey = ("V", 0 if it["v"][0] < 512 else 512)
            elif kind == "I":
                names, vkey = [("qk", 4 + h // 2), ("ik", 0)], None
            elif kind == "M":
                names, vkey = [("qn", h), ("kn", h), ("qp", h // 2), ("kpe", 0)], ("V", 0)
            else:
                names, vkey = [("qk", h), ("ak", 0)], ("av", 0)
            it["operands"] = [slot[n] for n in names]
            if vkey:
                it["values"] = [values[(vkey, t)] for t in range(it["tile"] + 1)][-2:]
            if kind == "B":
                it["cums"] = [cums[h], cums["turn"]]


def two_blocks(nc, a, out, only_block1=False):
    pl = plan(only_block1)
    steps, groups, slabs, items, units = (pl[k] for k in ("steps", "groups", "slabs", "items", "units"))

    def passed(kinds):
        at, c = [], 0
        for it in items:
            c += it["kind"] in kinds
            at.append(c)
        return at

    soft1_at, stick_at, turned_at = passed("ABXM"), passed("C"), passed("ABCXM")
    first_map, m = [], 0
    for it in items:
        first_map.append(m)
        m += it["maps"]
    owner = [n for n, it in enumerate(items) for _ in range(it["maps"])]

    def before(n, back):
        i = turned_at[n] - back
        return next((k for k in range(n) if turned_at[k] == i and items[k]["kind"] != "I"), None) if i > 0 else None

    def use(g):
        return g // PROJ_BANKS + 1

    with ExitStack() as ctx:
        def sb(name, shape, dt=F32):
            return ctx.enter_context(nc.sbuf_tensor(name, shape, dt))

        def sem(name):
            return ctx.enter_context(nc.semaphore(name))

        W = sb("weights", [P, W_SLOTS, KD * 512])
        bf_w = sb("bf_weights", [P, KD, 4])
        hT = sb("hT", [P, KD, S])
        h_tok = sb("h_tok", [P, NT, D])
        qk = sb("qk", [P, 8, S])
        V = sb("V", [P, NT, 1024])
        y = sb("y", [P, KD, S])
        E = sb("E", [P, 2, 2, S])
        PR = sb("probs", [P, 3, S])
        PT = sb("probs_T", [P, 2, S])
        L = sb("logits", [P, 2, S])
        raw = sb("raw", [P, 2, S])
        tg = sb("tg", [P, 2, S])
        z = sb("z", [P, D])
        RC = sb("rows_or_spread", [P, 4, S])
        rows = RC[:, :, :].rearrange("p (a b) c -> p a (b c)", a=2)
        ckb = RC
        oc = RC
        CN = sb("constants", [P, CONST_USED])
        identb = sb("identb", [P, P], BF16)
        negb = sb("negb", [P, 2, P], BF16)
        small = sb("small", [P, 256])
        cols = [0]

        def col(n):
            c = cols[0]
            cols[0] += n
            return small[:, c:c + n]

        sums, nmax, rsum = col(4), col(4), col(4)
        c2, mv, lnv, eps = col(2), col(2), col(2), col(3)
        stats = col(12)
        lam_s, lam, gcol, gin, bfc = col(8), col(1), col(1), col(DEPTH), col(DEPTH)
        cqc = sb("cum_by_query", [P, NT, 4])
        lam_in = sb("lam_in", [P, 4, HD])
        cum, cum_min = z[0:4, 0:S], z[0:4, S:2 * S]
        cum_l = y[0:4, 7, :]

        masks8 = sb("level_masks", [P, (LEVELS + 1) * P], U8)
        keep = sb("chunk_keep", [P, S], BF16)
        bias = sb("rel_bias", [P, 4, OFF[NT]])
        X2 = sb("index_and_shared", [P, 3, S])
        akT, avv, ikT = X2[:, 0, :], X2[:, 1, :].rearrange("p (t n) -> p t n", t=NT), X2[:, 2, :]
        iw = col(NT * IDX_HEADS).rearrange("p (t h) -> p t h", h=IDX_HEADS)
        m8, ss, dec = col(8), col(2), col(NCH)
        mq_g, mkv_g, out_g, lbx, lbs = col(3), col(2), col(1), col(4), col(4)
        log_lb, l1p, oml, l1a = col(4), col(4), col(4), col(4)
        X = W[:, 2, :].rearrange("p (c n) -> p c n", n=S)
        cqT, ckvT, qp, kpe = X[:, 0:3, :], X[:, 3:5, :], X[:, 5:7, :], X[:, 7, :]
        flat = h_tok[:, :, :].rearrange("p t (a n) -> p (t a) n", n=S)
        qn, kn = flat[:, 0:4, :], flat[:, 4:8, :]
        hF, hA, hK, hQ = (qk[:, 4 + i, :] for i in range(4))
        hB, hG, hQD, hKE, hATT = (X[:, i, :] for i in range(5))
        hQT, hKT = [hQD, z[:, 0:S]], [hKE, z[:, S:2 * S]]
        states = raw[:, :, :].rearrange("p a (b v) -> p (a b) v", v=P)
        mix = V[:, :, :].rearrange("p t (a n) -> p (t a) n", n=S)
        nz = [z[:, :], L[:, :, :].rearrange("p a n -> p (a n)")]
        final = nz + [E[:, i, :, :].rearrange("p a n -> p (a n)") for i in range(2)]
        pkb, below = X2[:, 0, :], [X2[:, 1, :], X2[:, 2, :]]
        pos_i = sb("pos_i", [P, NT], I32)
        pq = col(NT)
        deltas = sb("bias_deltas", [P, REL_BUCKETS, 4])
        starts = sb("bucket_limits", [P, NT])
        acts = [y[:, c, :] for c in range(8)] + [qk[:, c, :] for c in range(8)] + [mix[:, c, :] for c in range(8)]
        x_spill = nc.dram_tensor("x_spill", (S, D), F32, kind="Internal").ap()

        def cn(name):
            c, n = CONST_AT[name]
            return CN[:, c:c + n]

        def b_at(h, t):
            return bias[:, h, OFF[t]:OFF[t + 1]]

        def bank(name):
            return ctx.enter_context(nc.psum_tensor(name, [P, S], F32))

        proj = [bank(f"proj{i}") for i in range(PROJ_BANKS)]
        sc = [bank(f"score{i}") for i in range(SCORE_BANKS)]
        T = bank("turned_probs")
        O = [bank(f"attn_out{i}") for i in range(2)]
        down = [proj[0], proj[1], sc[0], sc[1], sc[2], T, O[0], O[1]]

        loaded = [sem(f"weights_loaded{i}") for i in range(W_SLOTS)]
        consts_in, staged_in, x_in, rows_in, lam_loaded = (
            sem("consts_in"), sem("staged_in"), [sem(f"x_in{t}") for t in range(NT)], sem("rows_in"), sem("lam_loaded"))
        group_full = sem("group_full")
        evac = [sem(f"bank_read{i}") for i in range(PROJ_BANKS)]
        prep, eps_set, ident_in = sem("prep_done"), sem("eps_set"), sem("ident_in")
        N_CONSTS_IN = 16 * (1 + 2 * DEPTH + (0 if only_block1 else 10))
        rot_done = sem("rotated")
        gate_ln, gate_min, gate_sig, gated = sem("gate_ln"), sem("gate_min"), sem("gate_sigmoid"), sem("gated")
        cum_ln, cum_done = sem("cum_ln"), sem("cum_done")
        scores_full, soft1_done, exp_done = sem("scores_full"), sem("soft1_done"), sem("exp_done")
        soft2_done, stick_done = sem("soft2_done"), sem("stick_done")
        turned, turned_out, pv_done = sem("turned"), sem("turned_out"), sem("pv_done")
        o_free = {k: sem(f"unit_done_{k}") for k in ("A", "C", "other")}
        sq_done = sem("squares_done")
        lam_dot, lam_exp, lam_done = sem("lam_dot"), sem("lam_exp"), sem("lam_done")
        var_done, rstd_done, ln_done = sem("var_done"), sem("rstd_done"), sem("ln_done")
        dve_step, act_step = sem("vector_step"), sem("scalar_step")
        stored = sem("stored")
        pos_in, pos_rows_in = sem("pos_in"), sem("pos_rows_in")
        bias_mask, bias_done = sem("bias_mask"), sem("bias_done")
        spilled, x_back = sem("x_spilled"), sem("x_back")
        lb_d, lb_a = sem("lb_vector"), sem("lb_scalar")
        table_a, table_d = sem("rope_table_scalar"), sem("rope_table_vector")
        norm_r, norm_done = sem("norm_rstd"), sem("norm_done")
        lat_sq, lat_done = sem("latent_squares"), sem("latents_normed")
        hg_act, hg_dve, hg_diff, hg_exp, hg_ready = (
            sem("hgrn_scalar"), sem("hgrn_vector"), sem("hgrn_diff"), sem("hgrn_exp"), sem("hgrn_ready"))
        hg_de, hg_kd = sem("hgrn_decay_exp"), sem("hgrn_decayed")
        hg_sq, hg_normed = sem("hgrn_squares"), sem("hgrn_normed")
        mix_done, down_full, hg_ready0 = sem("mix_done"), sem("down_full"), sem("hgrn_cleared")
        fin_sum, fin_done = sem("final_sum"), sem("final_done")

        def halves(x, half, b):
            return x.rearrange("p (n a b) -> p n a b", a=2, b=b)[:, :, half, :]

        def unit_done(eng, u):
            eng.wait_ge(o_free[units[u]["sem"]], units[u]["nth"])

        def bank_of(g):
            return proj[g % PROJ_BANKS], evac[g % PROJ_BANKS]

        def group_waits(eng):
            reached = {}

            def wait(g):
                b, n = g % PROJ_BANKS, use(g)
                if reached.get(b, 0) < n:
                    reached[b] = n
                    eng.wait_ge(evac[b], n)
            return wait

        def passed_token(eng, wait_group, token):
            what, n = token
            if what == "group":
                wait_group(n)
            elif what == "gated":
                eng.wait_ge(gated, n)
            else:
                unit_done(eng, n)

        w_in = a["w_in"].rearrange("l (k p) n -> l p k n", p=P)
        w_out = a["w_out"].rearrange("l (k p) n -> l p k n", p=P)

        def by_k(name):
            return a[name][0].rearrange("(k p) n -> p k n", p=P)

        w2 = by_k("w_in_2") if not only_block1 else None
        in_slabs = {"av": [(AV, 512)], "aq": [(AQ, 512)], "ak": [(AK, 512)],
                    "bvcv": [(BV, 256), (CV, 256), (BFG, 4)], "bqk": [(BQ, 512)], "cqk": [(CQ, 512)],
                    "ag": [(AG, 512)], "bgcg": [(BG, 256), (CG, 256)]}
        in2_slabs = {"iq": [(IQ, 512)], "avak": [(XV, 128), (IW, 8), (XK, 128), (IK, 64), (IK, 64)],
                     "saq": [(XQ, 512)], "mq": [(MQ, 384)], "mkv": [(MKV, 256), (MPE, 64), (MPE, 64)],
                     "hi": [(HI, 512)]}

        def slab_view(i):
            s_ = slabs[i]
            k, n = s_.get("K", KD), s_.get("cols", 512)
            return W[:, s_["slot"], 0:k * n].rearrange("p (k n) -> p k n", k=k)

        def pieces(i):
            s_, v = slabs[i], slab_view(i)
            name = s_["name"]
            got, c = [], 0
            if name == "wo":
                return [(v, w_out[s_["layer"], :, :, 512 * s_["half"]:512 * (s_["half"] + 1)])]
            if name in in_slabs and "layer" in s_:
                for c0, n in in_slabs[name]:
                    dst = bf_w[:, :, :] if n == 4 else v[:, :, c:c + n]
                    got.append((dst, w_in[s_["layer"], :, :, c0:c0 + n]))
                    c += n
                return got
            if name in in2_slabs:
                for c0, n in in2_slabs[name]:
                    got.append((v[:, :, c:c + n], w2[:, :, c0:c0 + n]))
                    c += n
                return got
            if name == "hgrn":
                h = s_["nth_of_kind"]
                return [(v[:, :, 128 * j:128 * j + 128], w2[:, :, c0 + 128 * h:c0 + 128 * h + 128])
                        for j, c0 in enumerate((HF, HQ, HG))]
            if name == "qb":
                w = by_k("mla_w_qb_2")
                for h in range(4):
                    got.append((v[:, :, 128 * h:128 * h + 128], w[:, :, 192 * h:192 * h + 128]))
                    got.append((v[:, :, 512 + 64 * h:576 + 64 * h], w[:, :, 192 * h + 128:192 * h + 192]))
                return got
            if name == "kvb":
                w = by_k("mla_w_kvb_2")
                for h in range(4):
                    got.append((v[:, :, 128 * h:128 * h + 128], w[:, :, 256 * h:256 * h + 128]))
                    got.append((v[:, :, 512 + 128 * h:640 + 128 * h], w[:, :, 256 * h + 128:256 * h + 256]))
                return got
            if name == "gates":
                return [(v, w2[:, :, GATE + s_["at"]:GATE + s_["at"] + 512])]
            if name == "up":
                return [(v, by_k(s_["what"]))]
            if name == "wo2":
                return [(v, by_k("w_out_2")[:, :, 512 * s_["half"]:512 * (s_["half"] + 1)])]
            if name in ("ffg", "ffu"):
                w = by_k("w_ffn_gate_2" if name == "ffg" else "w_ffn_up_2")
                return [(v, w[:, :, s_["at"]:s_["at"] + 512])]
            if name == "ffgu":
                return [(v[:, :, 0:256], by_k("w_ffn_gate_2")[:, :, s_["at"]:D_FF]),
                        (v[:, :, 256:512], by_k("w_ffn_up_2")[:, :, s_["at"]:D_FF])]
            assert name == "down"
            return [(v, by_k("w_ffn_down_2")[:, s_["at"]:s_["at"] + s_["K"], :])]

        landed, total = [], [0] * W_SLOTS
        for i in range(len(slabs)):
            total[slabs[i]["slot"]] += 16 * len(pieces(i))
            landed.append(total[slabs[i]["slot"]])

        last_B = [max((n for n, it in enumerate(items) if it["kind"] == "B" and units[it["unit"]]["layer"] == l))
                  for l in range(DEPTH)]
        last_M = max((n for n, it in enumerate(items) if it["kind"] == "M"), default=None)
        last_up = max((gr["g"] for gr in groups if gr["kind"] == "up"), default=None)
        n_ln = NT * (DEPTH + 1)

        arg_group = {gr["what"]: gr["g"] for gr in groups if gr["kind"] == "sumsq"}
        level_group = {(gr["head"], gr["level"]): gr["g"] for gr in groups if gr["kind"] == "hg_attn"}
        turn_group = {gr["head"]: gr["g"] for gr in groups if gr["kind"] == "hg_turn"}
        head_meansq = {gr["head"]: gr["g"] for gr in groups if gr["kind"] == "hg_meansq"}
        hf_group = [gr["g"] for gr in groups if (gr.get("dst") or ("",))[0] == "hf"]
        hq_group = [gr["g"] for gr in groups if (gr.get("dst") or ("",))[0] == "hq"]
        puts = sorted(level_group.values())
        arg_prev_put = dict(zip(puts[1:], puts[:-1]))

        block = ctx.enter_context(nc.Block())

        @block.sync
        def _(sp):
            for t in range(NT):
                sp.dma_start(h_tok[:, t, :], a["x"][0, t * P:(t + 1) * P, :]).then_inc(x_in[t], 16)
            for i, s_ in enumerate(slabs):
                if s_["prev"] is not None:
                    q = slabs[s_["prev"]]
                    if "last_down" in q:
                        sp.wait_ge(down_full, q["last_down"] + 1)
                    else:
                        sp.wait_ge(group_full, q["last"] + 1)
                if s_["slot"] == 2:
                    for what, n in s_["extra"]:
                        sp.wait_ge(group_full if what == "group" else scores_full, n + 1)
                for dst, src in pieces(i):
                    sp.dma_start(dst, src).then_inc(loaded[s_["slot"]], 16)
            if only_block1:
                sp.wait_ge(ln_done, n_ln)
                for t in range(NT):
                    sp.dma_start(out[0, t * P:(t + 1) * P, :], h_tok[:, t, :]).then_inc(stored, 16)
            else:
                for t in range(NT):
                    sp.wait_ge(fin_done, t + 1)
                    sp.dma_start(out[0, t * P:(t + 1) * P, :], final[t]).then_inc(stored, 16)
            sp.wait_ge(stored, 16 * NT)

        @block.gpsimd
        def _(pool):
            pool.dma_start(rows[:, 0, :], a["ln_in_g"].partition_broadcast(P)).then_inc(rows_in, 16)
            pool.dma_start(rows[:, 1, :], a["ln_in_b"].partition_broadcast(P)).then_inc(rows_in, 16)
            pool.dma_start(CN[:, 0:P], a["constants"][:, 0:P]).then_inc(ident_in, 16)
            pool.dma_start(CN[:, P:], a["constants"][:, P:CONST_USED]).then_inc(consts_in, 16)
            pool.dma_start(z[:, 0:STAGED_Z], a["constants"][:, CONST_USED:CONST_USED + STAGED_Z]).then_inc(staged_in, 16)
            pool.dma_start(raw[:, :, :].rearrange("p a n -> p (a n)")[:, 0:(LEVELS + 1) * P],
                           a["constants"][:, CONST_USED + STAGED_Z:]).then_inc(staged_in, 16)
            for l in range(DEPTH):
                pool.dma_start(gin[:, l:l + 1], a["subln_g"][l].rearrange("(p a) -> p a", a=1)).then_inc(consts_in, 16)
                pool.dma_start(bfc[0:4, l:l + 1], a["b_forget"][l].rearrange("(p a) -> p a", a=1)).then_inc(consts_in, 16)
            if not only_block1:
                for dst, name, n in ((mq_g, "mla_q_norm_2", 3), (mkv_g, "mla_kv_norm_2", 2),
                                     (out_g, "hgrn_out_norm_2", 1), (lbx, "hgrn_lb_logits_2", 4)):
                    for k in range(n):
                        pool.dma_start(dst[:, k:k + 1], a[name][0, P * k:P * k + P].rearrange("(p a) -> p a", a=1))\
                            .then_inc(consts_in, 16)
                for t in range(NT):
                    pool.dma_start(pos_i[:, t:t + 1], a["positions_2"][0, P * t:P * t + P].rearrange("(p a) -> p a", a=1))\
                        .then_inc(pos_in, 16)
                pool.dma_start(below[0].bitcast(I32), a["positions_2"][0].partition_broadcast(P)).then_inc(pos_in, 16)
                pool.dma_start(deltas[:, :, :].rearrange("p b h -> p (b h)"),
                               a["rel_bias_2"].rearrange("b h -> (b h)").partition_broadcast(P)).then_inc(pos_in, 16)
            for l in range(DEPTH):
                if l:
                    pool.wait_ge(lam_done, 2 * l)
                for i, name in enumerate(("lambda_q1", "lambda_k1", "lambda_q2", "lambda_k2")):
                    pool.dma_start(lam_in[:, i, :], a[name][l].partition_broadcast(P)).then_inc(lam_loaded, 16)
                pool.wait_ge(ln_done, NT * (l + 1))
                pool.wait_ge(soft1_done, soft1_at[last_B[l]])
                pool.dma_start(rows[:, 0, :], a["ln_g"][l].partition_broadcast(P)).then_inc(rows_in, 16)
                pool.dma_start(rows[:, 1, :], a["ln_b"][l].partition_broadcast(P)).then_inc(rows_in, 16)
            if not only_block1:
                pool.wait_ge(ln_done, n_ln)
                pool.dma_start(rows[:, 0, :], a["attn_norm_2"][0].partition_broadcast(P)).then_inc(rows_in, 16)
                for t in range(NT):
                    pool.dma_start(x_spill[t * P:(t + 1) * P, :], h_tok[:, t, :]).then_inc(spilled, 16)
                pool.wait_ge(spilled, 16 * NT)
                pool.wait_ge(scores_full, last_M + 1)
                for t in range(NT):
                    pool.dma_start(h_tok[:, t, :], x_spill[t * P:(t + 1) * P, :]).then_inc(x_back, 16)
                pool.wait_ge(group_full, last_up + 1)
                pool.dma_start(rows[:, 0, :], a["ffn_norm_2"][0].partition_broadcast(P)).then_inc(rows_in, 16)
                pool.dma_start(rows[:, 1, :], a["final_norm_2"].partition_broadcast(P)).then_inc(rows_in, 16)

        @block.tensor
        def _(pe):
            pe.wait_ge(ident_in, 16)
            seen = set()
            wait_group = group_waits(pe)

            def weights(i):
                if i not in seen:
                    seen.add(i)
                    pe.wait_ge(loaded[slabs[i]["slot"]], landed[i])
                return slab_view(i)

            for op, arg in steps:
                if op == "prep":
                    pe.wait_ge(consts_in, N_CONSTS_IN)
                    pe.wait_ge(prep, N_PREP)
                elif op in ("group", "half"):
                    gr = groups[arg]
                    g, kind = arg, gr["kind"]
                    ps, _ = bank_of(g)
                    if g >= PROJ_BANKS:
                        wait_group(g - PROJ_BANKS)
                    if gr["slab"] is not None:
                        w = weights(gr["slab"])
                        if (gr.get("dst") or ("",))[0] == "cumlog":
                            w, c0 = bf_w, 0
                        else:
                            c0 = gr["c0"]
                        src = gr.get("src", "hT")
                        if src == "y":
                            pass
                        elif src in ("cq", "ckv"):
                            pe.wait_ge(lat_done, 1 if src == "cq" else 2)
                        elif src in ("yb",):
                            passed_token(pe, wait_group, gr["done"])
                        elif src == "mix":
                            pe.wait_ge(mix_done, 24)
                        elif src in ("ya", "oc"):
                            unit_done(pe, len(units) - 1)
                        else:
                            for gg in (gr["hT_tile"] if kind == "T" else gr["hT_group"]):
                                wait_group(gg)
                        x = {"hT": hT[:, :, :], "y": y[:, :, :], "ya": y[:, 0:4, :], "yb": y[:, 4:8, :], "cq": cqT,
                             "ckv": ckvT, "oc": oc[:, :, :], "mix": mix}[src]
                        begin, end = 0, gr["K"]
                        if op == "half":
                            end = gr["K"] // 2
                        elif gr.get("split"):
                            begin = gr["K"] // 2
                        for i in range(begin, end):
                            k, first, last = i, i == 0, i == gr["K"] - 1
                            if src == "y":
                                k, token = gr["order"][i]
                                passed_token(pe, wait_group, token)
                            if kind == "T":
                                t = gr["tile"]
                                mm = nc.tensor.matmul(ps[:, 0:gr["N"]], x[:, k, t * P:(t + 1) * P],
                                                      w[:, k, c0:c0 + gr["N"]], start=first, stop=last)
                            else:
                                mm = nc.tensor.matmul(ps[0:gr["M"], :], w[:, k, c0:c0 + gr["M"]],
                                                      x[:, k, :], start=first, stop=last)
                        if op == "group":
                            mm.then_inc(group_full, 1)
                    elif kind == "swap":
                        wait_group(gr["raw"])
                        nc.tensor.matmul(ps[:, :], cn(f"swap{gr['table'] + 1}"), raw[:, gr["ring"], :],
                                         start=True, stop=True).then_inc(group_full, 1)
                    elif kind == "spread_cum":
                        pe.wait_ge(cum_done, gr["nth"])
                        h = gr["head"]
                        nc.tensor.matmul(ps[:, :], cn("ident")[0:4, h:h + 1].to_broadcast([4, P]), cum,
                                         start=True, stop=True).then_inc(group_full, 1)
                    elif kind == "turn_cum":
                        for t in range(NT):
                            mm = nc.tensor.transpose(ps[:, 4 * t:4 * t + 4], cum[:, t * P:(t + 1) * P],
                                                     cn("ident")[0:4, 0:4])
                        mm.then_inc(group_full, 1)
                    elif kind in ("meansq", "hg_meansq"):
                        if kind == "meansq":
                            pe.wait_ge(sq_done, gr["nth"])
                        else:
                            pe.wait_ge(hg_sq, gr["head"] + 1)
                        nc.tensor.matmul(ps[:, :], cn("ones"), tg[:, 1, :],
                                         start=True, stop=True).then_inc(group_full, 1)
                    elif kind == "sumsq":
                        pe.wait_ge(lat_sq, 1 if gr["what"] == "cq" else 2)
                        for k in range(gr["K"]):
                            mm = nc.tensor.matmul(ps[:, :], cn("ones"), qn[:, k, :], start=(k == 0),
                                                  stop=(k == gr["K"] - 1))
                        mm.then_inc(group_full, 1)
                    elif kind == "to_hT":
                        t = gr["tile"]
                        if "norm" in gr:
                            pe.wait_ge(norm_done, gr["norm"] + 1)
                            row = nz[gr["norm"] % 2]
                        else:
                            pe.wait_ge(ln_done, gr["after_ln"])
                            row = h_tok[:, t, :]
                        for j in range(4):
                            k = 4 * gr["half"] + j
                            mm = nc.tensor.transpose(ps[:, j * P:(j + 1) * P], row[:, k * P:(k + 1) * P], cn("ident"))
                        mm.then_inc(group_full, 1)
                    elif kind == "hg_attn":
                        h, lv = gr["head"], gr["level"]
                        if lv < 0:
                            pe.wait_ge(hg_dve, 3 * (h + 1))
                            wait_group(gr["slots"]["hq"][1])
                            kk, qq = hK, hQ
                        else:
                            pe.wait_ge(hg_ready, LEVELS * h + lv + 1)
                            kk, qq = hKT[lv % 2], hQT[lv % 2]
                        for i in range(NT):
                            r = slice(i * P, (i + 1) * P)
                            mm = nc.tensor.matmul(ps[:, r], kk[:, r], qq[:, r], start=True, stop=True)
                        mm.then_inc(group_full, 1)
                    elif kind == "hg_turn":
                        pe.wait_ge(hg_kd, gr["head"] + 1)
                        for i in range(NT):
                            r = slice(i * P, (i + 1) * P)
                            mm = nc.tensor.transpose(ps[:, r], hA[:, r], cn("ident"))
                        mm.then_inc(group_full, 1)
                    elif kind == "hg_state":
                        wait_group(turn_group[gr["head"]])
                        for gg in (gr["vals"][(("V", 512), t)] for t in range(NT)):
                            wait_group(gg)
                        v0 = 512 + P * gr["head"]
                        for n in range(gr["part"], NCH - 1, 2):
                            r = slice(64 * (n % 2), 64 * (n % 2) + 64)
                            mm = nc.tensor.matmul(ps[:, (n // 2) * P:(n // 2 + 1) * P],
                                                  hF[r, (n // 2) * P:(n // 2 + 1) * P], V[r, n // 2, v0:v0 + P],
                                                  start=True, stop=True)
                        mm.then_inc(group_full, 1)
                    elif kind == "hg_out":
                        for gg in gr["states"]:
                            wait_group(gg)
                        v0 = 512 + P * gr["head"]
                        for i in range(NT):
                            mm = nc.tensor.matmul(ps[:, i * P:(i + 1) * P], V[:, i, v0:v0 + P],
                                                  hATT[:, i * P:(i + 1) * P], start=True, stop=False)
                            for n in range(max(1, 2 * i), 2 * i + 2):
                                r = slice(CHUNK * n, CHUNK * n + CHUNK)
                                mm = nc.tensor.matmul(ps[:, r], states[:, n, :], hQD[:, r], start=False,
                                                      stop=(n == 2 * i + 1))
                        mm.then_inc(group_full, 1)
                elif op == "scores":
                    it = items[arg]
                    t, K, kind = it["tile"], it["K"], it["kind"]
                    for what, idx in it["operands"]:
                        if what == "rot":
                            pe.wait_ge(rot_done, idx)
                        else:
                            wait_group(idx)
                    for j in range(it["maps"]):
                        m_ = first_map[arg] + j
                        if m_ >= SCORE_BANKS:
                            b = owner[m_ - SCORE_BANKS]
                            kb = items[b]["kind"]
                            if kb in "AMI":
                                pe.wait_ge(exp_done, b + 1)
                            elif kb in "BX":
                                pe.wait_ge(soft1_done, soft1_at[b])
                            else:
                                pe.wait_ge(soft2_done, b + 1)
                        ps = sc[m_ % SCORE_BANKS]
                        tq = slice(t * P, (t + 1) * P)
                        if kind in "ABC":
                            r0, rn = (64 * j, 64) if kind == "A" else it["rows"]
                            r = slice(r0, r0 + rn)
                            nc.tensor.matmul(ps[:, 0:K], qk[r, it["q"], tq], qk[r, it["k"], 0:K], start=True, stop=False)
                            mm = nc.tensor.matmul(ps[:, K - P:K], identb[:, :], negb[:, int(kind == "C"), :],
                                                  start=False, stop=True)
                        elif kind == "I":
                            h = it["head"]
                            r = slice(64 * (h % 2), 64 * (h % 2) + 64)
                            mm = nc.tensor.matmul(ps[:, 0:K], qk[r, 4 + h // 2, tq], ikT[r, 0:K], start=True, stop=True)
                        elif kind == "M":
                            h = it["head"]
                            r = slice(64 * (h % 2), 64 * (h % 2) + 64)
                            nc.tensor.matmul(ps[:, 0:K], qn[:, h, tq], kn[:, h, 0:K], start=True, stop=False)
                            nc.tensor.matmul(ps[:, 0:K], qp[r, h // 2, tq], kpe[r, 0:K], start=False, stop=False)
                            mm = nc.tensor.matmul(ps[:, K - P:K], identb[:, :], negb[:, 0, :], start=False, stop=True)
                        else:
                            mm = nc.tensor.matmul(ps[:, 0:K], qk[:, it["head"], tq], akT[:, 0:K], start=True, stop=True)
                    mm.then_inc(scores_full, 1)
                elif op == "trans":
                    it = items[arg]
                    if it["kind"] == "C":
                        pe.wait_ge(stick_done, stick_at[arg])
                    else:
                        pe.wait_ge(soft2_done, arg + 1)
                    i = turned_at[arg] - 1
                    if i:
                        pe.wait_ge(turned_out, i)
                    for j in range(it["tile"] + 1):
                        mm = nc.tensor.transpose(T[:, j * P:(j + 1) * P], PR[:, i % 3, j * P:(j + 1) * P], cn("ident"))
                    mm.then_inc(turned, 1)
                elif op == "pv":
                    it = items[arg]
                    u, t, i = it["unit"], it["tile"], turned_at[arg] - 1
                    pe.wait_ge(turned_out, i + 1)
                    if u >= 2:
                        unit_done(pe, u - 2)
                    for gg in it["values"]:
                        wait_group(gg)
                    r0, rn = it["rows"]
                    v0, vn = it["v"]
                    for j in range(t + 1):
                        v = avv[:, j, :] if it["kind"] == "X" else V[:, j, v0:v0 + vn]
                        mm = nc.tensor.matmul(O[u % 2][r0:r0 + rn, t * P:(t + 1) * P], v,
                                              PT[:, i % 2, j * P:(j + 1) * P], start=(j == 0), stop=(j == t))
                    mm.then_inc(pv_done, 1)
                elif op == "down":
                    w = weights(arg["slab"])
                    for gg in (len(groups) - 2, len(groups) - 1):
                        wait_group(gg)
                    if arg["i"] == 0:
                        for u in (len(units) - 2, len(units) - 1):
                            unit_done(pe, u)
                    k0 = 4 * arg["i"]
                    for t in range(NT):
                        for k in range(arg["K"]):
                            for half in range(2):
                                mm = nc.tensor.matmul(down[2 * t + half][:, :], acts[k0 + k][:, t * P:(t + 1) * P],
                                                      w[:, k, 512 * half:512 * half + 512],
                                                      start=(k0 + k == 0), stop=(k0 + k == KF - 1))
                        if arg["last"] or t == NT - 1:
                            mm.then_inc(down_full, 1)

        @block.scalar
        def _(act):
            step = Count(act_step)
            wait_group = group_waits(act)
            n_ln_, n_gate, n_sig = 0, 0, 0

            def link(ins):
                act.wait_ge(act_step, step.on(ins))

            def log1p_exp_abs(dst, src, **kw):
                link(nc.scalar.activation(dst, src, ACT.Abs, **kw))
                link(nc.scalar.activation(dst, dst, ACT.Exp, scale=-1.0))
                return nc.scalar.activation(dst, dst, ACT.Ln, bias=1.0)

            def root(dst, src, n, which):
                link(nc.scalar.activation(dst, src, ACT.Ln, scale=1.0 / n, bias=eps[:, which:which + 1]))
                return nc.scalar.activation(dst, dst, ACT.Exp, scale=-0.5)

            nc.scalar.preload_act_table_set(EXP_AND_LN)
            act.wait_ge(eps_set, 3)
            plain = {"qk": lambda d: qk[:, d, :], "ik": lambda d: ikT, "ak": lambda d: akT,
                     "cq": lambda d: cqT[:, d, :], "ckv": lambda d: ckvT[:, d, :], "qn": lambda d: qn[:, d, :],
                     "kn": lambda d: kn[:, d, :], "hf": lambda d: hF, "hq": lambda d: hQ}
            for op, arg in steps:
                if op == "prep":
                    act.wait_ge(consts_in, N_CONSTS_IN)
                    act.wait_ge(prep, N_PREP)
                elif op == "group":
                    gr = groups[arg]
                    g, kind = arg, gr["kind"]
                    ps, read = bank_of(g)
                    dst = gr.get("dst") or ("", 0)
                    if kind in ("swap", "meansq", "hg_meansq", "sumsq", "hg_attn", "hg_state", "up", "ffup") \
                            or dst[0] in ("resid", "resid2"):
                        continue
                    act.wait_ge(group_full, g + 1)
                    if kind == "T" and dst[0] == "V":
                        nc.scalar.activation(V[:, gr["tile"], dst[1]:dst[1] + gr["N"]], ps[:, 0:gr["N"]],
                                             ACT.Copy).then_inc(read, 1)
                    elif kind == "T" and dst[0] == "av":
                        if gr["tile"] == 0:
                            act.wait_ge(bias_done, N_BIAS)
                        nc.scalar.activation(avv[:, gr["tile"], :], ps[:, 0:P], ACT.Copy)
                        nc.scalar.activation(iw[:, gr["tile"], :], ps[:, P:P + IDX_HEADS], ACT.Copy,
                                             scale=IDX_SCALE).then_inc(read, 1)
                    elif kind == "F" and dst[0] == "raw":
                        if gr["raw_free"]:
                            act.wait_ge(rot_done, gr["raw_free"])
                        nc.scalar.activation(raw[:, dst[1], :], ps[:, :], ACT.Copy, scale=gr["scale"]).then_inc(read, 1)
                    elif kind == "F" and dst[0] in plain:
                        if dst[0] in ("ik", "ak"):
                            act.wait_ge(bias_done, N_BIAS)
                        if dst == ("qn", 0):
                            act.wait_ge(spilled, 16 * NT)
                        nc.scalar.activation(plain[dst[0]](dst[1]), ps[:, :], ACT.Copy, scale=gr["scale"])\
                            .then_inc(read, 1)
                    elif kind == "F" and dst[0] == "cumlog":
                        if gr["nth"] > 1:
                            act.wait_ge(cum_done, gr["nth"] - 1)
                        log1p_exp_abs(cum_l, ps[0:4, :], bias=bfc[0:4, gr["layer"]:gr["layer"] + 1]).then_inc(cum_ln, 1)
                    elif kind == "spread_cum":
                        nc.scalar.activation(ckb[:, gr["head"], :], ps[:, :], ACT.Copy).then_inc(read, 1)
                    elif kind == "turn_cum":
                        nc.scalar.activation(cqc[:, :, :], ps[:, 0:4 * NT].rearrange("p (t h) -> p t h", h=4),
                                             ACT.Copy).then_inc(read, 1)
                    elif kind == "to_hT":
                        nc.scalar.activation(hT[:, 4 * gr["half"]:4 * gr["half"] + 4, gr["tile"] * P:(gr["tile"] + 1) * P],
                                             ps[:, :].rearrange("p (k t) -> p k t", k=4), ACT.Copy).then_inc(read, 1)
                    elif kind == "gate":
                        if gr["tg_rot"]:
                            act.wait_ge(rot_done, gr["tg_rot"])
                        if gr["last_gate"]:
                            passed_token(act, wait_group, gr["last_gate"])
                        log1p_exp_abs(tg[:, 0, :], ps[:, :]).then_inc(gate_ln, 1)
                        n_gate += 1
                    elif kind == "sigmoid":
                        e = tg[:, gr["ring"], :]
                        if gr["nth"] > 2:
                            act.wait_ge(mix_done, gr["nth"] - 2)
                        log1p_exp_abs(e, ps[:, :]).then_inc(gate_ln, 1)
                        n_gate += 1
                        act.wait_ge(read, use(g))
                        nc.scalar.activation(e, e, ACT.Exp).then_inc(gate_sig, 1)
                        n_sig += 1
                    elif kind == "ffgate":
                        e = tg[:, gr["ring"], :]
                        if gr["nth"] > 2:
                            wait_group(gr["free"])
                        log1p_exp_abs(e, ps[:, :]).then_inc(gate_ln, 1)
                        n_gate += 1
                        act.wait_ge(gate_min, gr["min_nth"])
                        nc.scalar.activation(e, e, ACT.Exp).then_inc(gate_sig, 1)
                        n_sig += 1
                    elif kind == "hg_turn":
                        nc.scalar.activation(hF, ps[:, :], ACT.Copy).then_inc(read, 1)
                    elif kind == "hg_out":
                        nc.scalar.activation(y[:, 4 + gr["head"], :], ps[:, :], ACT.Copy).then_inc(read, 1)
                        act.wait_ge(read, use(g))
                        if gr["head"]:
                            act.wait_ge(hg_normed, gr["head"])
                        nc.scalar.activation(tg[:, 1, :], y[:, 4 + gr["head"], :], ACT.Square).then_inc(hg_sq, 1)
                elif op == "gate2":
                    act.wait_ge(gate_min, groups[arg]["min_nth"])
                    nc.scalar.activation(tg[:, 0, :], tg[:, 0, :], ACT.Exp).then_inc(gate_sig, 1)
                    n_sig += 1
                elif op == "soft1":
                    n, it = arg, items[arg]
                    K = it["K"]
                    e = E[:, n % 2, :, 0:K]
                    s_ = sc[first_map[n] % SCORE_BANKS][:, 0:K]
                    if n >= 2:
                        act.wait_ge(soft2_done, n - 1)
                    if it["kind"] in "ABXM":
                        act.wait_ge(soft1_done, soft1_at[n])
                    else:
                        act.wait_ge(scores_full, n + 1)
                    c = 2 * (n % 2)
                    if it["kind"] == "A":
                        for j in range(2):
                            ins = nc.scalar.activation(e[:, j, :], sc[(first_map[n] + j) % SCORE_BANKS][:, 0:K], ACT.Exp,
                                                       bias=nmax[:, c + j:c + j + 1], accum_out=sums[:, c + j:c + j + 1])
                    elif it["kind"] in "BX":
                        ins = nc.scalar.activation(e[:, 0, :], L[:, n % 2, 0:K], ACT.Exp, bias=nmax[:, c:c + 1],
                                                   accum_out=sums[:, c:c + 1])
                    elif it["kind"] == "M":
                        ins = nc.scalar.activation(e[:, 0, :], s_, ACT.Exp, bias=nmax[:, c:c + 1], scale=MLA_SCALE,
                                                   accum_out=sums[:, c:c + 1])
                    elif it["kind"] == "C":
                        ins = log1p_exp_abs(e[:, 0, :], s_)
                    else:
                        ins = nc.scalar.activation(e[:, 0, :], s_, ACT.Relu)
                    ins.then_inc(exp_done, 1)
                elif op == "soft2":
                    n, it = arg, items[arg]
                    if it["kind"] == "C":
                        act.wait_ge(soft2_done, n + 1)
                        i = turned_at[n] - 1
                        if i >= 3:
                            act.wait_ge(turned, i - 2)
                        nc.scalar.activation(PR[:, i % 3, 0:it["K"]], L[:, n % 2, 0:it["K"]], ACT.Exp)\
                            .then_inc(stick_done, 1)
                elif op == "trans":
                    n, it = arg, items[arg]
                    i = turned_at[n] - 1
                    act.wait_ge(turned, i + 1)
                    if i >= 2:
                        act.wait_ge(pv_done, i - 1)
                    nc.scalar.activation(PT[:, i % 2, 0:it["K"]], T[:, 0:it["K"]], ACT.Copy).then_inc(turned_out, 1)
                elif op == "fin":
                    u = units[arg]
                    act.wait_ge(pv_done, turned_at[u["last"]])
                    if u["kind"] == "A":
                        if u["nth"] > 1:
                            act.wait_ge(o_free["A"], u["nth"] - 1)
                        nc.scalar.activation(tg[:, 1, :], O[arg % 2][:, :], ACT.Square).then_inc(sq_done, 1)
                    elif u["kind"] != "C":
                        dst = oc if u["kind"] == "M" else y
                        nc.scalar.activation(dst[:, u["chunk"], :], O[arg % 2][:, :], ACT.Copy).then_inc(o_free["other"], 1)
                elif op == "fin2":
                    g = units[arg]["meansq"]
                    act.wait_ge(group_full, g + 1)
                    root(tg[:, 1, :], bank_of(g)[0][:, :], P, 0).then_inc(bank_of(g)[1], 1)
                elif op in ("ln_in", "ln"):
                    n_ln_ += 1
                    act.wait_ge(var_done, n_ln_)
                    link(nc.scalar.activation(lnv[:, 0:1], mv[:, 1:2], ACT.Ln, bias=eps[:, 0:1]))
                    nc.scalar.activation(lnv[:, 1:2], lnv[:, 0:1], ACT.Exp, scale=-0.5).then_inc(rstd_done, 1)
                elif op == "layer":
                    act.wait_ge(lam_dot, 2 * (arg + 1))
                    nc.scalar.activation(lam_s[:, 2:4], lam_s[:, 0:2], ACT.Exp).then_inc(lam_exp, 1)
                elif op == "bounds":
                    act.wait_ge(lb_d, 1)
                    nc.scalar.activation(lbs, lbs, ACT.Exp).then_inc(lb_a, 1)
                    act.wait_ge(lb_d, 2)
                    nc.scalar.activation(l1p, lbx, ACT.Ln, scale=-1.0, bias=1.0)
                    nc.scalar.activation(log_lb, lbs, ACT.Ln, scale=LOG_SCALE).then_inc(lb_a, 1)
                elif op == "sines":
                    for i, name in enumerate(("sin1", "cos1")):
                        act.wait_ge(table_d, i + 1)
                        kw = dict(scale=cn("sin_sign")) if i == 0 else dict(bias=eps[:, 2:3])
                        nc.scalar.activation(cn(name), cn(name), ACT.Sin, **kw).then_inc(table_a, 1)
                    nc.scalar.preload_act_table_set(EXP_AND_LN)
                elif op == "norm":
                    t, k = arg["tile"], arg["nth"]
                    if k < NT:
                        act.wait_ge(ln_done, n_ln)
                    else:
                        for gg in arg["groups"]:
                            wait_group(gg)
                    if k >= 2:
                        act.wait_ge(group_full, arg["turned"])
                        act.wait_ge(norm_done, k - 1)
                    if k in (0, 1):
                        act.wait_ge(stick_done, stick_at[-1])
                        act.wait_ge(ln_done, n_ln)
                    link(nc.scalar.activation(nz[k % 2], h_tok[:, t, :], ACT.Square, accum_out=ss[:, k % 2:k % 2 + 1]))
                    root(ss[:, k % 2:k % 2 + 1], ss[:, k % 2:k % 2 + 1], D, 1).then_inc(norm_r, 1)
                elif op == "squares":
                    src = cqT if arg == "cq" else ckvT
                    if arg == "cq":
                        act.wait_ge(spilled, 16 * NT)
                        for gg in groups:
                            if (gg.get("dst") or ("",))[0] in ("cq", "ckv"):
                                wait_group(gg["g"])
                    else:
                        act.wait_ge(group_full, arg_group["cq"] + 1)
                    n = 3 if arg == "cq" else 2
                    for k in range(n):
                        ins = nc.scalar.activation(qn[:, k, :], src[:, k, :], ACT.Square)
                    ins.then_inc(lat_sq, 1)
                elif op == "latent":
                    g = arg_group[arg]
                    if arg == "ckv":
                        act.wait_ge(lat_done, 1)
                    act.wait_ge(group_full, g + 1)
                    root(tg[:, 1, :], bank_of(g)[0][:, :], 384 if arg == "cq" else 256, 1).then_inc(bank_of(g)[1], 1)
                elif op == "hg_gates":
                    h = arg
                    wait_group(hf_group[h])
                    log1p_exp_abs(hA, hF).then_inc(hg_act, 1)
                    act.wait_ge(hg_dve, 3 * h + 1)
                    nc.scalar.activation(hG, hB, ACT.Exp).then_inc(hg_act, 1)
                    act.wait_ge(hg_dve, 3 * h + 2)
                    log1p_exp_abs(hKE, hA).then_inc(hg_act, 1)
                elif op == "hg_diff":
                    h, lv = arg
                    act.wait_ge(hg_diff, (LEVELS + 1) * h + lv + 1)
                    if lv < LEVELS:
                        nc.scalar.activation(hG[:, 0:256], hG[:, 0:256], ACT.Exp)
                        nc.scalar.activation(hG[:, 256:512], hG[:, 256:512], ACT.Exp, scale=-1.0).then_inc(hg_exp, 1)
                    else:
                        nc.scalar.activation(hG, hG, ACT.Exp).then_inc(hg_exp, 1)
                elif op == "hg_decay":
                    h = arg
                    b8 = hB.rearrange("p (n c) -> p n c", c=CHUNK)
                    act.wait_ge(group_full, level_group[(h, LEVELS - 2)] + 1)
                    nc.scalar.activation(dec, b8[:, :, CHUNK - 1], ACT.Exp)
                    nc.scalar.activation(hQD, hB, ACT.Exp).then_inc(hg_de, 1)
                elif op == "hg_norm":
                    g = head_meansq[arg]
                    act.wait_ge(group_full, g + 1)
                    root(tg[:, 1, :], bank_of(g)[0][:, :], P, 1).then_inc(bank_of(g)[1], 1)
                elif op == "final":
                    t = arg
                    act.wait_ge(fin_sum, t + 1)
                    c = ss[:, t % 2:t % 2 + 1]
                    link(nc.scalar.activation(final[t], h_tok[:, t, :], ACT.Square, accum_out=c))
                    root(c, c, D, 1).then_inc(norm_r, 1)

        @block.vector
        def _(dve):
            step = Count(dve_step)
            wait_group = group_waits(dve)
            n_ln_ = n_cum = n_gate = n_min = n_sig = 0

            def link(ins):
                dve.wait_ge(dve_step, step.on(ins))

            for i, v in enumerate((1e-5, 1e-6, math.pi / 2)):
                nc.vector.memset(eps[:, i:i + 1], v).then_inc(eps_set, 1)
            dve.wait_ge(eps_set, 3)

            def layernorm(src, t, nth, rows_need):
                for i in range(2):
                    ins = nc.vector.bn_stats(stats[:, 6 * i:6 * i + 6], src[:, 512 * i:512 * i + 512])
                link(ins)
                nc.vector.bn_aggr(mv, stats).then_inc(var_done, 1)
                dve.wait_ge(rstd_done, nth)
                link(nc.vector.tensor_scalar(h_tok[:, t, :], src, mv[:, 0:1], lnv[:, 1:2], ALU.subtract, ALU.mult))
                dve.wait_ge(rows_in, rows_need)
                link(nc.vector.tensor_tensor(h_tok[:, t, :], h_tok[:, t, :], rows[:, 0, :], ALU.mult))
                nc.vector.tensor_tensor(h_tok[:, t, :], h_tok[:, t, :], rows[:, 1, :], ALU.add).then_inc(ln_done, 1)

            for op, arg in steps:
                if op == "group":
                    gr = groups[arg]
                    g, kind = arg, gr["kind"]
                    ps, read = bank_of(g)
                    dst = gr.get("dst") or ("", 0)
                    if kind == "swap":
                        r = raw[:, gr["ring"], :]
                        dve.wait_ge(group_full, g + 1)
                        wait_group(gr["raw"])
                        if gr["tg_gate"]:
                            passed_token(dve, wait_group, gr["tg_gate"])
                        if gr["nth"] > 1:
                            dve.wait_ge(rot_done, gr["nth"] - 1)
                        if gr["table"]:
                            dve.wait_ge(table_a, 2)
                        nc.vector.tensor_tensor(tg[:, 0, :], ps[:, :], cn("sin1"), ALU.mult).then_inc(read, 1)
                        link(nc.vector.tensor_tensor(r, r, cn("cos1"), ALU.mult))
                        o = {"qk": lambda d: qk[:, d, :], "kpe": lambda d: kpe, "qp": lambda d: qp[:, d, :]}[dst[0]](dst[1])
                        nc.vector.tensor_tensor(o, tg[:, 0, :], r, ALU.add).then_inc(rot_done, 1)
                    elif kind == "F" and dst[0] == "cumlog":
                        n_cum += 1
                        dve.wait_ge(group_full, g + 1)
                        b = bfc[0:4, gr["layer"]:gr["layer"] + 1]
                        dve.wait_ge(cum_ln, n_cum)
                        nc.vector.tensor_scalar(cum_min, ps[0:4, :], b, 0.0, ALU.add, ALU.min).then_inc(read, 1)
                        dve.wait_ge(read, use(g))
                        link(nc.vector.tensor_tensor(cum_min, cum_min, cum_l, ALU.subtract))
                        nc.vector.tensor_tensor_scan(cum, cum_min, cum_min, 0.0, ALU.add, ALU.min).then_inc(cum_done, 1)
                    elif kind == "gate":
                        n_gate += 1
                        n_min += 1
                        dve.wait_ge(gate_ln, n_gate)
                        nc.vector.scalar_tensor_tensor(tg[:, 0, :], ps[:, :], 0.0, tg[:, 0, :], ALU.min, ALU.subtract)\
                            .then_inc(gate_min, 1)
                    elif kind == "sigmoid":
                        n_gate += 1
                        n_sig += 1
                        e = tg[:, gr["ring"], :]
                        dve.wait_ge(gate_ln, n_gate)
                        nc.vector.scalar_tensor_tensor(e, ps[:, :], 0.0, e, ALU.min, ALU.subtract).then_inc(read, 1)
                    elif kind == "up":
                        e = tg[:, gr["ring"], :]
                        dve.wait_ge(group_full, g + 1)
                        dve.wait_ge(gate_sig, n_sig)
                        nc.vector.tensor_tensor(e, ps[:, :], e, ALU.mult).then_inc(read, 1)
                        dve.wait_ge(read, use(g))
                        o = mix[:, gr["chunk"], :]
                        if gr["branch"] == 0:
                            nc.vector.tensor_copy(o, e).then_inc(mix_done, 1)
                        else:
                            dve.wait_ge(mix_done, 8 * gr["branch"])
                            nc.vector.tensor_tensor(o, o, e, ALU.add).then_inc(mix_done, 1)
                    elif kind == "ffgate":
                        n_gate += 1
                        n_min += 1
                        n_sig += 1
                        e = tg[:, gr["ring"], :]
                        dve.wait_ge(gate_ln, n_gate)
                        nc.vector.scalar_tensor_tensor(e, ps[:, :], 0.0, e, ALU.min, ALU.subtract).then_inc(gate_min, 1)
                        dve.wait_ge(gate_sig, n_sig)
                        nc.vector.tensor_tensor(e, ps[:, :], e, ALU.mult).then_inc(read, 1)
                    elif kind == "ffup":
                        dve.wait_ge(group_full, g + 1)
                        wait_group(gr["gate"])
                        nc.vector.tensor_tensor(acts[gr["chunk"]], ps[:, :], tg[:, gr["ring"], :], ALU.mult).then_inc(read, 1)
                    elif kind == "T" and dst[0] == "resid":
                        dve.wait_ge(group_full, g + 1)
                        half = dst[1]
                        nc.vector.scalar_tensor_tensor(z[:, 512 * half:512 * half + 512],
                                                       h_tok[:, gr["tile"], 512 * half:512 * half + 512], ALPHA,
                                                       ps[:, :], ALU.mult, ALU.add).then_inc(read, 1)
                        dve.wait_ge(read, use(g))
                    elif kind == "T" and dst[0] == "resid2":
                        dve.wait_ge(group_full, g + 1)
                        dve.wait_ge(x_back, 16 * NT)
                        x = h_tok[:, gr["tile"], 512 * dst[1]:512 * dst[1] + 512]
                        nc.vector.tensor_tensor(x, x, ps[:, :], ALU.add).then_inc(read, 1)
                    elif kind == "hg_state":
                        pass
                elif op == "gate2":
                    gr = groups[arg]
                    ps, read = bank_of(arg)
                    n_sig += 1
                    dve.wait_ge(gate_sig, n_sig)
                    o = y[:, gr["chunk"], :] if gr["first"] else tg[:, 0, :]
                    nc.vector.tensor_tensor(o, ps[:, :], tg[:, 0, :], ALU.mult).then_inc(read, 1)
                elif op == "gate3":
                    gr = groups[arg]
                    if not gr["first"]:
                        dve.wait_ge(bank_of(arg)[1], use(arg))
                        c = gr["chunk"]
                        if gr["unit"] is not None:
                            unit_done(dve, gr["unit"])
                        else:
                            dve.wait_ge(hg_normed, c - 3)
                        nc.vector.tensor_tensor(y[:, c, :], y[:, c, :], tg[:, 0, :], ALU.mult).then_inc(gated, 1)
                elif op == "fin" and units[arg]["kind"] == "C":
                    u = units[arg]
                    dve.wait_ge(pv_done, turned_at[u["last"]])
                    wait_group(u["gate"])
                    nc.vector.tensor_tensor(y[:, u["chunk"], :], O[arg % 2][:, :], y[:, u["chunk"], :], ALU.mult)\
                        .then_inc(o_free["C"], 1)
                elif op == "bias":
                    t, b = arg
                    K = P * (t + 1)
                    k = NT_BIAS(t, b)
                    mk = below[k % 2][:, 0:K]
                    if k >= 1:
                        dve.wait_ge(bias_done, 4 * k)
                    link(nc.vector.tensor_scalar(starts[:, 0:1], pq[:, t:t + 1], float(-BUCKET_STARTS[b]), None, ALU.add))
                    nc.vector.tensor_scalar(mk, pkb[:, 0:K], starts[:, 0:1], None, ALU.is_le).then_inc(bias_mask, 1)
                    dve.wait_ge(bias_mask, k + 1)
                    for h in range(4):
                        o, d = b_at(h, t), deltas[:, b, h:h + 1]
                        if b == REL_BUCKETS - 1:
                            ins = nc.vector.tensor_scalar(o, mk, d, deltas[:, 0, h:h + 1], ALU.mult, ALU.add)
                        else:
                            ins = nc.vector.scalar_tensor_tensor(o, mk, d, o, ALU.mult, ALU.add)
                        ins.then_inc(bias_done, 1)
                elif op == "soft1":
                    n, it = arg, items[arg]
                    K, kind = it["K"], it["kind"]
                    if kind in "CI":
                        continue
                    dve.wait_ge(scores_full, n + 1)
                    if n >= 2:
                        dve.wait_ge(exp_done, n - 1)
                        if items[n - 2]["kind"] == "C":
                            dve.wait_ge(stick_done, stick_at[n - 2])
                    c = 2 * (n % 2)
                    s_ = sc[first_map[n] % SCORE_BANKS][:, 0:K]
                    l = L[:, n % 2, 0:K]
                    if kind == "A":
                        for j in range(2):
                            ins = nc.vector.tensor_reduce(nmax[:, c + j:c + j + 1],
                                                          sc[(first_map[n] + j) % SCORE_BANKS][:, 0:K],
                                                          AX, ALU.max, negate=True)
                        ins.then_inc(soft1_done, 1)
                        continue
                    if kind == "M":
                        link(nc.vector.tensor_reduce(nmax[:, c:c + 1], s_, AX, ALU.max, negate=True))
                        nc.vector.tensor_scalar(nmax[:, c:c + 1], nmax[:, c:c + 1], MLA_SCALE, None, ALU.mult)\
                            .then_inc(soft1_done, 1)
                        continue
                    h = it["head"]
                    if kind == "B":
                        for gg in it["cums"]:
                            wait_group(gg)
                        link(nc.vector.scalar_tensor_tensor(l, s_, cqc[:, it["tile"], h:h + 1], ckb[:, h, 0:K],
                                                            ALU.add, ALU.subtract))
                    else:
                        link(nc.vector.scalar_tensor_tensor(l, s_, SPARSE_SCALE, b_at(h, it["tile"]), ALU.mult, ALU.add))
                    nc.vector.tensor_reduce(nmax[:, c:c + 1], l, AX, ALU.max, negate=True).then_inc(soft1_done, 1)
                elif op == "soft2":
                    n, it = arg, items[arg]
                    K, e, l, kind = it["K"], E[:, n % 2, :, 0:it["K"]], L[:, n % 2, 0:it["K"]], it["kind"]
                    c = 2 * (n % 2)
                    dve.wait_ge(exp_done, n + 1)
                    i = turned_at[n] - 1
                    pr = PR[:, i % 3, 0:K]
                    if kind in "ABMX":
                        if i >= 3:
                            dve.wait_ge(turned, i - 2)
                        link(nc.vector.reciprocal(rsum[:, c:c + it["maps"]], sums[:, c:c + it["maps"]]))
                    if kind == "A":
                        link(nc.vector.tensor_scalar(c2[:, 0:1], rsum[:, c + 1:c + 2], lam, None, ALU.mult))
                        link(nc.vector.tensor_scalar(e[:, 1, :], e[:, 1, :], c2[:, 0:1], None, ALU.mult))
                        nc.vector.scalar_tensor_tensor(pr, e[:, 0, :], rsum[:, c:c + 1], e[:, 1, :],
                                                       ALU.mult, ALU.subtract).then_inc(soft2_done, 1)
                    elif kind in "BMX":
                        nc.vector.tensor_scalar(pr, e[:, 0, :], rsum[:, c:c + 1], None, ALU.mult).then_inc(soft2_done, 1)
                    elif kind == "I":
                        w_ = iw[:, it["tile"], it["head"]:it["head"] + 1]
                        acc = z[:, 0:K]
                        dve.wait_ge(soft2_done, n)
                        if it["head"] == 0:
                            nc.vector.tensor_scalar(acc, e[:, 0, :], w_, None, ALU.mult).then_inc(soft2_done, 1)
                        else:
                            nc.vector.scalar_tensor_tensor(acc, e[:, 0, :], w_, acc, ALU.mult, ALU.add)\
                                .then_inc(soft2_done, 1)
                    else:
                        s_ = sc[first_map[n] % SCORE_BANKS][:, 0:K]
                        link(nc.vector.scalar_tensor_tensor(e[:, 1, :], s_, 0.0, e[:, 0, :], ALU.max, ALU.add))
                        back = E[:, n % 2, 1, K - 1::-1]
                        link(nc.vector.tensor_tensor_scan(E[:, n % 2, 0, K - 1::-1], back, back, 0.0, ALU.add, ALU.max))
                        if n >= 2 and items[n - 2]["kind"] == "C":
                            dve.wait_ge(stick_done, stick_at[n - 2])
                        nc.vector.tensor_tensor(l, s_, e[:, 0, :], ALU.subtract).then_inc(soft2_done, 1)
                elif op == "topk":
                    t = arg
                    K = P * (t + 1)
                    buf = [z[:, 0:K], z[:, S:S + K]]
                    dve.wait_ge(soft2_done, max(n for n, it in enumerate(items) if it["kind"] == "I" and it["tile"] == t) + 1)
                    if t == 1:
                        dve.wait_ge(bias_done, N_BIAS)
                        for h in range(4):
                            link(nc.vector.tensor_tensor(b_at(h, 0), b_at(h, 0), negb[:, 0, :], ALU.add))
                    link(nc.vector.tensor_tensor(buf[0][:, K - P:K], buf[0][:, K - P:K], negb[:, 0, :], ALU.add))
                    for r in range(TOPK // 8):
                        link(nc.vector.max(m8, buf[r % 2]))
                        link(nc.vector.match_replace(buf[(r + 1) % 2], m8, buf[r % 2], STRUCK))
                    link(nc.vector.tensor_scalar(buf[1], buf[0], STRUCK / 2, NEG, ALU.is_gt, ALU.mult))
                    link(nc.vector.tensor_tensor(buf[1][:, K - P:K], buf[1][:, K - P:K], negb[:, 0, :], ALU.add))
                    for h in range(4):
                        link(nc.vector.tensor_tensor(b_at(h, t), b_at(h, t), buf[1], ALU.add))
                elif op == "fin2":
                    u = units[arg]
                    wait_group(u["meansq"])
                    nc.vector.scalar_tensor_tensor(y[:, u["chunk"], :], O[arg % 2][:, :], gcol, tg[:, 1, :],
                                                   ALU.mult, ALU.mult).then_inc(o_free["A"], 1)
                elif op == "layer":
                    l = arg
                    lam_init = 0.8 - 0.6 * math.exp(-0.3 * l)
                    dve.wait_ge(lam_loaded, 64 * (l + 1))
                    for i in range(2):
                        nc.vector.tensor_tensor_reduce(lam_in[:, 2 * i, :], lam_in[:, 2 * i, :], lam_in[:, 2 * i + 1, :],
                                                       1.0, 0.0, ALU.mult, ALU.add, lam_s[:, i:i + 1]).then_inc(lam_dot, 1)
                    dve.wait_ge(lam_exp, l + 1)
                    link(nc.vector.tensor_tensor(lam_s[:, 4:5], lam_s[:, 2:3], lam_s[:, 3:4], ALU.subtract))
                    nc.vector.tensor_scalar(lam, lam_s[:, 4:5], lam_init, None, ALU.add).then_inc(lam_done, 1)
                    nc.vector.tensor_scalar(gcol, gin[:, l:l + 1], 1.0 - lam_init, None, ALU.mult).then_inc(lam_done, 1)
                    dve.wait_ge(lam_done, 2 * (l + 1))
                elif op == "prep":
                    dve.wait_ge(consts_in, N_CONSTS_IN)
                    dve.wait_ge(staged_in, 32)
                    nc.vector.tensor_copy(identb[:, :], cn("ident")).then_inc(prep, 1)
                    nc.vector.tensor_copy(negb[:, :, :].rearrange("p a n -> p (a n)"), z[:, 0:2 * P]).then_inc(prep, 1)
                    nc.vector.tensor_copy(keep[:, :], z[:, 2 * P:2 * P + S]).then_inc(prep, 1)
                    nc.vector.tensor_copy(masks8[:, :], raw[:, :, :].rearrange("p a n -> p (a n)")[:, 0:(LEVELS + 1) * P])\
                        .then_inc(prep, 1)
                    dve.wait_ge(prep, N_PREP)
                    if not only_block1:
                        dve.wait_ge(pos_in, 16 * (NT + 2))
                        link(nc.vector.tensor_copy(pq, pos_i[:, :]))
                        link(nc.vector.tensor_copy(pkb, below[0].bitcast(I32)))
                        link(nc.vector.tensor_copy(below[1][:, 0:4 * REL_BUCKETS], deltas[:, :, :].rearrange("p b h -> p (b h)")))
                        link(nc.vector.tensor_tensor(
                            deltas[:, 1:REL_BUCKETS, :].rearrange("p b h -> p (b h)"),
                            deltas[:, 1:REL_BUCKETS, :].rearrange("p b h -> p (b h)"),
                            below[1][:, 0:4 * (REL_BUCKETS - 1)], ALU.subtract))
                elif op == "ln_in":
                    n_ln_ += 1
                    dve.wait_ge(x_in[arg], 16)
                    layernorm(h_tok[:, arg, :], arg, n_ln_, 32)
                elif op == "ln":
                    n_ln_ += 1
                    layernorm(z[:, :], arg[1], n_ln_, 32 * (arg[0] + 2))
                elif op == "bounds":
                    link(nc.vector.tensor_tensor(lbs, lbx, lbx, ALU.subtract))
                    nc.vector.tensor_copy(lbs, lbs).then_inc(lb_d, 1)
                    dve.wait_ge(lb_a, 1)
                    link(nc.vector.reciprocal(oml, lbs))
                    link(nc.vector.tensor_tensor(lbs, lbs, oml, ALU.mult))
                    link(nc.vector.tensor_tensor(lbx, lbs, lbs, ALU.subtract))
                    link(nc.vector.tensor_scalar(oml, lbx, -1.0, 1.0, ALU.mult, ALU.add))
                    nc.vector.tensor_scalar(lbs, lbx, LB_FLOOR, None, ALU.max).then_inc(lb_d, 1)
                    dve.wait_ge(lb_a, 2)
                    link(nc.vector.tensor_scalar(log_lb, log_lb, -math.log(LOG_SCALE), None, ALU.add))
                    link(nc.vector.tensor_tensor(l1a, l1p, log_lb, ALU.subtract))
                elif op == "angles":
                    sin_, cos_, ang = cn("sin1"), cn("cos1"), tg[:, 1, :]
                    dve.wait_ge(rot_done, NT * 2 * DEPTH)
                    link(nc.vector.tensor_scalar(ang, pkb, cn("inv_freq"), None, ALU.mult))
                    for o, shift in ((sin_, 0.0), (cos_, 0.25)):
                        turn = tg[:, 0, :]
                        link(nc.vector.tensor_scalar(turn, ang, 1.0 / (2 * math.pi), shift, ALU.mult, ALU.add))
                        link(nc.vector.tensor_scalar(turn, turn, MAGIC, None, ALU.add))
                        link(nc.vector.tensor_scalar(turn, turn, MAGIC, None, ALU.subtract))
                        link(nc.vector.scalar_tensor_tensor(o, turn, -TWO_PI[0], ang, ALU.mult, ALU.add))
                        link(nc.vector.scalar_tensor_tensor(o, turn, -TWO_PI[1], o, ALU.mult, ALU.add))
                        link(nc.vector.scalar_tensor_tensor(o, turn, -TWO_PI[2], o, ALU.mult, ALU.add))
                        lo = -PI_F - (math.pi / 2 if shift else 0.0)
                        nc.vector.tensor_scalar(o, o, lo, lo + 2 * PI_F, ALU.max, ALU.min).then_inc(table_d, 1)
                        dve.wait_ge(table_d, 1 + (shift > 0))
                elif op == "norm":
                    t, k = arg["tile"], arg["nth"]
                    dve.wait_ge(norm_r, k + 1)
                    dve.wait_ge(rows_in, 32 * (DEPTH + 1) + (16 if k < NT else 48))
                    link(nc.vector.tensor_scalar(nz[k % 2], h_tok[:, t, :], ss[:, k % 2:k % 2 + 1], None, ALU.mult))
                    nc.vector.tensor_tensor(nz[k % 2], nz[k % 2], rows[:, 0, :], ALU.mult).then_inc(norm_done, 1)
                elif op == "latent":
                    wait_group(arg_group[arg])
                    x, gg, n = (cqT, mq_g, 3) if arg == "cq" else (ckvT, mkv_g, 2)
                    for k in range(n):
                        ins = nc.vector.scalar_tensor_tensor(x[:, k, :], x[:, k, :], gg[:, k:k + 1], tg[:, 1, :],
                                                             ALU.mult, ALU.mult)
                    ins.then_inc(lat_done, 1)
                elif op == "hg_gates":
                    h = arg
                    if h == 0:
                        for b_ in (hQD, hATT, z[:, :]):
                            nc.vector.memset(b_, 0.0).then_inc(hg_ready0, 1)
                        dve.wait_ge(hg_ready0, 3)
                    wait_group(hf_group[h])
                    wait_group(hq_group[h])
                    dve.wait_ge(hg_act, 3 * h + 1)
                    link(nc.vector.scalar_tensor_tensor(hK, hF, 0.0, hA, ALU.min, ALU.subtract))
                    nc.vector.tensor_tensor(hB, hK, hF, ALU.subtract).then_inc(hg_dve, 1)
                    dve.wait_ge(hg_act, 3 * h + 2)
                    nc.vector.tensor_scalar(hA, hK, l1a[:, h:h + 1], None, ALU.add).then_inc(hg_dve, 1)
                    dve.wait_ge(hg_act, 3 * h + 3)
                    link(nc.vector.tensor_scalar(hK, hK, l1p[:, h:h + 1], log_lb[:, h:h + 1], ALU.add, ALU.max))
                    link(nc.vector.tensor_tensor(hKE, hKE, hK, ALU.add))
                    link(nc.vector.tensor_tensor_scan(hB, keep[:, :], hKE, 0.0, ALU.mult, ALU.add))
                    nc.vector.tensor_scalar(hK, hG, oml[:, h:h + 1], None, ALU.mult).then_inc(hg_dve, 1)
                    dve.wait_ge(hg_dve, 3 * (h + 1))
                elif op == "hg_diff":
                    h, lv = arg
                    if lv < LEVELS:
                        hb = 1 << lv
                        gu, gl = (hG[:, 256 * i:256 * i + 256].rearrange("p (n b) -> p n b", b=hb) for i in range(2))
                        ref = halves(hB, 0, hb)[:, :, hb - 1:hb].to_broadcast([P, S // (2 * hb), hb])
                        nc.vector.tensor_tensor(gu, halves(hB, 1, hb), ref, ALU.subtract)
                        nc.vector.tensor_tensor(gl, halves(hB, 0, hb), ref, ALU.subtract).then_inc(hg_diff, 1)
                    else:
                        b8 = hB.rearrange("p (n c) -> p n c", c=CHUNK)
                        last = b8[:, :, CHUNK - 1:CHUNK].to_broadcast([P, NCH, CHUNK])
                        nc.vector.tensor_tensor(hG.rearrange("p (n c) -> p n c", c=CHUNK), last, b8, ALU.subtract)\
                            .then_inc(hg_diff, 1)
                elif op == "hg_level":
                    h, lv = arg
                    hb = 1 << lv
                    gu, gl = (hG[:, 256 * i:256 * i + 256].rearrange("p (n b) -> p n b", b=hb) for i in range(2))
                    if lv >= 2:
                        dve.wait_ge(group_full, level_group[(h, lv - 2)] + 1)
                    dve.wait_ge(hg_exp, (LEVELS + 1) * h + lv + 1)
                    nc.vector.tensor_tensor(halves(hQT[lv % 2], 1, hb), halves(hQ, 1, hb), gu, ALU.mult)
                    nc.vector.tensor_tensor(halves(hKT[lv % 2], 0, hb), halves(hK, 0, hb), gl, ALU.mult)\
                        .then_inc(hg_ready, 1)
                    dve.wait_ge(hg_ready, LEVELS * h + lv + 1)
                elif op == "hg_put":
                    gr = groups[arg]
                    ps, read = bank_of(arg)
                    dve.wait_ge(group_full, arg + 1)
                    mk = masks8[:, (gr["level"] + 1) * P:(gr["level"] + 2) * P]
                    if arg_prev_put.get(arg) is not None:
                        wait_group(arg_prev_put[arg])
                    nc.vector.copy_predicated(hATT.rearrange("p (i t) -> p i t", i=NT),
                                              mk[:, None, :].to_broadcast([P, NT, P]),
                                              ps[:, :].rearrange("p (i t) -> p i t", i=NT)).then_inc(read, 1)
                elif op == "hg_decay":
                    h = arg
                    dve.wait_ge(hg_exp, (LEVELS + 1) * (h + 1))
                    dve.wait_ge(hg_de, h + 1)
                    nc.vector.tensor_tensor(hQD, hQD, hQ, ALU.mult)
                    nc.vector.tensor_tensor(hA, hK, hG, ALU.mult).then_inc(hg_kd, 1)
                elif op == "hg_chain":
                    h, gs = arg
                    for g in gs:
                        dve.wait_ge(group_full, g + 1)
                    for n in range(NCH - 1):
                        ps, read = bank_of(gs[n % 2])
                        new, p_ = states[:, n + 1, :], ps[:, (n // 2) * P:(n // 2 + 1) * P]
                        if n == 0:
                            ins = nc.vector.tensor_copy(new, p_)
                        else:
                            ins = nc.vector.scalar_tensor_tensor(new, states[:, n, :], dec[:, n:n + 1], p_,
                                                                 ALU.mult, ALU.add)
                        if n >= NCH - 3:
                            ins.then_inc(read, 1)
                            dve.wait_ge(read, use(gs[n % 2]))
                        else:
                            link(ins)
                elif op == "hg_norm":
                    h = arg
                    wait_group(head_meansq[h])
                    nc.vector.scalar_tensor_tensor(y[:, 4 + h, :], y[:, 4 + h, :], out_g, tg[:, 1, :],
                                                   ALU.mult, ALU.mult).then_inc(hg_normed, 1)
                elif op == "final":
                    t = arg
                    dve.wait_ge(down_full, N_DOWN + t)
                    for half in range(2):
                        x = h_tok[:, t, 512 * half:512 * half + 512]
                        ins = nc.vector.tensor_tensor(x, x, down[2 * t + half][:, :], ALU.add)
                    ins.then_inc(fin_sum, 1)
                    dve.wait_ge(norm_r, 2 * NT + t + 1)
                    link(nc.vector.tensor_scalar(final[t], h_tok[:, t, :], ss[:, t % 2:t % 2 + 1], None, ALU.mult))
                    nc.vector.tensor_tensor(final[t], final[t], rows[:, 1, :], ALU.mult).then_inc(fin_done, 1)


def kernel(**inputs):
    import concourse.bacc as bacc
    from concourse.bass_utils import run_bass_kernel_spmd

    nc = bacc.Bacc("TRN2", target_bir_lowering=False, num_devices=1)
    arrays, aps = {}, {}
    given = dict(inputs, constants=constants())
    for name, v in given.items():
        v = np.ascontiguousarray(v)
        arrays[f"in_{name}"] = v
        aps[name] = nc.dram_tensor(f"in_{name}", v.shape, mybir.dt.from_np(v.dtype), kind="ExternalInput").ap()
    out = nc.dram_tensor("out_0", (1, S, D), F32, kind="ExternalOutput").ap()
    two_blocks(nc, aps, out)
    return run_bass_kernel_spmd(nc, [arrays], core_ids=[0]).results[0]["out_0"]
```

```python
import math
from contextlib import ExitStack

import numpy as np
import concourse.bass as bass
from concourse import mybir

F32 = mybir.dt.float32
F32R = mybir.dt.float32r
BF16 = mybir.dt.bfloat16
I32 = mybir.dt.int32
U8 = mybir.dt.uint8
ACT = mybir.ActivationFunctionType
ALU = mybir.AluOpType
AX = mybir.AxisListType.X

P = 128
S = 512
NT = S // P
D = 1024
KD = D // P
DEPTH = 2
HD = 64
NEG = -1e30
ALPHA = (2 * DEPTH) ** 0.25
W_SLOTS = 3
PROJ_BANKS = 2
SCORE_BANKS = 3
FREQS = 32
LEVELS = 6
CHUNK = 64
DRAIN = 4
EXP_AND_LN = "natural_log_exp_and_others"
NCH = S // CHUNK
REL_BUCKETS = 32
REL_MAX_DIST = 128
TOPK = 128
IDX_HEADS = 8
D_FF = 2816
KF = D_FF // P

AQ, AK, AV, AG, BQ, BK, BV, BFG, BG, CQ, CK, CV, CG = (
    0, 512, 1024, 1536, 2048, 2304, 2560, 2816, 2820, 3076, 3332, 3588, 3844)
(XQ, XK, XV, IQ, IK, IW, HQ, HF, HI, HG, MQ, MKV, MPE, GATE) = (
    0, 512, 640, 768, 1280, 1344, 1352, 1864, 2376, 2888, 3400, 3784, 4040, 4104)


def bucket_starts():
    exact = REL_BUCKETS // 2
    d = np.arange(4 * REL_MAX_DIST)
    large = exact + (np.log(np.maximum(d, exact).astype(np.float32) / exact) / math.log(REL_MAX_DIST / exact)
                     * (REL_BUCKETS - exact)).astype(np.int32)
    b = np.where(d < exact, d, np.minimum(large, REL_BUCKETS - 1))
    return [int(np.argmax(b >= k)) for k in range(REL_BUCKETS)]


CONST_COLS = {}


def constants():
    p = np.arange(P)
    q = np.arange(S)
    out = {}
    out["ident"] = np.eye(P)
    out["ones"] = np.ones((P, P))
    half, inv1 = 8, (500000.0 ** (-np.arange(0, 16, 2, dtype=np.float32) / 16)).astype(np.float32)
    r = p % HD
    partner = np.where(r < half, p + half, np.where(r < 2 * half, p - half, p))
    out["swap1"] = (p[:, None] == partner[None, :]).astype(np.float32)
    ang = (q.astype(np.float32)[None, :] * inv1[r % half][:, None]).astype(np.float32)
    rot = (r < 2 * half)[:, None]
    out["cos1"] = np.where(rot, np.cos(ang), 1.0)
    out["sin1"] = np.where(rot, np.where((r < half)[:, None], -1.0, 1.0) * np.sin(ang), 0.0)
    partner2 = np.where(r < FREQS, p + FREQS, p - FREQS)
    out["swap2"] = (p[:, None] == partner2[None, :]).astype(np.float32)
    inv2 = (10000.0 ** (-np.arange(0, HD, 2, dtype=np.float32) / HD)).astype(np.float32)
    out["inv_freq"] = inv2[r % FREQS][:, None]
    out["sin_sign"] = np.where(r < FREQS, -1.0, 1.0)[:, None]
    out["neg_causal"] = np.where(p[None, :] <= p[:, None], 0.0, NEG)
    out["neg_strict"] = np.where(p[None, :] < p[:, None], 0.0, NEG)
    out["chunk_keep"] = np.broadcast_to((q % CHUNK != 0).astype(np.float32), (P, S))
    s_, t_ = p[:, None], p[None, :]
    same = (s_ // CHUNK) == (t_ // CHUNK)
    masks = [s_ == t_]
    for lv in range(LEVELS):
        h = 1 << lv
        masks.append(same & (s_ // (2 * h) == t_ // (2 * h)) & (s_ % (2 * h) < h) & (t_ % (2 * h) >= h))
    out["level_masks"] = np.concatenate([m.astype(np.float32) for m in masks], 1)
    col, parts = 0, []
    for name, a in out.items():
        a = np.ascontiguousarray(a, np.float32)
        CONST_COLS[name] = (col, a.shape[1])
        col += a.shape[1]
        parts.append(a)
    return np.ascontiguousarray(np.concatenate(parts, 1))


N_CONST = constants().shape[1]
CONST_AT = CONST_COLS
STAGED_Z = 2 * P + S
CONST_USED = N_CONST - STAGED_Z - (LEVELS + 1) * P
OFF = [P * t * (t + 1) // 2 for t in range(NT + 1)]
BUCKET_STARTS = bucket_starts()
N_BIAS = 4 * NT * (REL_BUCKETS - 1)
N_PREP = 4
BIAS_RATES = {"A": 2.1, "B": 1.0, "C": 0.75}
RATES = {"A": 1.1, "B": 2.0, "C": 2.2, "I": 2.0, "M": 0.75, "X": 0.75}
N_DOWN = KF // 2
EARLY = 8
IDX_SCALE = HD ** -0.5 * IDX_HEADS ** -0.5
SPARSE_SCALE = P ** -0.5
MLA_SCALE = 192 ** -0.5
LB_FLOOR = 1e-30
LOG_SCALE = 2.0 ** 50
STRUCK = -3e38
MAGIC = 1.5 * 2.0 ** 23
PI_F = 3.1415925


def split_two_pi():
    rest, parts = 2 * math.pi, []
    for bits in (8, 11):
        unit = 2.0 ** (math.floor(math.log2(rest)) - bits + 1)
        parts.append(math.floor(rest / unit) * unit)
        rest -= parts[-1]
    return parts + [rest]


TWO_PI = split_two_pi()


def NT_BIAS(t, b):
    return t * (REL_BUCKETS - 1) + REL_BUCKETS - 1 - b


class Count:

    def __init__(self, sem):
        self.sem, self.n = sem, 0

    def on(self, ins, k=1):
        ins.then_inc(self.sem, k)
        self.n += k
        return self.n


def plan(only_block1=False):
    steps, groups, slabs, items, units = [], [], [], [], []

    def slab(name, **kw):
        slabs.append(dict(name=name, last=None, **kw))
        slot_for(len(slabs) - 1)
        return len(slabs) - 1

    def group(kind, slab=None, **kw):
        g = len(groups)
        groups.append(dict(kind=kind, slab=slab, g=g, **kw))
        if slab is not None:
            slabs[slab]["last"] = g
            if state["mid"] and kw.get("K") == KD:
                steps.append(("half", g))
                groups[g]["split"] = True
                state["mid"]()
        if not kw.get("late"):
            steps.append(("group", g))
        return g

    def slot_for(i):
        s_ = slabs[i]
        slot = state["slots"][state["turn"] % len(state["slots"])]
        state["turn"] += 1
        s_["slot"] = slot
        s_["halves"] = (2 * slot, 2 * slot + 1) if slot < W_SLOTS else (slot - W_SLOTS,)
        before = [[j for j in range(i) if h in slabs[j]["halves"]] for h in s_["halves"]]
        s_["prev"] = sorted({b[-1] for b in before if b})

    stages = [("scores", 0), ("soft1", 0), ("soft2", 1), ("soft3", 2), ("trans", 3), ("pv", 4)]
    state = dict(lo=0, n=0, fin=0, slots=list(range(W_SLOTS)), turn=0, bias=0, bias_due=0.0, squared=None, mid=None)
    bias_steps = [(t, b) for t in range(NT) for b in range(REL_BUCKETS - 1, 0, -1)]

    def tick():
        n = state["n"]
        for name, lag in stages:
            if state["lo"] <= n - lag < len(items):
                it = items[n - lag]
                if (it["kind"] == "I" and lag >= 2) or (name == "soft3" and it["kind"] != "C"):
                    continue
                steps.append((name, n - lag))
                if name == "soft2" and it["kind"] == "I" and it["head"] == IDX_HEADS - 1:
                    steps.append(("topk", it["tile"]))
        state["bias_due"] += BIAS_RATES.get(items[min(n, len(items) - 1)]["kind"], 2)
        while state["bias_due"] >= 1:
            state["bias_due"] -= 1
            if state["bias"] < len(bias_steps) and not only_block1:
                steps.append(("bias", bias_steps[state["bias"]]))
                state["bias"] += 1
        if state["squared"] is not None:
            group("meansq", unit=state["squared"])
            steps.append(("fin2", state["squared"]))
            state["squared"] = None
        while state["fin"] < len(units) and units[state["fin"]]["last"] <= n - DRAIN:
            u = state["fin"]
            steps.append(("fin", u))
            if units[u]["kind"] == "A":
                state["squared"] = u
            state["fin"] += 1
        state["n"] += 1

    def flush():
        while state["fin"] < len(units) or state["n"] < len(items) + DRAIN or state["squared"] is not None:
            tick()
        state["lo"] = state["n"] = len(items)

    def add_items(its):
        for it in its:
            it["n"] = len(items)
            items.append(it)
            if it.get("unit") is not None:
                units[it["unit"]]["last"] = it["n"]

    def weave(jobs, new_items):
        base = len(items)
        add_items(new_items)
        due = dict(done=0, credit=0.0, gain=0.0)

        def ticks(most):
            due["credit"] = min(due["credit"] + due["gain"], 3.0)
            while due["credit"] >= 1 and most and state["n"] < len(items) + DRAIN \
                    and (state["n"] >= len(items) or items[state["n"]]["after"] <= due["done"]):
                tick()
                due["credit"] -= 1
                most -= 1

        def between():
            if items[min(state["n"], len(items) - 1)]["kind"] in "BC" and state["squared"] is None:
                ticks(1)

        for fn, weight, needs in jobs:
            while state["n"] < base + needs:
                tick()
            due["gain"] = weight * RATES[items[min(state["n"], len(items) - 1)]["kind"]] / 2
            state["mid"] = between if items[min(state["n"], len(items) - 1)]["kind"] in "BC" else None
            if state["mid"] is None:
                due["credit"] += due["gain"]
            fn()
            state["mid"] = None
            due["done"] += 1
            ticks(3)

    for t in range(NT + 1):
        if t < NT:
            steps.append(("ln_in", t))
        if t:
            for half in range(2):
                group("to_hT", tile=t - 1, half=half)
    for l in range(DEPTH):
        sv = slab("av", layer=l)
        sq = slab("aq", layer=l)
        sk = slab("ak", layer=l)
        for t in range(NT):
            group("T", sv, c0=0, N=512, K=KD, tile=t, dst=("V", 0), layer=l)
        if l == 0:
            steps.append(("prep", 0))
        steps.append(("layer", l))

        raws = {}

        def rope_raw(h, i, l=l, s2=(sq, sk), raws=raws):
            raws[i] = group("F", s2[i], c0=128 * h, M=P, K=KD, dst=("raw", i), scale=HD ** -0.5 if i == 0 else 1.0,
                            layer=l)

        def rope_turn(h, i, raws=raws):
            group("swap", raw=raws[i], dst=("qk", 2 * h + i), ring=i, table=0)

        def rope_two(h):
            rope_raw(h, 1)
            rope_turn(h, 0)

        rope_raw(0, 0)
        rope_two(0)
        rope_turn(0, 1)
        jobs = []
        for h in range(1, 4):
            jobs += [(lambda h=h: rope_raw(h, 0), 1, 0), (lambda h=h: rope_two(h), 1.1, 0),
                     (lambda h=h: rope_turn(h, 1), 0.1, 0)]

        hold = {}

        def vv(t, l=l):
            if t == 0:
                hold["bv"] = slab("bvcv", layer=l)
            group("T", hold["bv"], c0=0, N=512, K=KD, tile=t, dst=("V", 512), layer=l)

        for t in range(NT):
            jobs.append((lambda t=t: vv(t), 1, 0))
            if t == 2:
                jobs.append((lambda: cum_log(), 1, 0))

        def cum_log(l=l):
            group("F", hold["bv"], c0=512, M=4, K=KD, dst=("cumlog", 0), layer=l)

        def cum_groups(l=l):
            for h in range(4):
                group("spread_cum", head=h)
            group("turn_cum")

        jobs.append((cum_groups, 0.5, 0))

        def bqk(c, i, l=l):
            if c == 0 and i == 0:
                hold["bqk"] = slab("bqk", layer=l)
            group("F", hold["bqk"], c0=256 * i + 128 * c, M=P, K=KD, dst=("qk", 2 * c + i),
                  scale=HD ** -0.5 if i == 0 else 1.0, layer=l)

        for c in range(2):
            for i in range(2):
                jobs.append((lambda c=c, i=i: bqk(c, i), 1, 4 * (c + 1)))

        def cqk(c, i, l=l):
            if c == 0 and i == 0:
                hold["cqk"] = slab("cqk", layer=l)
            group("F", hold["cqk"], c0=256 * i + 128 * c, M=P, K=KD, dst=("qk", 4 + 2 * c + i),
                  scale=HD ** -0.5 if i == 0 else 1.0, layer=l)

        for c in range(2):
            for i in range(2):
                jobs.append((lambda c=c, i=i: cqk(c, i), 1, 4 * (c + 3)))

        def gate(c, l=l):
            if c == 0:
                hold["ag"] = slab("ag", layer=l)
            if c == 6:
                hold["ag"] = slab("bgcg", layer=l)
            g = group("gate", hold["ag"], c0=128 * (c % 4), M=P, K=KD, chunk=c, layer=l, first=c >= 6)
            steps.append(("gate2", g))
            steps.append(("gate3", g))

        for c in (0, 1, 2, 3, 6, 7, 4, 5):
            need = 0 if c >= 6 else 4 * (c + 1) + 6 if c < 4 else 16 + 8 * (c - 3) + 6
            jobs.append((lambda c=c: gate(c), 1, need))
        its = []
        for h in range(4):
            units.append(dict(kind="A", chunk=h, layer=l))
            for t in range(NT):
                its.append(dict(kind="A", head=h, tile=t, K=P * (t + 1), maps=2, unit=len(units) - 1,
                                rows=(0, P), q=2 * h, k=2 * h + 1, v=(128 * h, 128), after=3 * h))
        for kind, base in (("B", 0), ("C", 2)):
            for c in range(2):
                units.append(dict(kind=kind, chunk=4 + base + c, layer=l))
                for e in range(2):
                    for t in range(NT):
                        its.append(dict(kind=kind, head=2 * c + e, tile=t, K=P * (t + 1), maps=1,
                                        unit=len(units) - 1, rows=(64 * e, 64),
                                        q=2 * (c + base), k=2 * (c + base) + 1,
                                        v=(512 + 128 * (c + base) + 64 * e, 64),
                                        after=(15 + 2 * (c + 1) if kind == "B" else 19 + 2 * (c + 1))))
        weave(jobs, its)
        wo = [slab("wo", layer=l, half=h) for h in range(2)]
        final_layer = l == DEPTH - 1 and not only_block1
        for t in range(NT):
            for half in range(2):
                if t == 0:
                    state["mid"] = (lambda: [tick() for _ in range(2)]) if half == 0 else None
                g = group("T", wo[half], c0=0, N=512, K=KD, tile=t, dst=("resid", half), src="y", layer=l, late=t == 0)
                if t == 0 and half == 0:
                    state["mid"] = None
                if t == 0 and half == 1:
                    steps.append(("half", g))
                    groups[g]["split"] = True
                    flush()
                    steps.extend([("group", g - 1), ("group", g)])
            steps.append(("ln", (l, t)))
            if final_layer:
                if t:
                    steps.append(("norm", dict(tile=t - 1, nth=t - 1)))
            elif t:
                for half in range(2):
                    group("to_hT", tile=t - 1, half=half, layer=l)
            if final_layer and t >= 2:
                for half in range(2):
                    group("to_hT", tile=t - 2, half=half, layer=l, norm=t - 2)
        if final_layer:
            steps.append(("norm", dict(tile=NT - 1, nth=NT - 1)))
        for t in ((NT - 2, NT - 1) if final_layer else (NT - 1,)):
            for half in range(2):
                group("to_hT", tile=t, half=half, layer=l, **(dict(norm=t) if final_layer else {}))
    if not only_block1:
        second(steps, groups, slabs, items, units, state, slab, group, weave, flush)
    annotate(steps, groups, items, units)
    return dict(steps=steps, groups=groups, slabs=slabs, items=items, units=units)


def second(steps, groups, slabs, items, units, state, slab, group, weave, flush):
    l = DEPTH
    steps.append(("bounds", 0))
    steps.append(("angles", 0))
    state["slots"] = [0, 1]
    s_iq = slab("iq", K=KD, cols=512)
    s_ak = slab("avak", K=KD, cols=392)
    for c in range(4):
        group("F", s_iq, c0=128 * c, M=P, K=KD, dst=("qk", 4 + c), scale=1.0)
    steps.append(("sines", 0))
    group("F", s_ak, c0=264, M=P, K=KD, dst=("ik", 0), scale=1.0)
    for t in range(NT):
        group("T", s_ak, c0=0, N=136, K=KD, tile=t, dst=("av", 0))
    hold, made = {}, {}

    def from_slab(name, new, K=KD, cols=512):
        if new:
            made[name] = made.get(name, -1) + 1
            hold[name] = slab(name, K=K, cols=cols, nth_of_kind=made[name])
        return hold[name]

    jobs = [(lambda: group("F", s_ak, c0=136, M=P, K=KD, dst=("ak", 0), scale=1.0), 1, 0)]
    for c in range(4):
        jobs.append((lambda c=c: group("F", from_slab("saq", c == 0), c0=128 * c, M=P, K=KD, dst=("qk", c), scale=1.0), 1, 0))
    for c in range(3):
        jobs.append((lambda c=c: group("F", from_slab("mq", c == 0, cols=384), c0=128 * c, M=P, K=KD,
                                       dst=("cq", c), scale=1.0), 1, 0))
    for c in range(2):
        jobs.append((lambda c=c: group("F", from_slab("mkv", c == 0, cols=384), c0=128 * c, M=P, K=KD,
                                       dst=("ckv", c), scale=1.0), 1, 0))
    rot = {}

    def kpe():
        rot["kpe"] = group("F", hold["mkv"], c0=256, M=P, K=KD, dst=("raw", 0), scale=1.0)

    jobs.append((kpe, 1, 0))
    for t in range(NT):
        jobs.append((lambda t=t: group("T", from_slab("hi", t == 0), c0=0, N=512, K=KD, tile=t, dst=("V", 512)), 1, 0))
    its = [dict(kind="I", head=h, tile=t, K=P * (t + 1), maps=1, unit=None, after=0)
           for t in range(1, NT) for h in range(IDX_HEADS)]
    weave(jobs, its)
    flush()
    steps.append(("squares", "cq"))
    group("sumsq", what="cq", K=3)
    steps.append(("latent", "cq"))
    steps.append(("squares", "ckv"))
    group("sumsq", what="ckv", K=2)
    steps.append(("latent", "ckv"))
    group("swap", raw=rot["kpe"], dst=("kpe", 0), ring=0, table=1)
    s_qb = slab("qb", K=3, cols=768)
    s_kv = slab("kvb", K=2, cols=1024)
    raws = [group("F", s_qb, c0=512 + 128 * c, M=P, K=3, src="cq", dst=("raw", c), scale=1.0) for c in range(2)]
    for h in range(4):
        group("F", s_qb, c0=128 * h, M=P, K=3, src="cq", dst=("qn", h), scale=1.0)
        if h == 0:
            group("swap", raw=raws[0], dst=("qp", 0), ring=0, table=1)
        if h == 1:
            group("swap", raw=raws[1], dst=("qp", 1), ring=1, table=1)
    for h in range(4):
        group("F", s_kv, c0=128 * h, M=P, K=2, src="ckv", dst=("kn", h), scale=1.0)
    for t in range(NT):
        group("T", s_kv, c0=512, N=512, K=2, tile=t, src="ckv", dst=("V", 0))
    jobs = []

    def hgrn_q(h):
        hold["last_hgrn"] = hold.get("hgrn")
        group("F", from_slab("hgrn", True, cols=384), c0=128, M=P, K=KD, dst=("hq", 0), scale=P ** -0.5)

    def hgrn_f(h):
        group("F", hold["hgrn"], c0=0, M=P, K=KD, dst=("hf", 0), scale=1.0)

    def hgrn_project(h):
        hgrn_q(h)
        hgrn_f(h)

    def hgrn_level(h, lv):
        if lv + 1 < LEVELS:
            steps.append(("hg_level", (h, lv + 1)))
            steps.append(("hg_diff", (h, lv + 2)))
        else:
            steps.append(("hg_decay", h))
        g = group("hg_attn", head=h, level=lv)
        if lv >= 0:
            steps.append(("hg_put", hold["put"]))
        hold["put"] = g

    def hgrn_state(h):
        group("hg_turn", head=h)
        steps.append(("hg_put", hold["put"]))
        if h < 3:
            hgrn_q(h + 1)
        gs = [group("hg_state", head=h, part=i) for i in range(2)]
        if h < 3:
            hgrn_f(h + 1)
        steps.append(("hg_chain", (h, gs)))
        hold["states"] = gs
        if h < 3:
            steps.append(("hg_gate_a", (h + 1, 0)))
        hold["g"] = hgrn_gate(h)
        if h < 3:
            steps.append(("hg_gate_d", (h + 1, 0)))

    def hgrn_out(h):
        hold["hgout"] = group("hg_out", head=h, states=hold["states"])
        if h < 3:
            steps.append(("hg_gate_a", (h + 1, 1)))
        group("hg_meansq", head=h)
        steps.append(("hg_norm", h))
        steps.append(("gate3", hold["g"]))
        if h < 3:
            steps.append(("hg_gate_d", (h + 1, 1)))
            steps.append(("hg_diff", (h + 1, 0)))

    def hgrn_gate(h):
        g = group("gate", hold["last_hgrn"] if h < 3 else hold["hgrn"], c0=256, M=P, K=KD, chunk=4 + h, layer=l,
                  first=False, unit=None)
        steps.append(("gate2", g))
        return g

    for h in range(4):
        if h == 0:
            jobs.append((lambda h=h: hgrn_project(h), 2, 0))
            jobs.append((lambda: steps.extend([("hg_gate_a", (0, 0)), ("hg_gate_d", (0, 0))]), 1, 0))
            jobs.append((lambda: steps.extend([("hg_gate_a", (0, 1)), ("hg_gate_d", (0, 1)), ("hg_diff", (0, 0))]), 1, 0))
        for lv in range(-1, LEVELS):
            jobs.append((lambda h=h, lv=lv: hgrn_level(h, lv), 1, 0))
        jobs.append((lambda h=h: hgrn_state(h), 3, 0))
        jobs.append((lambda h=h: hgrn_out(h), 2, 0))
    its = []
    for kind in "MX":
        for h in range(4):
            units.append(dict(kind=kind, chunk=h, layer=l))
            for t in range(NT):
                its.append(dict(kind=kind, head=h, tile=t, K=P * (t + 1), maps=1, unit=len(units) - 1,
                                rows=(0, P), q=h, k=None, v=(128 * h if kind == "M" else 0, 128), after=0))
    weave(jobs, its)
    flush()
    state["slots"], state["turn"] = [W_SLOTS + j for j in range(4)], 0
    tail = [slab("gateup", K=KD, cols=192, at=1024 * b + 128 * c, up=128 * c, what=name)
            for b, name in enumerate(("w_up_a_2", "w_up_b_2", "w_up_c_2")) for c in range(8)]
    tail += [slab("wo2", K=KD, cols=256, quarter=h) for h in range(4)]
    tail += [slab("ffgu", K=KD, cols=256, at=128 * c) for c in range(KF)]
    tail += [slab("down", K=2, cols=1024, at=2 * i, last_down=i) for i in range(N_DOWN)]
    state["pieces"] = [(i, q) for i in tail for q in range(2)]
    for n, i in enumerate(tail):
        slabs[i]["parts_at"] = 2 * (n + 1)

    def split_weights(n=1):
        for _ in range(min(n, len(state["pieces"]))):
            i, q = state["pieces"].pop(0)
            steps.append(("split", dict(slab=i, piece=q, cols=slabs[i]["K"] * slabs[i]["cols"] // 2,
                                        nth=2 * tail.index(i) + q + 1)))

    steps.append(("tail", 0))
    split_weights(2)
    for q in range(4):
        steps.append(("split_x", ("hT", 2 * q, 2)))
    split_weights(2)
    steps.append(("split_x", ("ya", 0, 4)))
    for b, src in enumerate(("ya", "yb", "oc")):
        for c in range(8):
            sl = tail[8 * b + c]
            group("sigmoid", sl, c0=0, M=P, K=KD, ring=c % 2, parts=True)
            split_weights()
            group("up", sl, c0=0, M=P, K=4, src=src, branch=b, chunk=c, ring=c % 2, parts=True)
            split_weights()
            if c == 2 and b < 2:
                steps.append(("split_x", (("yb", "oc")[b], 0, 4)))
            if b == 2 and c:
                steps.append(("split_x", ("mix", c - 1, 1)))
    steps.append(("split_x", ("mix", 7, 1)))
    wo = tail[24:28]
    for quarter in range(4):
        last = quarter == 3
        for t in range(NT + last):
            if t < NT:
                group("T", wo[quarter], c0=0, N=256, K=KD, tile=t, dst=("resid2", quarter), src="mix", parts=True)
                if t in (1, 2):
                    split_weights()
            if last:
                if t < NT:
                    steps.append(("norm", dict(tile=t, nth=NT + t)))
                if t:
                    for hh in range(2):
                        group("to_hT", tile=t - 1, half=hh, norm=NT + t - 1, parts=True)
    for c in range(KF):
        sl = tail[28 + c]
        g = group("ffgate", sl, c0=0, M=P, K=KD, ring=c % 2, parts=True)
        split_weights()
        group("ffup", sl, c0=128, M=P, K=KD, chunk=c, ring=c % 2, gate=g, parts=True)
        split_weights()
        if 2 <= c < EARLY + 2:
            steps.append(("split_x", ("act", c - 2, 1)))
    for i in range(N_DOWN):
        if i == 0:
            for c in range(EARLY, EARLY + 4):
                steps.append(("split_x", ("act", c, 1)))
        for c in range(EARLY + 4 + 2 * i, min(KF, EARLY + 6 + 2 * i)):
            steps.append(("split_x", ("act", c, 1)))
        steps.append(("down", dict(i=i, slab=tail[28 + KF + i])))
        split_weights(2)
    for t in range(NT):
        steps.append(("final", t))


def annotate(steps, groups, items, units):
    count = {}

    def nth(key):
        count[key] = count.get(key, 0) + 1
        return count[key]

    hT_groups, tile_groups, norms = [], {}, 0
    slot, values, cums, seen = {}, {}, {}, {}
    ffups, resid2, turned_norm = [], {}, {}
    last_gate, done, order, parts_of = None, {}, [], {}
    for i, u in enumerate(units):
        u["sem"] = u["kind"] if u["kind"] in "AC" else "other"
        u["nth"] = nth(u["sem"])
        if u["kind"] == "C":
            done[(u["layer"], u["chunk"])] = ("unit", i)
    for op, arg in steps:
        if op == "gate3" and not groups[arg]["first"]:
            order.append((groups[arg]["layer"], groups[arg]["chunk"]))
        if op == "fin" and units[arg]["kind"] == "C":
            u = units[arg]
            order.append((u["layer"], u["chunk"]))
            u["gate"] = max(g["g"] for g in groups if g["kind"] == "gate" and (g["layer"], g["chunk"]) == order[-1])
            assert any(s_ == ("gate3", u["gate"]) for s_ in steps[:steps.index((op, arg))])
        if op in ("ln_in", "ln"):
            norms += 1
            seen[arg if op == "ln_in" else arg[1]] = norms
        elif op == "group":
            gr = groups[arg]
            kind, dst = gr["kind"], gr.get("dst") or ("", 0)
            if kind == "to_hT":
                if "norm" not in gr:
                    gr["after_ln"] = seen[gr["tile"]]
                hT_groups = (hT_groups + [arg])[-2:]
                tile_groups[gr["tile"]] = tile_groups.get(gr["tile"], [])[-1:] + [arg]
            gr["hT_group"], gr["hT_tile"] = list(hT_groups), list(tile_groups.get(gr.get("tile"), []))
            if dst[0] == "raw":
                gr["raw_free"] = count.get("swap", 0)
            if kind == "swap":
                gr["nth"] = nth("swap")
                slot[dst] = ("rot", gr["nth"])
                gr["tg_gate"] = last_gate
            if kind == "F" and dst[0] not in ("raw", "cumlog"):
                slot[dst] = ("group", arg)
            if dst[0] in ("V", "av"):
                values[(dst, gr["tile"])] = arg
            if dst[0] == "cumlog":
                gr["nth"] = nth("cumlog")
            if kind == "spread_cum":
                cums[gr["head"]] = arg
                gr["nth"] = count["cumlog"]
            if kind == "turn_cum":
                cums["turn"] = arg
            if kind == "gate":
                gr["nth"] = nth("gate")
                gr["tg_rot"] = count.get("swap", 0)
                gr["last_gate"] = last_gate
                if gr["first"]:
                    last_gate = ("group", arg)
                else:
                    last_gate = ("gated", nth("gated"))
                    done[(gr["layer"], gr["chunk"])] = last_gate
                if gr["layer"] < DEPTH:
                    gr["unit"] = max(i for i, u in enumerate(units)
                                     if u["chunk"] == gr["chunk"] and u["layer"] == gr["layer"])
            if kind == "meansq":
                units[gr["unit"]]["meansq"] = arg
                gr["nth"] = units[gr["unit"]]["nth"]
            if kind in ("gate", "ffgate"):
                gr["min_nth"] = nth("min")
            if kind == "ffup":
                ffups.append(arg)
            if kind == "ffgate":
                gr["free"] = ffups[-2] if len(ffups) >= 2 else None
            if dst[0] == "resid2":
                resid2[gr["tile"]] = resid2.get(gr["tile"], []) + [arg]
            if "norm" in gr:
                turned_norm[gr["norm"]] = arg + 1
            if kind in ("sigmoid", "up", "ffgate", "ffup", "hg_state", "hg_attn", "hg_turn", "hg_out"):
                gr["nth"] = nth(kind)
            if dst[0] in ("hf", "hq"):
                slot[dst[0]] = ("group", arg)
            if gr.get("src") == "y":
                gr["order"] = [(c, done[(gr["layer"], c)]) for c in sorted(range(KD), key=lambda c: order.index((gr["layer"], c)))]
            if gr.get("parts"):
                gr["x_low"] = parts_of.get(gr.get("src", "hT"), 0)
                src = gr.get("src", "hT")
                gr["chunks_low"] = [parts_of.get((src, k)) for k in range(KD)] if src in ("hT", "mix") and gr["x_low"] else None
                if kind == "to_hT":
                    parts_of["hT"] = 0
            gr["slots"] = dict(slot) if kind.startswith("hg_") else None
            gr["vals"] = dict(values) if kind.startswith("hg_") else None
        elif op == "split_x":
            parts_of[arg[0]] = nth("x_part")
            for k in range(arg[1], arg[1] + arg[2]):
                parts_of[(arg[0], k)] = parts_of[arg[0]]
        elif op == "down":
            arg["acts_low"] = [parts_of[("act", 2 * arg["i"] + k)] for k in range(2)]
        elif op == "norm":
            if arg["nth"] >= NT:
                arg["groups"] = resid2[arg["tile"]]
            if arg["nth"] >= 2:
                arg["turned"] = turned_norm[arg["nth"] - 2]
        elif op == "scores":
            it = items[arg]
            kind, h = it["kind"], it["head"]
            if kind in "ABC":
                names = [("qk", it["q"]), ("qk", it["k"])]
                vkey = ("V", 0 if it["v"][0] < 512 else 512)
            elif kind == "I":
                names, vkey = [("qk", 4 + h // 2), ("ik", 0)], None
            elif kind == "M":
                names, vkey = [("qn", h), ("kn", h), ("qp", h // 2), ("kpe", 0)], ("V", 0)
            else:
                names, vkey = [("qk", h), ("ak", 0)], ("av", 0)
            it["operands"] = [slot[n] for n in names]
            if vkey:
                it["values"] = [values[(vkey, t)] for t in range(it["tile"] + 1)][-2:]
            if kind == "B":
                it["cums"] = [cums[h], cums["turn"]]


def two_blocks(nc, a, out, only_block1=False):
    pl = plan(only_block1)
    steps, groups, slabs, items, units = (pl[k] for k in ("steps", "groups", "slabs", "items", "units"))

    def passed(kinds):
        at, c = [], 0
        for it in items:
            c += it["kind"] in kinds
            at.append(c)
        return at

    soft1_at, stick_at, turned_at = passed("ABXM"), passed("C"), passed("ABCXM")
    first_map, m = [], 0
    for it in items:
        first_map.append(m)
        m += it["maps"]
    owner = [n for n, it in enumerate(items) for _ in range(it["maps"])]

    def use(g):
        return g // PROJ_BANKS + 1

    with ExitStack() as ctx:
        def sb(name, shape, dt=F32):
            return ctx.enter_context(nc.sbuf_tensor(name, shape, dt))

        def sem(name):
            return ctx.enter_context(nc.semaphore(name))

        def next_place():
            return -(-nc.sbuf_base // 32) * 32

        base = next_place()
        W = sb("weights", [P, W_SLOTS, KD * 512])
        qk = sb("qk", [P, 8, S])
        bias = sb("rel_bias", [P, 4, OFF[NT]])
        X2 = sb("index_and_shared", [P, 3, S])
        E = sb("E", [P, 2, 2, S])
        PR = sb("probs", [P, 3, S])
        PT = sb("probs_T", [P, 2, S])
        raw = sb("raw", [P, 2, S])
        arena_end = next_place()

        def over(name, at, shape, dt=F32R):
            assert at + 4 * int(np.prod(shape[1:])) <= nc.sbuf_usable_end
            return nc.alloc_sbuf_tensor_at(name, shape, dt, offset=at)

        slot_bytes = 4 * KD * 512
        bias_at, shared_at = base + 4 * slot_bytes, base + 4 * slot_bytes + 4 * 4 * OFF[NT]
        WH = over("weights_high", base + 2 * slot_bytes, [P, 2, KD * 512])
        WL = over("weights_low", base, [P, 2, KD * 512])
        xh = {"hT": over("hT_high", bias_at, [P, KD, S])}
        yh = over("branches_high", shared_at, [P, 12, S])
        xh.update(ya=yh[:, 0:4, :], yb=yh[:, 4:8, :], oc=yh[:, 8:12, :])
        assert shared_at + 4 * 12 * S <= arena_end
        acts_more = over("acts_more", shared_at, [P, 6, S], F32)
        more_low = over("acts_more_low", shared_at, [P, 6, S])
        early_high = over("acts_early_high", shared_at + 4 * 6 * S, [P, EARLY, S])
        assert shared_at + 4 * (6 + EARLY) * S <= arena_end
        bf_w = sb("bf_weights", [P, KD, 4])
        xl = {}
        hT_at = next_place()
        hT = sb("hT", [P, KD, S])
        h_tok = sb("h_tok", [P, NT, D])
        V_at = next_place()
        V = sb("V", [P, NT, 1024])
        y_at = next_place()
        y = sb("y", [P, KD, S])
        L = sb("logits", [P, 2, S])
        tg = sb("tg", [P, 2, S])
        z = sb("z", [P, D])
        RC_at = next_place()
        RC = sb("rows_or_spread", [P, 4, S])
        rows = RC[:, :, :].rearrange("p (a b) c -> p a (b c)", a=2)
        ckb = RC
        oc = RC
        xl["hT"] = over("hT_low", hT_at, [P, KD, S])
        yl = over("branches_low", y_at, [P, KD, S])
        xl.update(ya=yl[:, 0:4, :], yb=yl[:, 4:8, :], oc=over("oc_low", RC_at, [P, 4, S]),
                  mix=over("mix_low", V_at, [P, KD, S]))
        xh["mix"] = over("mix_high", y_at, [P, KD, S])
        CN = sb("constants", [P, CONST_USED])
        identb = sb("identb", [P, P], BF16)
        negb = sb("negb", [P, 2, P], BF16)
        small = sb("small", [P, 256])
        cols = [0]

        def col(n):
            c = cols[0]
            cols[0] += n
            return small[:, c:c + n]

        sums, nmax, rsum = col(4), col(4), col(4)
        c2, mv, lnv, eps = col(2), col(2), col(2), col(3)
        stats = col(12)
        lam_s, lam, gcol, gin, bfc = col(8), col(1), col(1), col(DEPTH), col(DEPTH)
        cqc = sb("cum_by_query", [P, NT, 4])
        lam_in = sb("lam_in", [P, 4, HD])
        cum, cum_min = z[0:4, 0:S], z[0:4, S:2 * S]
        cum_l = y[0:4, 7, :]

        masks8 = sb("level_masks", [P, (LEVELS + 1) * P], U8)
        keep = sb("chunk_keep", [P, S], BF16)
        akT, avv, ikT = X2[:, 0, :], X2[:, 1, :].rearrange("p (t n) -> p t n", t=NT), X2[:, 2, :]
        iw = col(NT * IDX_HEADS).rearrange("p (t h) -> p t h", h=IDX_HEADS)
        m8, ss, dec = col(8), col(2), col(NCH)
        mq_g, mkv_g, out_g, lbx, lbs = col(3), col(2), col(1), col(4), col(4)
        log_lb, l1p, oml, l1a = col(4), col(4), col(4), col(4)
        X = W[:, 2, :].rearrange("p (c n) -> p c n", n=S)
        cqT, ckvT, qp, kpe = X[:, 0:3, :], X[:, 3:5, :], X[:, 5:7, :], X[:, 7, :]
        flat = h_tok[:, :, :].rearrange("p t (a n) -> p (t a) n", n=S)
        qn, kn = flat[:, 0:4, :], flat[:, 4:8, :]
        hF, hA, hK, hQ = (qk[:, 4 + i, :] for i in range(4))
        hB, hG, hQD, hKE, hATT = (X[:, i, :] for i in range(5))
        hQT, hKT = [hQD, z[:, 0:S]], [hKE, z[:, S:2 * S]]
        states = raw[:, :, :].rearrange("p a (b v) -> p (a b) v", v=P)
        mix = V[:, :, :].rearrange("p t (a n) -> p (t a) n", n=S)
        nz = [z[:, :], L[:, :, :].rearrange("p a n -> p (a n)")]
        final_3 = over("final_3", bias_at + 4 * KD * S, [P, D], F32)
        assert 4 * (KD * S + D) <= 4 * 4 * OFF[NT]
        final = nz + [hT[:, 6:8, :].rearrange("p a n -> p (a n)"), final_3[:, :]]
        attn_row = raw[:, :, :].rearrange("p a n -> p (a n)")

        def norm_rows(k):
            return E[:, k % 2, :, :].rearrange("p a n -> p (a n)") if k < NT else nz[k % 2]

        pkb, below = X2[:, 0, :], [X2[:, 1, :], X2[:, 2, :]]
        pos_i = sb("pos_i", [P, NT], I32)
        pq = col(NT)
        deltas = sb("bias_deltas", [P, REL_BUCKETS, 4])
        starts = sb("bucket_limits", [P, NT])
        acts = [x_[:, c, :] for x_, n in ((y, 8), (mix, 8), (acts_more, 6)) for c in range(n)]
        acts_low = [x_[:, c, :] for x_, n in ((yl, 8), (xl["mix"], 8), (more_low, 6)) for c in range(n)]
        acts_high = [x_[:, c, :] for x_, n in ((early_high, EARLY), (xh["hT"], 8), (xl["hT"], 6)) for c in range(n)]
        whole = {"hT": hT, "ya": y[:, 0:4, :], "yb": y[:, 4:8, :], "oc": oc, "mix": mix}
        x_spill = nc.dram_tensor("x_spill", (S, D), F32, kind="Internal").ap()

        def cn(name):
            c, n = CONST_AT[name]
            return CN[:, c:c + n]

        def b_at(h, t):
            return bias[:, h, OFF[t]:OFF[t + 1]]

        def bank(name):
            return ctx.enter_context(nc.psum_tensor(name, [P, S], F32))

        proj = [bank(f"proj{i}") for i in range(PROJ_BANKS)]
        sc = [bank(f"score{i}") for i in range(SCORE_BANKS)]
        T = bank("turned_probs")
        O = [bank(f"attn_out{i}") for i in range(2)]
        down = [proj[0], proj[1], sc[0], sc[1], sc[2], T, O[0], O[1]]

        loaded = [sem(f"weights_loaded{i}") for i in range(W_SLOTS + 4)]
        consts_in, staged_in, x_in, rows_in, lam_loaded = (
            sem("consts_in"), sem("staged_in"), [sem(f"x_in{t}") for t in range(NT)], sem("rows_in"), sem("lam_loaded"))
        group_full = sem("group_full")
        evac = [sem(f"bank_read{i}") for i in range(PROJ_BANKS)]
        prep, eps_set, ident_in = sem("prep_done"), sem("eps_set"), sem("ident_in")
        N_CONSTS_IN = 16 * (1 + 2 * DEPTH + (0 if only_block1 else 10))
        rot_done = sem("rotated")
        gate_ln, gate_min, gate_sig, gated = sem("gate_ln"), sem("gate_min"), sem("gate_sigmoid"), sem("gated")
        cum_ln, cum_done = sem("cum_ln"), sem("cum_done")
        scores_full, soft1_done, exp_done = sem("scores_full"), sem("soft1_done"), sem("exp_done")
        soft2_done, stick_done = sem("soft2_done"), sem("stick_done")
        turned, turned_out, pv_done = sem("turned"), sem("turned_out"), sem("pv_done")
        o_free = {k: sem(f"unit_done_{k}") for k in ("A", "C", "other")}
        sq_done = sem("squares_done")
        lam_dot, lam_exp, lam_done = sem("lam_dot"), sem("lam_exp"), sem("lam_done")
        var_done, rstd_done, ln_done = sem("var_done"), sem("rstd_done"), sem("ln_done")
        dve_step, act_step = sem("vector_step"), sem("scalar_step")
        stored = sem("stored")
        pos_in = sem("pos_in")
        bias_mask, bias_done = sem("bias_mask"), sem("bias_done")
        attn_row_in, first_rows_in = sem("attn_norm_in"), sem("first_rows_in")
        spilled, x_back = sem("x_spilled"), sem("x_back")
        lb_d, lb_a = sem("lb_vector"), sem("lb_scalar")
        table_a, table_d = sem("rope_table_scalar"), sem("rope_table_vector")
        norm_r, norm_done = sem("norm_rstd"), sem("norm_done")
        lat_sq, lat_done = sem("latent_squares"), sem("latents_normed")
        hg_act, hg_dve, hg_diff, hg_exp, hg_ready = (
            sem("hgrn_scalar"), sem("hgrn_vector"), sem("hgrn_diff"), sem("hgrn_exp"), sem("hgrn_ready"))
        hg_de, hg_kd = sem("hgrn_decay_exp"), sem("hgrn_decayed")
        w_high, w_low, x_high, x_low = sem("weights_high"), sem("weights_low"), sem("x_high"), sem("x_low")
        hg_sq, hg_normed = sem("hgrn_squares"), sem("hgrn_normed")
        mix_done, down_full, hg_ready0 = sem("mix_done"), sem("down_full"), sem("hgrn_cleared")
        fin_sum, fin_done = sem("final_sum"), sem("final_done")

        def halves(x, half, b):
            return x.rearrange("p (n a b) -> p n a b", a=2, b=b)[:, :, half, :]

        def unit_done(eng, u):
            eng.wait_ge(o_free[units[u]["sem"]], units[u]["nth"])

        def bank_of(g):
            return proj[g % PROJ_BANKS], evac[g % PROJ_BANKS]

        def group_waits(eng):
            reached = {}

            def wait(g):
                b, n = g % PROJ_BANKS, use(g)
                if reached.get(b, 0) < n:
                    reached[b] = n
                    eng.wait_ge(evac[b], n)
            return wait

        def passed_token(eng, wait_group, token):
            what, n = token
            if what == "group":
                wait_group(n)
            elif what == "gated":
                eng.wait_ge(gated, n)
            else:
                unit_done(eng, n)

        w_in = a["w_in"].rearrange("l (k p) n -> l p k n", p=P)
        w_out = a["w_out"].rearrange("l (k p) n -> l p k n", p=P)

        def by_k(name):
            return a[name][0].rearrange("(k p) n -> p k n", p=P)

        w2 = by_k("w_in_2") if not only_block1 else None
        in_slabs = {"av": [(AV, 512)], "aq": [(AQ, 512)], "ak": [(AK, 512)],
                    "bvcv": [(BV, 256), (CV, 256), (BFG, 4)], "bqk": [(BQ, 512)], "cqk": [(CQ, 512)],
                    "ag": [(AG, 512)], "bgcg": [(BG, 256), (CG, 256)]}
        in2_slabs = {"iq": [(IQ, 512)], "avak": [(XV, 128), (IW, 8), (XK, 128), (IK, 64), (IK, 64)],
                     "saq": [(XQ, 512)], "mq": [(MQ, 384)], "mkv": [(MKV, 256), (MPE, 64), (MPE, 64)],
                     "hi": [(HI, 512)]}

        def half_slots(w, s_):
            n, h = KD * 512 // 2, s_["halves"]
            return w[:, :, :].rearrange("p s n -> p (s n)")[:, n * h[0]:n * (h[-1] + 1)]

        def slab_view(i):
            s_ = slabs[i]
            k, n = s_.get("K", KD), s_.get("cols", 512)
            return half_slots(W, s_)[:, 0:k * n].rearrange("p (k n) -> p k n", k=k)

        def pieces(i):
            s_, v = slabs[i], slab_view(i)
            name = s_["name"]
            got, c = [], 0
            if name == "wo":
                return [(v, w_out[s_["layer"], :, :, 512 * s_["half"]:512 * (s_["half"] + 1)])]
            if name in in_slabs and "layer" in s_:
                for c0, n in in_slabs[name]:
                    dst = bf_w[:, :, :] if n == 4 else v[:, :, c:c + n]
                    got.append((dst, w_in[s_["layer"], :, :, c0:c0 + n]))
                    c += n
                return got
            if name in in2_slabs:
                for c0, n in in2_slabs[name]:
                    got.append((v[:, :, c:c + n], w2[:, :, c0:c0 + n]))
                    c += n
                return got
            if name == "hgrn":
                h = s_["nth_of_kind"]
                return [(v[:, :, 128 * j:128 * j + 128], w2[:, :, c0 + 128 * h:c0 + 128 * h + 128])
                        for j, c0 in enumerate((HF, HQ, HG))]
            if name == "qb":
                w = by_k("mla_w_qb_2")
                for h in range(4):
                    got.append((v[:, :, 128 * h:128 * h + 128], w[:, :, 192 * h:192 * h + 128]))
                    got.append((v[:, :, 512 + 64 * h:576 + 64 * h], w[:, :, 192 * h + 128:192 * h + 192]))
                return got
            if name == "kvb":
                w = by_k("mla_w_kvb_2")
                for h in range(4):
                    got.append((v[:, :, 128 * h:128 * h + 128], w[:, :, 256 * h:256 * h + 128]))
                    got.append((v[:, :, 512 + 128 * h:640 + 128 * h], w[:, :, 256 * h + 128:256 * h + 256]))
                return got
            if name == "gateup":
                flat_w = half_slots(W, s_)
                return [(flat_w[:, 0:KD * P].rearrange("p (k n) -> p k n", k=KD),
                         w2[:, :, GATE + s_["at"]:GATE + s_["at"] + P]),
                        (flat_w[:, KD * P:(KD + 4) * P].rearrange("p (k n) -> p k n", k=4),
                         by_k(s_["what"])[:, :, s_["up"]:s_["up"] + P])]
            if name == "wo2":
                return [(v, by_k("w_out_2")[:, :, 256 * s_["quarter"]:256 * (s_["quarter"] + 1)])]
            if name == "ffgu":
                at = slice(s_["at"], s_["at"] + P)
                return [(v[:, :, 0:P], by_k("w_ffn_gate_2")[:, :, at]), (v[:, :, P:2 * P], by_k("w_ffn_up_2")[:, :, at])]
            assert name == "down"
            return [(v, by_k("w_ffn_down_2")[:, s_["at"]:s_["at"] + s_["K"], :])]

        landed, total = [], [0] * (W_SLOTS + 4)
        for i in range(len(slabs)):
            total[slabs[i]["slot"]] += 16 * len(pieces(i))
            landed.append(total[slabs[i]["slot"]])

        last_B = [max((n for n, it in enumerate(items) if it["kind"] == "B" and units[it["unit"]]["layer"] == l))
                  for l in range(DEPTH)]
        last_C = max(n for n, it in enumerate(items) if it["kind"] == "C")
        last_M = max((n for n, it in enumerate(items) if it["kind"] == "M"), default=None)
        last_up = max((gr["g"] for gr in groups if gr["kind"] == "up"), default=None)
        n_ln = NT * (DEPTH + 1)

        ffup_group = [gr["g"] for gr in groups if gr["kind"] == "ffup"]
        tail_group = next((gr["g"] for gr in groups if gr.get("parts")), None)
        n_gated = sum(gr["kind"] == "gate" and not gr["first"] for gr in groups)
        arg_group = {gr["what"]: gr["g"] for gr in groups if gr["kind"] == "sumsq"}
        level_group = {(gr["head"], gr["level"]): gr["g"] for gr in groups if gr["kind"] == "hg_attn"}
        turn_group = {gr["head"]: gr["g"] for gr in groups if gr["kind"] == "hg_turn"}
        head_meansq = {gr["head"]: gr["g"] for gr in groups if gr["kind"] == "hg_meansq"}
        hf_group = [gr["g"] for gr in groups if (gr.get("dst") or ("",))[0] == "hf"]
        hq_group = [gr["g"] for gr in groups if (gr.get("dst") or ("",))[0] == "hq"]
        puts = sorted(level_group.values())
        arg_prev_put = dict(zip(puts[1:], puts[:-1]))

        block = ctx.enter_context(nc.Block())

        @block.sync
        def _(sp):
            for t in range(NT):
                sp.dma_start(h_tok[:, t, :], a["x"][0, t * P:(t + 1) * P, :]).then_inc(x_in[t], 16)
                if t == 0:
                    sp.dma_start(rows[:, 0, :], a["ln_in_g"].partition_broadcast(P)).then_inc(first_rows_in, 16)
                    sp.dma_start(rows[:, 1, :], a["ln_in_b"].partition_broadcast(P)).then_inc(first_rows_in, 16)
                    sp.dma_start(CN[:, 0:P], a["constants"][:, 0:P]).then_inc(ident_in, 16)
            for i, s_ in enumerate(slabs):
                for q in (slabs[j] for j in s_["prev"]):
                    if "last_down" in q:
                        sp.wait_ge(down_full, q["last_down"] + 1)
                    else:
                        sp.wait_ge(group_full, q["last"] + 1)
                for dst, src in pieces(i):
                    sp.dma_start(dst, src).then_inc(loaded[s_["slot"]], 16)
            if only_block1:
                sp.wait_ge(ln_done, n_ln)
                for t in range(NT):
                    sp.dma_start(out[0, t * P:(t + 1) * P, :], h_tok[:, t, :]).then_inc(stored, 16)
            else:
                for t in range(NT):
                    sp.wait_ge(fin_done, t + 1)
                    sp.dma_start(out[0, t * P:(t + 1) * P, :], final[t]).then_inc(stored, 16)
            sp.wait_ge(stored, 16 * NT)

        @block.gpsimd
        def _(pool):
            pool.dma_start(CN[:, P:], a["constants"][:, P:CONST_USED]).then_inc(consts_in, 16)
            pool.dma_start(z[:, 0:STAGED_Z], a["constants"][:, CONST_USED:CONST_USED + STAGED_Z]).then_inc(staged_in, 16)
            pool.dma_start(raw[:, :, :].rearrange("p a n -> p (a n)")[:, 0:(LEVELS + 1) * P],
                           a["constants"][:, CONST_USED + STAGED_Z:]).then_inc(staged_in, 16)
            for l in range(DEPTH):
                pool.dma_start(gin[:, l:l + 1], a["subln_g"][l].rearrange("(p a) -> p a", a=1)).then_inc(consts_in, 16)
                pool.dma_start(bfc[0:4, l:l + 1], a["b_forget"][l].rearrange("(p a) -> p a", a=1)).then_inc(consts_in, 16)
            if not only_block1:
                for dst, name, n in ((mq_g, "mla_q_norm_2", 3), (mkv_g, "mla_kv_norm_2", 2),
                                     (out_g, "hgrn_out_norm_2", 1), (lbx, "hgrn_lb_logits_2", 4)):
                    for k in range(n):
                        pool.dma_start(dst[:, k:k + 1], a[name][0, P * k:P * k + P].rearrange("(p a) -> p a", a=1))\
                            .then_inc(consts_in, 16)
                for t in range(NT):
                    pool.dma_start(pos_i[:, t:t + 1], a["positions_2"][0, P * t:P * t + P].rearrange("(p a) -> p a", a=1))\
                        .then_inc(pos_in, 16)
                pool.dma_start(below[0].bitcast(I32), a["positions_2"][0].partition_broadcast(P)).then_inc(pos_in, 16)
                pool.dma_start(deltas[:, :, :].rearrange("p b h -> p (b h)"),
                               a["rel_bias_2"].rearrange("b h -> (b h)").partition_broadcast(P)).then_inc(pos_in, 16)
            for l in range(DEPTH):
                if l:
                    pool.wait_ge(lam_done, 2 * l)
                for i, name in enumerate(("lambda_q1", "lambda_k1", "lambda_q2", "lambda_k2")):
                    pool.dma_start(lam_in[:, i, :], a[name][l].partition_broadcast(P)).then_inc(lam_loaded, 16)
                pool.wait_ge(ln_done, NT * (l + 1))
                pool.wait_ge(soft1_done, soft1_at[last_B[l]])
                if l == DEPTH - 1 and not only_block1:
                    pool.wait_ge(rot_done, NT * 2 * DEPTH)
                    pool.dma_start(attn_row, a["attn_norm_2"][0].partition_broadcast(P)).then_inc(attn_row_in, 16)
                pool.dma_start(rows[:, 0, :], a["ln_g"][l].partition_broadcast(P)).then_inc(rows_in, 16)
                pool.dma_start(rows[:, 1, :], a["ln_b"][l].partition_broadcast(P)).then_inc(rows_in, 16)
            if not only_block1:
                pool.wait_ge(ln_done, n_ln)
                for t in range(NT):
                    pool.dma_start(x_spill[t * P:(t + 1) * P, :], h_tok[:, t, :]).then_inc(spilled, 16)
                pool.wait_ge(spilled, 16 * NT)
                pool.wait_ge(scores_full, last_M + 1)
                for t in range(NT):
                    pool.dma_start(h_tok[:, t, :], x_spill[t * P:(t + 1) * P, :]).then_inc(x_back, 16)
                pool.wait_ge(group_full, last_up + 1)
                pool.dma_start(rows[:, 0, :], a["ffn_norm_2"][0].partition_broadcast(P)).then_inc(rows_in, 16)
                pool.dma_start(rows[:, 1, :], a["final_norm_2"].partition_broadcast(P)).then_inc(rows_in, 16)

        @block.tensor
        def _(pe):
            pe.wait_ge(ident_in, 16)
            seen = set()
            wait_group = group_waits(pe)

            def weights(i):
                if i not in seen:
                    seen.add(i)
                    pe.wait_ge(loaded[slabs[i]["slot"]], landed[i])
                return slab_view(i)

            for op, arg in steps:
                if op == "prep":
                    pe.wait_ge(consts_in, N_CONSTS_IN)
                    pe.wait_ge(prep, N_PREP)
                elif op in ("group", "half"):
                    gr = groups[arg]
                    g, kind = arg, gr["kind"]
                    ps, _ = bank_of(g)
                    if g >= PROJ_BANKS:
                        wait_group(g - PROJ_BANKS)
                    if gr["slab"] is not None:
                        w = weights(gr["slab"])
                        if (gr.get("dst") or ("",))[0] == "cumlog":
                            w, c0 = bf_w, 0
                        else:
                            c0 = gr["c0"]
                        src = gr.get("src", "hT")
                        if src == "y":
                            pass
                        elif gr.get("chunks_low"):
                            pass
                        elif gr.get("parts") and src != "hT":
                            pe.wait_ge(x_low, gr["x_low"])
                        elif gr.get("parts") and gr["x_low"]:
                            pe.wait_ge(x_low, gr["x_low"])
                        elif src in ("cq", "ckv"):
                            pe.wait_ge(lat_done, 1 if src == "cq" else 2)
                        else:
                            for gg in (gr["hT_tile"] if kind == "T" else gr["hT_group"]):
                                wait_group(gg)
                        if gr.get("parts"):
                            i, K = gr["slab"], gr["K"]
                            pe.wait_ge(w_low, slabs[i]["parts_at"])
                            n_, off = slabs[i]["cols"], 0
                            if slabs[i]["name"] == "gateup":
                                n_, off = P, 0 if K == KD else KD * P
                            wh, wl = (half_slots(w_, slabs[i])[:, off:off + K * n_].rearrange("p (k n) -> p k n", k=K)
                                      for w_ in (WH, WL))
                            for k in range(K):
                                if gr["chunks_low"] is not None:
                                    pe.wait_ge(x_low, gr["chunks_low"][k])
                                for j, (w_, x_) in enumerate(((wh, xh[src]), (wh, xl[src]), (wl, xh[src]))):
                                    first, last = k == 0 and j == 0, k == K - 1 and j == 2
                                    if kind == "T":
                                        t = gr["tile"]
                                        mm = nc.tensor.matmul(ps[:, 0:gr["N"]], x_[:, k, t * P:(t + 1) * P],
                                                              w_[:, k, c0:c0 + gr["N"]], start=first, stop=last)
                                    else:
                                        mm = nc.tensor.matmul(ps[:, :], w_[:, k, c0:c0 + P], x_[:, k, :],
                                                              start=first, stop=last)
                            mm.then_inc(group_full, 1)
                            continue
                        x = {"hT": hT[:, :, :], "y": y[:, :, :], "cq": cqT, "ckv": ckvT}[src]
                        begin, end = 0, gr["K"]
                        if op == "half":
                            end = gr["K"] // 2
                        elif gr.get("split"):
                            begin = gr["K"] // 2
                        for i in range(begin, end):
                            k, first, last = i, i == 0, i == gr["K"] - 1
                            if src == "y":
                                k, token = gr["order"][i]
                                passed_token(pe, wait_group, token)
                            if kind == "T":
                                t = gr["tile"]
                                mm = nc.tensor.matmul(ps[:, 0:gr["N"]], x[:, k, t * P:(t + 1) * P],
                                                      w[:, k, c0:c0 + gr["N"]], start=first, stop=last)
                            else:
                                mm = nc.tensor.matmul(ps[0:gr["M"], :], w[:, k, c0:c0 + gr["M"]],
                                                      x[:, k, :], start=first, stop=last)
                        if op == "group":
                            mm.then_inc(group_full, 1)
                    elif kind == "swap":
                        wait_group(gr["raw"])
                        nc.tensor.matmul(ps[:, :], cn(f"swap{gr['table'] + 1}"), raw[:, gr["ring"], :],
                                         start=True, stop=True).then_inc(group_full, 1)
                    elif kind == "spread_cum":
                        pe.wait_ge(cum_done, gr["nth"])
                        h = gr["head"]
                        nc.tensor.matmul(ps[:, :], cn("ident")[0:4, h:h + 1].to_broadcast([4, P]), cum,
                                         start=True, stop=True).then_inc(group_full, 1)
                    elif kind == "turn_cum":
                        for t in range(NT):
                            mm = nc.tensor.transpose(ps[:, 4 * t:4 * t + 4], cum[:, t * P:(t + 1) * P],
                                                     cn("ident")[0:4, 0:4])
                        mm.then_inc(group_full, 1)
                    elif kind in ("meansq", "hg_meansq"):
                        if kind == "meansq":
                            pe.wait_ge(sq_done, gr["nth"])
                        else:
                            pe.wait_ge(hg_sq, gr["head"] + 1)
                        nc.tensor.matmul(ps[:, :], cn("ones"), tg[:, 1, :],
                                         start=True, stop=True).then_inc(group_full, 1)
                    elif kind == "sumsq":
                        pe.wait_ge(lat_sq, 1 if gr["what"] == "cq" else 2)
                        for k in range(gr["K"]):
                            mm = nc.tensor.matmul(ps[:, :], cn("ones"), qn[:, k, :], start=(k == 0),
                                                  stop=(k == gr["K"] - 1))
                        mm.then_inc(group_full, 1)
                    elif kind == "to_hT":
                        t = gr["tile"]
                        if "norm" in gr:
                            pe.wait_ge(norm_done, gr["norm"] + 1)
                            row = norm_rows(gr["norm"])
                        else:
                            pe.wait_ge(ln_done, gr["after_ln"])
                            row = h_tok[:, t, :]
                        for j in range(4):
                            k = 4 * gr["half"] + j
                            mm = nc.tensor.transpose(ps[:, j * P:(j + 1) * P], row[:, k * P:(k + 1) * P], cn("ident"))
                        mm.then_inc(group_full, 1)
                    elif kind == "hg_attn":
                        h, lv = gr["head"], gr["level"]
                        if lv < 0:
                            pe.wait_ge(hg_dve, 2 * (h + 1))
                            wait_group(gr["slots"]["hq"][1])
                            kk, qq = hK, hQ
                        else:
                            pe.wait_ge(hg_ready, LEVELS * h + lv + 1)
                            kk, qq = hKT[lv % 2], hQT[lv % 2]
                        for i in range(NT):
                            r = slice(i * P, (i + 1) * P)
                            mm = nc.tensor.matmul(ps[:, r], kk[:, r], qq[:, r], start=True, stop=True)
                        mm.then_inc(group_full, 1)
                    elif kind == "hg_turn":
                        pe.wait_ge(hg_kd, gr["head"] + 1)
                        for i in range(NT):
                            r = slice(i * P, (i + 1) * P)
                            mm = nc.tensor.transpose(ps[:, r], hA[:, r], cn("ident"))
                        mm.then_inc(group_full, 1)
                    elif kind == "hg_state":
                        wait_group(turn_group[gr["head"]])
                        for gg in (gr["vals"][(("V", 512), t)] for t in range(NT)):
                            wait_group(gg)
                        v0 = 512 + P * gr["head"]
                        for n in range(gr["part"], NCH - 1, 2):
                            r = slice(64 * (n % 2), 64 * (n % 2) + 64)
                            mm = nc.tensor.matmul(ps[:, (n // 2) * P:(n // 2 + 1) * P],
                                                  hF[r, (n // 2) * P:(n // 2 + 1) * P], V[r, n // 2, v0:v0 + P],
                                                  start=True, stop=True)
                        mm.then_inc(group_full, 1)
                    elif kind == "hg_out":
                        for gg in gr["states"]:
                            wait_group(gg)
                        v0 = 512 + P * gr["head"]
                        for i in range(NT):
                            mm = nc.tensor.matmul(ps[:, i * P:(i + 1) * P], V[:, i, v0:v0 + P],
                                                  hATT[:, i * P:(i + 1) * P], start=True, stop=False)
                            for n in range(max(1, 2 * i), 2 * i + 2):
                                r = slice(CHUNK * n, CHUNK * n + CHUNK)
                                mm = nc.tensor.matmul(ps[:, r], states[:, n, :], hQD[:, r], start=False,
                                                      stop=(n == 2 * i + 1))
                        mm.then_inc(group_full, 1)
                elif op == "scores":
                    it = items[arg]
                    t, K, kind = it["tile"], it["K"], it["kind"]
                    for what, idx in it["operands"]:
                        if what == "rot":
                            pe.wait_ge(rot_done, idx)
                        else:
                            wait_group(idx)
                    for j in range(it["maps"]):
                        m_ = first_map[arg] + j
                        if m_ >= SCORE_BANKS:
                            b = owner[m_ - SCORE_BANKS]
                            kb = items[b]["kind"]
                            if kb in "AMI":
                                pe.wait_ge(exp_done, b + 1)
                            elif kb in "BX":
                                pe.wait_ge(soft1_done, soft1_at[b])
                            else:
                                pe.wait_ge(soft2_done, b + 1)
                        ps = sc[m_ % SCORE_BANKS]
                        tq = slice(t * P, (t + 1) * P)
                        if kind in "ABC":
                            r0, rn = (64 * j, 64) if kind == "A" else it["rows"]
                            r = slice(r0, r0 + rn)
                            nc.tensor.matmul(ps[:, 0:K], qk[r, it["q"], tq], qk[r, it["k"], 0:K], start=True, stop=False)
                            if j == it["maps"] - 1:
                                for b in range(first_map[arg], m_ + 1):
                                    mm = nc.tensor.matmul(sc[b % SCORE_BANKS][:, K - P:K], identb[:, :],
                                                          negb[:, int(kind == "C"), :], start=False, stop=True)
                        elif kind == "I":
                            h = it["head"]
                            r = slice(64 * (h % 2), 64 * (h % 2) + 64)
                            mm = nc.tensor.matmul(ps[:, 0:K], qk[r, 4 + h // 2, tq], ikT[r, 0:K], start=True, stop=True)
                        elif kind == "M":
                            h = it["head"]
                            r = slice(64 * (h % 2), 64 * (h % 2) + 64)
                            nc.tensor.matmul(ps[:, 0:K], qn[:, h, tq], kn[:, h, 0:K], start=True, stop=False)
                            nc.tensor.matmul(ps[:, 0:K], qp[r, h // 2, tq], kpe[r, 0:K], start=False, stop=False)
                            mm = nc.tensor.matmul(ps[:, K - P:K], identb[:, :], negb[:, 0, :], start=False, stop=True)
                        else:
                            mm = nc.tensor.matmul(ps[:, 0:K], qk[:, it["head"], tq], akT[:, 0:K], start=True, stop=True)
                    mm.then_inc(scores_full, 1)
                elif op == "trans":
                    it = items[arg]
                    if it["kind"] == "C":
                        pe.wait_ge(stick_done, stick_at[arg])
                    else:
                        pe.wait_ge(soft2_done, arg + 1)
                    i = turned_at[arg] - 1
                    if i:
                        pe.wait_ge(turned_out, i)
                    for j in range(it["tile"] + 1):
                        mm = nc.tensor.transpose(T[:, j * P:(j + 1) * P], PR[:, i % 3, j * P:(j + 1) * P], cn("ident"))
                    mm.then_inc(turned, 1)
                elif op == "pv":
                    it = items[arg]
                    u, t, i = it["unit"], it["tile"], turned_at[arg] - 1
                    pe.wait_ge(turned_out, i + 1)
                    if u >= 2:
                        unit_done(pe, u - 2)
                    for gg in it["values"]:
                        wait_group(gg)
                    r0, rn = it["rows"]
                    v0, vn = it["v"]
                    for j in range(t + 1):
                        v = avv[:, j, :] if it["kind"] == "X" else V[:, j, v0:v0 + vn]
                        mm = nc.tensor.matmul(O[u % 2][r0:r0 + rn, t * P:(t + 1) * P], v,
                                              PT[:, i % 2, j * P:(j + 1) * P], start=(j == 0), stop=(j == t))
                    mm.then_inc(pv_done, 1)
                elif op == "down":
                    sl, i = slabs[arg["slab"]], arg["i"]
                    wh, wl = (half_slots(w_, sl).rearrange("p (k n) -> p k n", k=2) for w_ in (WH, WL))
                    pe.wait_ge(w_low, sl["parts_at"])
                    if i == 0:
                        for gg in (len(groups) - 2, len(groups) - 1):
                            wait_group(gg)
                        for u in (len(units) - 2, len(units) - 1):
                            unit_done(pe, u)
                    for t in range(NT):
                        for k in range(2):
                            c = 2 * i + k
                            if t == 0:
                                pe.wait_ge(x_low, arg["acts_low"][k])
                            for half in range(2):
                                for j, (w_, x_) in enumerate(((wh, acts_high), (wl, acts_high), (wh, acts_low))):
                                    mm = nc.tensor.matmul(down[2 * t + half][:, :], x_[c][:, t * P:(t + 1) * P],
                                                          w_[:, k, 512 * half:512 * half + 512],
                                                          start=(c == 0 and j == 0), stop=(c == KF - 1 and j == 2))
                        if i == N_DOWN - 1 or t == NT - 1:
                            mm.then_inc(down_full, 1)

        @block.scalar
        def _(act):
            step = Count(act_step)
            wait_group = group_waits(act)
            n_ln_, n_gate, n_sig = 0, 0, 0

            def link(ins):
                act.wait_ge(act_step, step.on(ins))

            def log1p_exp_abs(dst, src, **kw):
                link(nc.scalar.activation(dst, src, ACT.Abs, **kw))
                link(nc.scalar.activation(dst, dst, ACT.Exp, scale=-1.0))
                return nc.scalar.activation(dst, dst, ACT.Ln, bias=1.0)

            def root(dst, src, n, which):
                link(nc.scalar.activation(dst, src, ACT.Ln, scale=1.0 / n, bias=eps[:, which:which + 1]))
                return nc.scalar.activation(dst, dst, ACT.Exp, scale=-0.5)

            nc.scalar.preload_act_table_set(EXP_AND_LN)
            act.wait_ge(eps_set, 3)
            plain = {"qk": lambda d: qk[:, d, :], "ik": lambda d: ikT, "ak": lambda d: akT,
                     "cq": lambda d: cqT[:, d, :], "ckv": lambda d: ckvT[:, d, :], "qn": lambda d: qn[:, d, :],
                     "kn": lambda d: kn[:, d, :], "hf": lambda d: hF, "hq": lambda d: hQ}
            for op, arg in steps:
                if op == "prep":
                    act.wait_ge(consts_in, N_CONSTS_IN)
                    act.wait_ge(prep, N_PREP)
                elif op == "group":
                    gr = groups[arg]
                    g, kind = arg, gr["kind"]
                    ps, read = bank_of(g)
                    dst = gr.get("dst") or ("", 0)
                    if kind in ("swap", "meansq", "hg_meansq", "sumsq", "hg_attn", "hg_state", "up", "ffup") \
                            or dst[0] in ("resid", "resid2"):
                        continue
                    act.wait_ge(group_full, g + 1)
                    if kind == "T" and dst[0] == "V":
                        nc.scalar.activation(V[:, gr["tile"], dst[1]:dst[1] + gr["N"]], ps[:, 0:gr["N"]],
                                             ACT.Copy).then_inc(read, 1)
                    elif kind == "T" and dst[0] == "av":
                        if gr["tile"] == 0:
                            act.wait_ge(bias_done, N_BIAS)
                        nc.scalar.activation(avv[:, gr["tile"], :], ps[:, 0:P], ACT.Copy)
                        nc.scalar.activation(iw[:, gr["tile"], :], ps[:, P:P + IDX_HEADS], ACT.Copy,
                                             scale=IDX_SCALE).then_inc(read, 1)
                    elif kind == "F" and dst[0] == "raw":
                        if gr["raw_free"]:
                            act.wait_ge(rot_done, gr["raw_free"])
                        nc.scalar.activation(raw[:, dst[1], :], ps[:, :], ACT.Copy, scale=gr["scale"]).then_inc(read, 1)
                    elif kind == "F" and dst[0] in plain:
                        if dst[0] in ("ik", "ak"):
                            act.wait_ge(bias_done, N_BIAS)
                        if dst == ("qn", 0):
                            act.wait_ge(spilled, 16 * NT)
                        nc.scalar.activation(plain[dst[0]](dst[1]), ps[:, :], ACT.Copy, scale=gr["scale"])\
                            .then_inc(read, 1)
                    elif kind == "F" and dst[0] == "cumlog":
                        if gr["nth"] > 1:
                            act.wait_ge(cum_done, gr["nth"] - 1)
                        log1p_exp_abs(cum_l, ps[0:4, :], bias=bfc[0:4, gr["layer"]:gr["layer"] + 1]).then_inc(cum_ln, 1)
                    elif kind == "spread_cum":
                        nc.scalar.activation(ckb[:, gr["head"], :], ps[:, :], ACT.Copy).then_inc(read, 1)
                    elif kind == "turn_cum":
                        nc.scalar.activation(cqc[:, :, :], ps[:, 0:4 * NT].rearrange("p (t h) -> p t h", h=4),
                                             ACT.Copy).then_inc(read, 1)
                    elif kind == "to_hT" and gr.get("parts"):
                        cols = slice(gr["tile"] * P, (gr["tile"] + 1) * P)
                        nc.scalar.activation(xh["hT"][:, 4 * gr["half"]:4 * gr["half"] + 4, cols],
                                             ps[:, :].rearrange("p (k t) -> p k t", k=4), ACT.Copy).then_inc(x_high, 1)
                    elif kind == "to_hT":
                        nc.scalar.activation(hT[:, 4 * gr["half"]:4 * gr["half"] + 4, gr["tile"] * P:(gr["tile"] + 1) * P],
                                             ps[:, :].rearrange("p (k t) -> p k t", k=4), ACT.Copy).then_inc(read, 1)
                    elif kind == "gate":
                        if gr["tg_rot"]:
                            act.wait_ge(rot_done, gr["tg_rot"])
                        if gr["last_gate"]:
                            passed_token(act, wait_group, gr["last_gate"])
                        log1p_exp_abs(tg[:, 0, :], ps[:, :]).then_inc(gate_ln, 1)
                        n_gate += 1
                    elif kind == "sigmoid":
                        e = tg[:, gr["ring"], :]
                        if gr["nth"] > 2:
                            act.wait_ge(mix_done, gr["nth"] - 2)
                        log1p_exp_abs(e, ps[:, :]).then_inc(gate_ln, 1)
                        n_gate += 1
                        act.wait_ge(read, use(g))
                        nc.scalar.activation(e, e, ACT.Exp).then_inc(gate_sig, 1)
                        n_sig += 1
                    elif kind == "ffgate":
                        e = tg[:, gr["ring"], :]
                        if gr["nth"] > 2:
                            wait_group(gr["free"])
                        log1p_exp_abs(e, ps[:, :]).then_inc(gate_ln, 1)
                        n_gate += 1
                        act.wait_ge(gate_min, gr["min_nth"])
                        nc.scalar.activation(e, e, ACT.Exp).then_inc(gate_sig, 1)
                        n_sig += 1
                    elif kind == "hg_turn":
                        nc.scalar.activation(hF, ps[:, :], ACT.Copy).then_inc(read, 1)
                    elif kind == "hg_out":
                        nc.scalar.activation(y[:, 4 + gr["head"], :], ps[:, :], ACT.Copy).then_inc(read, 1)
                        act.wait_ge(read, use(g))
                        if gr["head"]:
                            act.wait_ge(hg_normed, gr["head"])
                        nc.scalar.activation(tg[:, 1, :], y[:, 4 + gr["head"], :], ACT.Square).then_inc(hg_sq, 1)
                elif op == "gate2":
                    act.wait_ge(gate_min, groups[arg]["min_nth"])
                    nc.scalar.activation(tg[:, 0, :], tg[:, 0, :], ACT.Exp).then_inc(gate_sig, 1)
                    n_sig += 1
                elif op == "soft1":
                    n, it = arg, items[arg]
                    K = it["K"]
                    e = E[:, n % 2, :, 0:K]
                    s_ = sc[first_map[n] % SCORE_BANKS][:, 0:K]
                    if n >= 2:
                        act.wait_ge(soft2_done, n - 1)
                    if it["kind"] in "ABXM":
                        act.wait_ge(soft1_done, soft1_at[n])
                    else:
                        act.wait_ge(scores_full, n + 1)
                    c = 2 * (n % 2)
                    if it["kind"] == "A":
                        for j in range(2):
                            ins = nc.scalar.activation(e[:, j, :], sc[(first_map[n] + j) % SCORE_BANKS][:, 0:K], ACT.Exp,
                                                       bias=nmax[:, c + j:c + j + 1], accum_out=sums[:, c + j:c + j + 1])
                    elif it["kind"] in "BX":
                        ins = nc.scalar.activation(e[:, 0, :], L[:, n % 2, 0:K], ACT.Exp, bias=nmax[:, c:c + 1],
                                                   accum_out=sums[:, c:c + 1])
                    elif it["kind"] == "M":
                        ins = nc.scalar.activation(e[:, 0, :], s_, ACT.Exp, bias=nmax[:, c:c + 1], scale=MLA_SCALE,
                                                   accum_out=sums[:, c:c + 1])
                    elif it["kind"] == "C":
                        ins = log1p_exp_abs(e[:, 0, :], s_)
                    else:
                        ins = nc.scalar.activation(e[:, 0, :], s_, ACT.Relu)
                    ins.then_inc(exp_done, 1)
                elif op == "soft3":
                    n, it = arg, items[arg]
                    if it["kind"] == "C":
                        act.wait_ge(soft2_done, n + 1)
                        i = turned_at[n] - 1
                        if i >= 3:
                            act.wait_ge(turned, i - 2)
                        nc.scalar.activation(PR[:, i % 3, 0:it["K"]], L[:, n % 2, 0:it["K"]], ACT.Exp)\
                            .then_inc(stick_done, 1)
                elif op == "trans":
                    n, it = arg, items[arg]
                    i = turned_at[n] - 1
                    act.wait_ge(turned, i + 1)
                    if i >= 2:
                        act.wait_ge(pv_done, i - 1)
                    nc.scalar.activation(PT[:, i % 2, 0:it["K"]], T[:, 0:it["K"]], ACT.Copy).then_inc(turned_out, 1)
                elif op == "fin":
                    u = units[arg]
                    act.wait_ge(pv_done, turned_at[u["last"]])
                    if u["kind"] == "A":
                        if u["nth"] > 1:
                            act.wait_ge(o_free["A"], u["nth"] - 1)
                        nc.scalar.activation(tg[:, 1, :], O[arg % 2][:, :], ACT.Square).then_inc(sq_done, 1)
                    elif u["kind"] != "C":
                        dst = oc if u["kind"] == "M" else y
                        nc.scalar.activation(dst[:, u["chunk"], :], O[arg % 2][:, :], ACT.Copy).then_inc(o_free["other"], 1)
                elif op == "fin2":
                    g = units[arg]["meansq"]
                    act.wait_ge(group_full, g + 1)
                    root(tg[:, 1, :], bank_of(g)[0][:, :], P, 0).then_inc(bank_of(g)[1], 1)
                elif op in ("ln_in", "ln"):
                    n_ln_ += 1
                    act.wait_ge(var_done, n_ln_)
                    link(nc.scalar.activation(lnv[:, 0:1], mv[:, 1:2], ACT.Ln, bias=eps[:, 0:1]))
                    nc.scalar.activation(lnv[:, 1:2], lnv[:, 0:1], ACT.Exp, scale=-0.5).then_inc(rstd_done, 1)
                elif op == "layer":
                    act.wait_ge(lam_dot, 2 * (arg + 1))
                    nc.scalar.activation(lam_s[:, 2:4], lam_s[:, 0:2], ACT.Exp).then_inc(lam_exp, 1)
                elif op == "bounds":
                    act.wait_ge(lb_d, 1)
                    nc.scalar.activation(lbs, lbs, ACT.Exp).then_inc(lb_a, 1)
                    act.wait_ge(lb_d, 2)
                    nc.scalar.activation(l1p, lbx, ACT.Ln, scale=-1.0, bias=1.0)
                    nc.scalar.activation(log_lb, lbs, ACT.Ln, scale=LOG_SCALE).then_inc(lb_a, 1)
                elif op == "sines":
                    for i, name in enumerate(("sin1", "cos1")):
                        act.wait_ge(table_d, i + 1)
                        kw = dict(scale=cn("sin_sign")) if i == 0 else dict(bias=eps[:, 2:3])
                        nc.scalar.activation(cn(name), cn(name), ACT.Sin, **kw).then_inc(table_a, 1)
                    nc.scalar.preload_act_table_set(EXP_AND_LN)
                elif op == "norm":
                    t, k = arg["tile"], arg["nth"]
                    if k < NT:
                        act.wait_ge(ln_done, n_ln - NT + k + 1)
                    else:
                        for gg in arg["groups"]:
                            wait_group(gg)
                    if k >= 2:
                        act.wait_ge(group_full, arg["turned"])
                        act.wait_ge(norm_done, k - 1)
                    if k == 0:
                        act.wait_ge(soft2_done, last_C + 1)
                    link(nc.scalar.activation(norm_rows(k), h_tok[:, t, :], ACT.Square, accum_out=ss[:, k % 2:k % 2 + 1]))
                    root(ss[:, k % 2:k % 2 + 1], ss[:, k % 2:k % 2 + 1], D, 1).then_inc(norm_r, 1)
                elif op == "squares":
                    src = cqT if arg == "cq" else ckvT
                    if arg == "cq":
                        act.wait_ge(spilled, 16 * NT)
                        for gg in groups:
                            if (gg.get("dst") or ("",))[0] in ("cq", "ckv"):
                                wait_group(gg["g"])
                    else:
                        act.wait_ge(group_full, arg_group["cq"] + 1)
                    n = 3 if arg == "cq" else 2
                    for k in range(n):
                        ins = nc.scalar.activation(qn[:, k, :], src[:, k, :], ACT.Square)
                    ins.then_inc(lat_sq, 1)
                elif op == "latent":
                    g = arg_group[arg]
                    if arg == "ckv":
                        act.wait_ge(lat_done, 1)
                    act.wait_ge(group_full, g + 1)
                    root(tg[:, 1, :], bank_of(g)[0][:, :], 384 if arg == "cq" else 256, 1).then_inc(bank_of(g)[1], 1)
                elif op == "hg_gate_a":
                    h, part = arg
                    if part == 0:
                        wait_group(hf_group[h])
                        log1p_exp_abs(hA, hF).then_inc(hg_act, 1)
                    else:
                        act.wait_ge(hg_dve, 2 * h + 1)
                        nc.scalar.activation(hG, hB, ACT.Exp)
                        log1p_exp_abs(hKE, hA).then_inc(hg_act, 1)
                elif op == "hg_diff":
                    h, lv = arg
                    act.wait_ge(hg_diff, (LEVELS + 1) * h + lv + 1)
                    if lv < LEVELS:
                        nc.scalar.activation(hG[:, 0:256], hG[:, 0:256], ACT.Exp)
                        nc.scalar.activation(hG[:, 256:512], hG[:, 256:512], ACT.Exp, scale=-1.0).then_inc(hg_exp, 1)
                    else:
                        nc.scalar.activation(hG, hG, ACT.Exp).then_inc(hg_exp, 1)
                elif op == "hg_decay":
                    h = arg
                    b8 = hB.rearrange("p (n c) -> p n c", c=CHUNK)
                    act.wait_ge(group_full, level_group[(h, LEVELS - 2)] + 1)
                    nc.scalar.activation(dec, b8[:, :, CHUNK - 1], ACT.Exp)
                    nc.scalar.activation(hQD, hB, ACT.Exp).then_inc(hg_de, 1)
                elif op == "hg_norm":
                    g = head_meansq[arg]
                    act.wait_ge(group_full, g + 1)
                    root(tg[:, 1, :], bank_of(g)[0][:, :], P, 1).then_inc(bank_of(g)[1], 1)
                elif op == "tail":
                    act.wait_ge(group_full, tail_group)
                    act.wait_ge(scores_full, len(items))
                    act.wait_ge(soft1_done, soft1_at[-1])
                    act.wait_ge(soft2_done, len(items))
                    act.wait_ge(turned, turned_at[-1])
                    act.wait_ge(pv_done, turned_at[-1])
                    unit_done(act, len(units) - 1)
                elif op == "split":
                    i, q, n = arg["slab"], arg["piece"], arg["cols"]
                    if q == 0:
                        act.wait_ge(loaded[slabs[i]["slot"]], landed[i])
                    r = slice(q * n, (q + 1) * n)
                    nc.scalar.activation(half_slots(WH, slabs[i])[:, r], half_slots(W, slabs[i])[:, r], ACT.Copy).then_inc(w_high, 1)
                elif op == "split_x":
                    name, k0, n = arg
                    if name == "yb":
                        passed_token(act, wait_group, ("gated", n_gated))
                    elif name == "mix":
                        act.wait_ge(mix_done, 2 * 8 + k0 + 1)
                    elif name == "act":
                        wait_group(ffup_group[k0])
                        if k0 >= EARLY:
                            act.wait_ge(group_full, ffup_group[-1] + 1)
                        nc.scalar.activation(acts_high[k0], acts[k0], ACT.Copy).then_inc(x_high, 1)
                        continue
                    nc.scalar.activation(xh[name][:, k0:k0 + n, :], whole[name][:, k0:k0 + n, :], ACT.Copy).then_inc(x_high, 1)
                elif op == "final":
                    t = arg
                    act.wait_ge(fin_sum, t + 1)
                    c = ss[:, t % 2:t % 2 + 1]
                    link(nc.scalar.activation(final[t], h_tok[:, t, :], ACT.Square, accum_out=c))
                    root(c, c, D, 1).then_inc(norm_r, 1)

        @block.vector
        def _(dve):
            step = Count(dve_step)
            wait_group = group_waits(dve)
            n_ln_ = n_cum = n_gate = n_min = n_sig = n_x = 0

            def link(ins):
                dve.wait_ge(dve_step, step.on(ins))

            for i, v in enumerate((1e-5, 1e-6, math.pi / 2)):
                nc.vector.memset(eps[:, i:i + 1], v).then_inc(eps_set, 1)
            dve.wait_ge(eps_set, 3)

            def layernorm(src, t, nth, rows_need):
                for i in range(2):
                    ins = nc.vector.bn_stats(stats[:, 6 * i:6 * i + 6], src[:, 512 * i:512 * i + 512])
                link(ins)
                nc.vector.bn_aggr(mv, stats).then_inc(var_done, 1)
                dve.wait_ge(rstd_done, nth)
                link(nc.vector.tensor_scalar(h_tok[:, t, :], src, mv[:, 0:1], lnv[:, 1:2], ALU.subtract, ALU.mult))
                if rows_need:
                    dve.wait_ge(rows_in, rows_need)
                else:
                    dve.wait_ge(first_rows_in, 32)
                link(nc.vector.tensor_tensor(h_tok[:, t, :], h_tok[:, t, :], rows[:, 0, :], ALU.mult))
                nc.vector.tensor_tensor(h_tok[:, t, :], h_tok[:, t, :], rows[:, 1, :], ALU.add).then_inc(ln_done, 1)

            for op, arg in steps:
                if op == "group":
                    gr = groups[arg]
                    g, kind = arg, gr["kind"]
                    ps, read = bank_of(g)
                    dst = gr.get("dst") or ("", 0)
                    if kind == "swap":
                        r = raw[:, gr["ring"], :]
                        dve.wait_ge(group_full, g + 1)
                        wait_group(gr["raw"])
                        if gr["tg_gate"]:
                            passed_token(dve, wait_group, gr["tg_gate"])
                        if gr["nth"] > 1:
                            dve.wait_ge(rot_done, gr["nth"] - 1)
                        if gr["table"]:
                            dve.wait_ge(table_a, 2)
                        nc.vector.tensor_tensor(tg[:, 0, :], ps[:, :], cn("sin1"), ALU.mult).then_inc(read, 1)
                        link(nc.vector.tensor_tensor(r, r, cn("cos1"), ALU.mult))
                        o = {"qk": lambda d: qk[:, d, :], "kpe": lambda d: kpe, "qp": lambda d: qp[:, d, :]}[dst[0]](dst[1])
                        nc.vector.tensor_tensor(o, tg[:, 0, :], r, ALU.add).then_inc(rot_done, 1)
                    elif kind == "to_hT" and gr.get("parts"):
                        n_x += 1
                        cols = slice(gr["tile"] * P, (gr["tile"] + 1) * P)
                        dve.wait_ge(x_high, n_x)
                        k = slice(4 * gr["half"], 4 * gr["half"] + 4)
                        nc.vector.tensor_tensor(xl["hT"][:, k, cols], ps[:, :].rearrange("p (k t) -> p k t", k=4),
                                                xh["hT"][:, k, cols], ALU.subtract).then_inc(read, 1)
                    elif kind == "F" and dst[0] == "cumlog":
                        n_cum += 1
                        dve.wait_ge(group_full, g + 1)
                        b = bfc[0:4, gr["layer"]:gr["layer"] + 1]
                        dve.wait_ge(cum_ln, n_cum)
                        nc.vector.tensor_scalar(cum_min, ps[0:4, :], b, 0.0, ALU.add, ALU.min).then_inc(read, 1)
                        dve.wait_ge(read, use(g))
                        link(nc.vector.tensor_tensor(cum_min, cum_min, cum_l, ALU.subtract))
                        nc.vector.tensor_tensor_scan(cum, cum_min, cum_min, 0.0, ALU.add, ALU.min).then_inc(cum_done, 1)
                    elif kind == "gate":
                        n_gate += 1
                        n_min += 1
                        dve.wait_ge(gate_ln, n_gate)
                        nc.vector.scalar_tensor_tensor(tg[:, 0, :], ps[:, :], 0.0, tg[:, 0, :], ALU.min, ALU.subtract)\
                            .then_inc(gate_min, 1)
                    elif kind == "sigmoid":
                        n_gate += 1
                        n_sig += 1
                        e = tg[:, gr["ring"], :]
                        dve.wait_ge(gate_ln, n_gate)
                        nc.vector.scalar_tensor_tensor(e, ps[:, :], 0.0, e, ALU.min, ALU.subtract).then_inc(read, 1)
                    elif kind == "up":
                        e = tg[:, gr["ring"], :]
                        dve.wait_ge(group_full, g + 1)
                        dve.wait_ge(gate_sig, n_sig)
                        nc.vector.tensor_tensor(e, ps[:, :], e, ALU.mult).then_inc(read, 1)
                        dve.wait_ge(read, use(g))
                        o = mix[:, gr["chunk"], :]
                        if gr["branch"] == 0:
                            nc.vector.tensor_copy(o, e).then_inc(mix_done, 1)
                        else:
                            dve.wait_ge(mix_done, 8 * gr["branch"])
                            nc.vector.tensor_tensor(o, o, e, ALU.add).then_inc(mix_done, 1)
                    elif kind == "ffgate":
                        n_gate += 1
                        n_min += 1
                        n_sig += 1
                        e = tg[:, gr["ring"], :]
                        dve.wait_ge(gate_ln, n_gate)
                        nc.vector.scalar_tensor_tensor(e, ps[:, :], 0.0, e, ALU.min, ALU.subtract).then_inc(gate_min, 1)
                        dve.wait_ge(gate_sig, n_sig)
                        nc.vector.tensor_tensor(e, ps[:, :], e, ALU.mult).then_inc(read, 1)
                    elif kind == "ffup":
                        dve.wait_ge(group_full, g + 1)
                        wait_group(gr["gate"])
                        nc.vector.tensor_tensor(acts[gr["chunk"]], ps[:, :], tg[:, gr["ring"], :], ALU.mult).then_inc(read, 1)
                    elif kind == "T" and dst[0] == "resid":
                        dve.wait_ge(group_full, g + 1)
                        half = dst[1]
                        nc.vector.scalar_tensor_tensor(z[:, 512 * half:512 * half + 512],
                                                       h_tok[:, gr["tile"], 512 * half:512 * half + 512], ALPHA,
                                                       ps[:, :], ALU.mult, ALU.add).then_inc(read, 1)
                        dve.wait_ge(read, use(g))
                    elif kind == "T" and dst[0] == "resid2":
                        dve.wait_ge(group_full, g + 1)
                        dve.wait_ge(x_back, 16 * NT)
                        x = h_tok[:, gr["tile"], 256 * dst[1]:256 * dst[1] + 256]
                        nc.vector.tensor_tensor(x, x, ps[:, 0:256], ALU.add).then_inc(read, 1)
                elif op == "gate2":
                    gr = groups[arg]
                    ps, read = bank_of(arg)
                    n_sig += 1
                    dve.wait_ge(gate_sig, n_sig)
                    o = y[:, gr["chunk"], :] if gr["first"] else tg[:, 0, :]
                    nc.vector.tensor_tensor(o, ps[:, :], tg[:, 0, :], ALU.mult).then_inc(read, 1)
                elif op == "gate3":
                    gr = groups[arg]
                    if not gr["first"]:
                        dve.wait_ge(bank_of(arg)[1], use(arg))
                        c = gr["chunk"]
                        if gr["unit"] is not None:
                            unit_done(dve, gr["unit"])
                        else:
                            dve.wait_ge(hg_normed, c - 3)
                        nc.vector.tensor_tensor(y[:, c, :], y[:, c, :], tg[:, 0, :], ALU.mult).then_inc(gated, 1)
                elif op == "fin" and units[arg]["kind"] == "C":
                    u = units[arg]
                    dve.wait_ge(pv_done, turned_at[u["last"]])
                    wait_group(u["gate"])
                    nc.vector.tensor_tensor(y[:, u["chunk"], :], O[arg % 2][:, :], y[:, u["chunk"], :], ALU.mult)\
                        .then_inc(o_free["C"], 1)
                elif op == "bias":
                    t, b = arg
                    K = P * (t + 1)
                    k = NT_BIAS(t, b)
                    mk = below[k % 2][:, 0:K]
                    if k >= 1:
                        dve.wait_ge(bias_done, 4 * k)
                    link(nc.vector.tensor_scalar(starts[:, 0:1], pq[:, t:t + 1], float(-BUCKET_STARTS[b]), None, ALU.add))
                    nc.vector.tensor_scalar(mk, pkb[:, 0:K], starts[:, 0:1], None, ALU.is_le).then_inc(bias_mask, 1)
                    dve.wait_ge(bias_mask, k + 1)
                    for h in range(4):
                        o, d = b_at(h, t), deltas[:, b, h:h + 1]
                        if b == REL_BUCKETS - 1:
                            ins = nc.vector.tensor_scalar(o, mk, d, deltas[:, 0, h:h + 1], ALU.mult, ALU.add)
                        else:
                            ins = nc.vector.scalar_tensor_tensor(o, mk, d, o, ALU.mult, ALU.add)
                        ins.then_inc(bias_done, 1)
                elif op == "soft1":
                    n, it = arg, items[arg]
                    K, kind = it["K"], it["kind"]
                    if kind in "CI":
                        continue
                    dve.wait_ge(scores_full, n + 1)
                    if n >= 2:
                        dve.wait_ge(exp_done, n - 1)
                        if items[n - 2]["kind"] == "C":
                            dve.wait_ge(stick_done, stick_at[n - 2])
                    c = 2 * (n % 2)
                    s_ = sc[first_map[n] % SCORE_BANKS][:, 0:K]
                    l = L[:, n % 2, 0:K]
                    if kind == "A":
                        for j in range(2):
                            ins = nc.vector.tensor_reduce(nmax[:, c + j:c + j + 1],
                                                          sc[(first_map[n] + j) % SCORE_BANKS][:, 0:K],
                                                          AX, ALU.max, negate=True)
                        ins.then_inc(soft1_done, 1)
                        continue
                    if kind == "M":
                        link(nc.vector.tensor_reduce(nmax[:, c:c + 1], s_, AX, ALU.max, negate=True))
                        nc.vector.tensor_scalar(nmax[:, c:c + 1], nmax[:, c:c + 1], MLA_SCALE, None, ALU.mult)\
                            .then_inc(soft1_done, 1)
                        continue
                    h = it["head"]
                    if kind == "B":
                        for gg in it["cums"]:
                            wait_group(gg)
                        link(nc.vector.scalar_tensor_tensor(l, s_, cqc[:, it["tile"], h:h + 1], ckb[:, h, 0:K],
                                                            ALU.add, ALU.subtract))
                    else:
                        link(nc.vector.scalar_tensor_tensor(l, s_, SPARSE_SCALE, b_at(h, it["tile"]), ALU.mult, ALU.add))
                    nc.vector.tensor_reduce(nmax[:, c:c + 1], l, AX, ALU.max, negate=True).then_inc(soft1_done, 1)
                elif op == "soft2":
                    n, it = arg, items[arg]
                    K, e, l, kind = it["K"], E[:, n % 2, :, 0:it["K"]], L[:, n % 2, 0:it["K"]], it["kind"]
                    c = 2 * (n % 2)
                    dve.wait_ge(exp_done, n + 1)
                    i = turned_at[n] - 1
                    pr = PR[:, i % 3, 0:K]
                    if kind in "ABMX":
                        if i >= 3:
                            dve.wait_ge(turned, i - 2)
                        link(nc.vector.reciprocal(rsum[:, c:c + it["maps"]], sums[:, c:c + it["maps"]]))
                    if kind == "A":
                        link(nc.vector.tensor_scalar(c2[:, 0:1], rsum[:, c + 1:c + 2], lam, None, ALU.mult))
                        link(nc.vector.tensor_scalar(e[:, 1, :], e[:, 1, :], c2[:, 0:1], None, ALU.mult))
                        nc.vector.scalar_tensor_tensor(pr, e[:, 0, :], rsum[:, c:c + 1], e[:, 1, :],
                                                       ALU.mult, ALU.subtract).then_inc(soft2_done, 1)
                    elif kind in "BMX":
                        nc.vector.tensor_scalar(pr, e[:, 0, :], rsum[:, c:c + 1], None, ALU.mult).then_inc(soft2_done, 1)
                    elif kind == "I":
                        w_ = iw[:, it["tile"], it["head"]:it["head"] + 1]
                        acc = z[:, 0:K]
                        dve.wait_ge(soft2_done, n)
                        if it["head"] == 0:
                            nc.vector.tensor_scalar(acc, e[:, 0, :], w_, None, ALU.mult).then_inc(soft2_done, 1)
                        else:
                            nc.vector.scalar_tensor_tensor(acc, e[:, 0, :], w_, acc, ALU.mult, ALU.add)\
                                .then_inc(soft2_done, 1)
                    else:
                        s_ = sc[first_map[n] % SCORE_BANKS][:, 0:K]
                        link(nc.vector.scalar_tensor_tensor(e[:, 1, :], s_, 0.0, e[:, 0, :], ALU.max, ALU.add))
                        back = E[:, n % 2, 1, K - 1::-1]
                        link(nc.vector.tensor_tensor_scan(E[:, n % 2, 0, K - 1::-1], back, back, 0.0, ALU.add, ALU.max))
                        if n >= 2 and items[n - 2]["kind"] == "C":
                            dve.wait_ge(stick_done, stick_at[n - 2])
                        nc.vector.tensor_tensor(l, s_, e[:, 0, :], ALU.subtract).then_inc(soft2_done, 1)
                elif op == "topk":
                    t = arg
                    K = P * (t + 1)
                    buf = [z[:, 0:K], z[:, S:S + K]]
                    dve.wait_ge(soft2_done, max(n for n, it in enumerate(items) if it["kind"] == "I" and it["tile"] == t) + 1)
                    if t == 1:
                        dve.wait_ge(bias_done, N_BIAS)
                        for h in range(4):
                            link(nc.vector.tensor_tensor(b_at(h, 0), b_at(h, 0), negb[:, 0, :], ALU.add))
                    link(nc.vector.tensor_tensor(buf[0][:, K - P:K], buf[0][:, K - P:K], negb[:, 0, :], ALU.add))
                    for r in range(TOPK // 8):
                        link(nc.vector.max(m8, buf[r % 2]))
                        link(nc.vector.match_replace(buf[(r + 1) % 2], m8, buf[r % 2], STRUCK))
                    link(nc.vector.tensor_scalar(buf[1], buf[0], STRUCK / 2, NEG, ALU.is_gt, ALU.mult))
                    link(nc.vector.tensor_tensor(buf[1][:, K - P:K], buf[1][:, K - P:K], negb[:, 0, :], ALU.add))
                    for h in range(4):
                        link(nc.vector.tensor_tensor(b_at(h, t), b_at(h, t), buf[1], ALU.add))
                elif op == "fin2":
                    u = units[arg]
                    wait_group(u["meansq"])
                    nc.vector.scalar_tensor_tensor(y[:, u["chunk"], :], O[arg % 2][:, :], gcol, tg[:, 1, :],
                                                   ALU.mult, ALU.mult).then_inc(o_free["A"], 1)
                elif op == "layer":
                    l = arg
                    lam_init = 0.8 - 0.6 * math.exp(-0.3 * l)
                    dve.wait_ge(lam_loaded, 64 * (l + 1))
                    for i in range(2):
                        nc.vector.tensor_tensor_reduce(lam_in[:, 2 * i, :], lam_in[:, 2 * i, :], lam_in[:, 2 * i + 1, :],
                                                       1.0, 0.0, ALU.mult, ALU.add, lam_s[:, i:i + 1]).then_inc(lam_dot, 1)
                    dve.wait_ge(lam_exp, l + 1)
                    link(nc.vector.tensor_tensor(lam_s[:, 4:5], lam_s[:, 2:3], lam_s[:, 3:4], ALU.subtract))
                    nc.vector.tensor_scalar(lam, lam_s[:, 4:5], lam_init, None, ALU.add).then_inc(lam_done, 1)
                    nc.vector.tensor_scalar(gcol, gin[:, l:l + 1], 1.0 - lam_init, None, ALU.mult).then_inc(lam_done, 1)
                    dve.wait_ge(lam_done, 2 * (l + 1))
                elif op == "prep":
                    dve.wait_ge(consts_in, N_CONSTS_IN)
                    dve.wait_ge(staged_in, 32)
                    nc.vector.tensor_copy(identb[:, :], cn("ident")).then_inc(prep, 1)
                    nc.vector.tensor_copy(negb[:, :, :].rearrange("p a n -> p (a n)"), z[:, 0:2 * P]).then_inc(prep, 1)
                    nc.vector.tensor_copy(keep[:, :], z[:, 2 * P:2 * P + S]).then_inc(prep, 1)
                    nc.vector.tensor_copy(masks8[:, :], raw[:, :, :].rearrange("p a n -> p (a n)")[:, 0:(LEVELS + 1) * P])\
                        .then_inc(prep, 1)
                    dve.wait_ge(prep, N_PREP)
                    if not only_block1:
                        dve.wait_ge(pos_in, 16 * (NT + 2))
                        link(nc.vector.tensor_copy(pq, pos_i[:, :]))
                        link(nc.vector.tensor_copy(pkb, below[0].bitcast(I32)))
                        link(nc.vector.tensor_copy(below[1][:, 0:4 * REL_BUCKETS], deltas[:, :, :].rearrange("p b h -> p (b h)")))
                        link(nc.vector.tensor_tensor(
                            deltas[:, 1:REL_BUCKETS, :].rearrange("p b h -> p (b h)"),
                            deltas[:, 1:REL_BUCKETS, :].rearrange("p b h -> p (b h)"),
                            below[1][:, 0:4 * (REL_BUCKETS - 1)], ALU.subtract))
                elif op == "ln_in":
                    n_ln_ += 1
                    dve.wait_ge(x_in[arg], 16)
                    layernorm(h_tok[:, arg, :], arg, n_ln_, 0)
                elif op == "ln":
                    n_ln_ += 1
                    layernorm(z[:, :], arg[1], n_ln_, 32 * (arg[0] + 1))
                elif op == "bounds":
                    link(nc.vector.tensor_tensor(lbs, lbx, lbx, ALU.subtract))
                    nc.vector.tensor_copy(lbs, lbs).then_inc(lb_d, 1)
                    dve.wait_ge(lb_a, 1)
                    link(nc.vector.reciprocal(oml, lbs))
                    link(nc.vector.tensor_tensor(lbs, lbs, oml, ALU.mult))
                    link(nc.vector.tensor_tensor(lbx, lbs, lbs, ALU.subtract))
                    link(nc.vector.tensor_scalar(oml, lbx, -1.0, 1.0, ALU.mult, ALU.add))
                    nc.vector.tensor_scalar(lbs, lbx, LB_FLOOR, None, ALU.max).then_inc(lb_d, 1)
                    dve.wait_ge(lb_a, 2)
                    link(nc.vector.tensor_scalar(log_lb, log_lb, -math.log(LOG_SCALE), None, ALU.add))
                    link(nc.vector.tensor_tensor(l1a, l1p, log_lb, ALU.subtract))
                elif op == "angles":
                    sin_, cos_, ang = cn("sin1"), cn("cos1"), tg[:, 1, :]
                    dve.wait_ge(rot_done, NT * 2 * DEPTH)
                    link(nc.vector.tensor_scalar(ang, pkb, cn("inv_freq"), None, ALU.mult))
                    for o, shift in ((sin_, 0.0), (cos_, 0.25)):
                        turn = tg[:, 0, :]
                        link(nc.vector.tensor_scalar(turn, ang, 1.0 / (2 * math.pi), shift, ALU.mult, ALU.add))
                        link(nc.vector.tensor_scalar(turn, turn, MAGIC, None, ALU.add))
                        link(nc.vector.tensor_scalar(turn, turn, MAGIC, None, ALU.subtract))
                        link(nc.vector.scalar_tensor_tensor(o, turn, -TWO_PI[0], ang, ALU.mult, ALU.add))
                        link(nc.vector.scalar_tensor_tensor(o, turn, -TWO_PI[1], o, ALU.mult, ALU.add))
                        link(nc.vector.scalar_tensor_tensor(o, turn, -TWO_PI[2], o, ALU.mult, ALU.add))
                        lo = -PI_F - (math.pi / 2 if shift else 0.0)
                        nc.vector.tensor_scalar(o, o, lo, lo + 2 * PI_F, ALU.max, ALU.min).then_inc(table_d, 1)
                        dve.wait_ge(table_d, 1 + (shift > 0))
                elif op == "norm":
                    t, k = arg["tile"], arg["nth"]
                    dve.wait_ge(norm_r, k + 1)
                    if k < NT:
                        dve.wait_ge(attn_row_in, 16)
                    else:
                        dve.wait_ge(rows_in, 32 * (DEPTH + 1))
                    o, gain = norm_rows(k), rows[:, 0, :] if k >= NT else attn_row
                    link(nc.vector.tensor_scalar(o, h_tok[:, t, :], ss[:, k % 2:k % 2 + 1], None, ALU.mult))
                    nc.vector.tensor_tensor(o, o, gain, ALU.mult).then_inc(norm_done, 1)
                elif op == "latent":
                    wait_group(arg_group[arg])
                    x, gg, n = (cqT, mq_g, 3) if arg == "cq" else (ckvT, mkv_g, 2)
                    for k in range(n):
                        ins = nc.vector.scalar_tensor_tensor(x[:, k, :], x[:, k, :], gg[:, k:k + 1], tg[:, 1, :],
                                                             ALU.mult, ALU.mult)
                    ins.then_inc(lat_done, 1)
                elif op == "hg_gate_d" and arg[1] == 0:
                    h = arg[0]
                    if h == 0:
                        for b_ in (hQD, hATT, z[:, :]):
                            nc.vector.memset(b_, 0.0).then_inc(hg_ready0, 1)
                        dve.wait_ge(hg_ready0, 3)
                    wait_group(hf_group[h])
                    wait_group(hq_group[h])
                    dve.wait_ge(hg_act, 2 * h + 1)
                    link(nc.vector.scalar_tensor_tensor(hK, hF, 0.0, hA, ALU.min, ALU.subtract))
                    nc.vector.tensor_tensor(hB, hK, hF, ALU.subtract)
                    nc.vector.tensor_scalar(hA, hK, l1a[:, h:h + 1], None, ALU.add).then_inc(hg_dve, 1)
                    dve.wait_ge(hg_dve, 2 * h + 1)
                elif op == "hg_gate_d":
                    h = arg[0]
                    dve.wait_ge(hg_act, 2 * h + 2)
                    link(nc.vector.tensor_scalar(hK, hK, l1p[:, h:h + 1], log_lb[:, h:h + 1], ALU.add, ALU.max))
                    link(nc.vector.tensor_tensor(hKE, hKE, hK, ALU.add))
                    link(nc.vector.tensor_tensor_scan(hB, keep[:, :], hKE, 0.0, ALU.mult, ALU.add))
                    nc.vector.tensor_scalar(hK, hG, oml[:, h:h + 1], None, ALU.mult).then_inc(hg_dve, 1)
                    dve.wait_ge(hg_dve, 2 * (h + 1))
                elif op == "hg_diff":
                    h, lv = arg
                    if lv < LEVELS:
                        hb = 1 << lv
                        gu, gl = (hG[:, 256 * i:256 * i + 256].rearrange("p (n b) -> p n b", b=hb) for i in range(2))
                        ref = halves(hB, 0, hb)[:, :, hb - 1:hb].to_broadcast([P, S // (2 * hb), hb])
                        nc.vector.tensor_tensor(gu, halves(hB, 1, hb), ref, ALU.subtract)
                        nc.vector.tensor_tensor(gl, halves(hB, 0, hb), ref, ALU.subtract).then_inc(hg_diff, 1)
                    else:
                        b8 = hB.rearrange("p (n c) -> p n c", c=CHUNK)
                        last = b8[:, :, CHUNK - 1:CHUNK].to_broadcast([P, NCH, CHUNK])
                        nc.vector.tensor_tensor(hG.rearrange("p (n c) -> p n c", c=CHUNK), last, b8, ALU.subtract)\
                            .then_inc(hg_diff, 1)
                elif op == "hg_level":
                    h, lv = arg
                    hb = 1 << lv
                    gu, gl = (hG[:, 256 * i:256 * i + 256].rearrange("p (n b) -> p n b", b=hb) for i in range(2))
                    if lv >= 2:
                        dve.wait_ge(group_full, level_group[(h, lv - 2)] + 1)
                    dve.wait_ge(hg_exp, (LEVELS + 1) * h + lv + 1)
                    nc.vector.tensor_tensor(halves(hQT[lv % 2], 1, hb), halves(hQ, 1, hb), gu, ALU.mult)
                    nc.vector.tensor_tensor(halves(hKT[lv % 2], 0, hb), halves(hK, 0, hb), gl, ALU.mult)\
                        .then_inc(hg_ready, 1)
                    dve.wait_ge(hg_ready, LEVELS * h + lv + 1)
                elif op == "hg_put":
                    gr = groups[arg]
                    ps, read = bank_of(arg)
                    dve.wait_ge(group_full, arg + 1)
                    mk = masks8[:, (gr["level"] + 1) * P:(gr["level"] + 2) * P]
                    if arg_prev_put.get(arg) is not None:
                        wait_group(arg_prev_put[arg])
                    nc.vector.copy_predicated(hATT.rearrange("p (i t) -> p i t", i=NT),
                                              mk[:, None, :].to_broadcast([P, NT, P]),
                                              ps[:, :].rearrange("p (i t) -> p i t", i=NT)).then_inc(read, 1)
                elif op == "hg_decay":
                    h = arg
                    dve.wait_ge(hg_exp, (LEVELS + 1) * (h + 1))
                    dve.wait_ge(hg_de, h + 1)
                    nc.vector.tensor_tensor(hQD, hQD, hQ, ALU.mult)
                    nc.vector.tensor_tensor(hA, hK, hG, ALU.mult).then_inc(hg_kd, 1)
                elif op == "hg_chain":
                    h, gs = arg
                    for g in gs:
                        dve.wait_ge(group_full, g + 1)
                    for n in range(NCH - 1):
                        ps, read = bank_of(gs[n % 2])
                        new, p_ = states[:, n + 1, :], ps[:, (n // 2) * P:(n // 2 + 1) * P]
                        if n == 0:
                            ins = nc.vector.tensor_copy(new, p_)
                        else:
                            ins = nc.vector.scalar_tensor_tensor(new, states[:, n, :], dec[:, n:n + 1], p_,
                                                                 ALU.mult, ALU.add)
                        if n >= NCH - 3:
                            ins.then_inc(read, 1)
                            dve.wait_ge(read, use(gs[n % 2]))
                        else:
                            link(ins)
                elif op == "hg_norm":
                    h = arg
                    wait_group(head_meansq[h])
                    nc.vector.scalar_tensor_tensor(y[:, 4 + h, :], y[:, 4 + h, :], out_g, tg[:, 1, :],
                                                   ALU.mult, ALU.mult).then_inc(hg_normed, 1)
                elif op == "split":
                    i, q, n = arg["slab"], arg["piece"], arg["cols"]
                    r = slice(q * n, (q + 1) * n)
                    dve.wait_ge(w_high, arg["nth"])
                    nc.vector.tensor_tensor(half_slots(WL, slabs[i])[:, r], half_slots(W, slabs[i])[:, r],
                                            half_slots(WH, slabs[i])[:, r], ALU.subtract).then_inc(w_low, 1)
                elif op == "split_x":
                    name, k0, n = arg
                    n_x += 1
                    dve.wait_ge(x_high, n_x)
                    if name == "act":
                        nc.vector.tensor_tensor(acts_low[k0], acts[k0], acts_high[k0], ALU.subtract).then_inc(x_low, 1)
                        continue
                    nc.vector.tensor_tensor(xl[name][:, k0:k0 + n, :], whole[name][:, k0:k0 + n, :],
                                            xh[name][:, k0:k0 + n, :], ALU.subtract).then_inc(x_low, 1)
                elif op == "final":
                    t = arg
                    dve.wait_ge(down_full, N_DOWN + t)
                    for half in range(2):
                        x = h_tok[:, t, 512 * half:512 * half + 512]
                        ins = nc.vector.tensor_tensor(x, x, down[2 * t + half][:, :], ALU.add)
                    ins.then_inc(fin_sum, 1)
                    dve.wait_ge(norm_r, 2 * NT + t + 1)
                    link(nc.vector.tensor_scalar(final[t], h_tok[:, t, :], ss[:, t % 2:t % 2 + 1], None, ALU.mult))
                    nc.vector.tensor_tensor(final[t], final[t], rows[:, 1, :], ALU.mult).then_inc(fin_done, 1)


def kernel(**inputs):
    import concourse.bacc as bacc
    from concourse.bass_utils import run_bass_kernel_spmd

    nc = bacc.Bacc("TRN2", target_bir_lowering=False, num_devices=1)
    arrays, aps = {}, {}
    given = dict(inputs, constants=constants())
    for name, v in given.items():
        v = np.ascontiguousarray(v)
        arrays[f"in_{name}"] = v
        aps[name] = nc.dram_tensor(f"in_{name}", v.shape, mybir.dt.from_np(v.dtype), kind="ExternalInput").ap()
    out = nc.dram_tensor("out_0", (1, S, D), F32, kind="ExternalOutput").ap()
    two_blocks(nc, aps, out)
    return run_bass_kernel_spmd(nc, [arrays], core_ids=[0]).results[0]["out_0"]
```
